# Optimizing a Trainium2 kernel written in Bass

```python
import math
import jax, jax.numpy as jnp
from jax import lax
import numpy as np

D_MODEL = 1024
BATCH = 1
SEQ = 256
DEPTH = 2

CTX_LEN = 256
GRID_W = 64
A_HEADS = 4
A_HD = 64
A_VD = 2 * A_HD
A_QK = A_HEADS * 2 * A_HD
A_VW = A_HEADS * A_VD
M_HEADS = 4
M_QK = 64
M_V = 128
M_QKW = M_HEADS * M_QK
M_VW = M_HEADS * M_V
G_HEADS = 4
G_HD = 128
G_W = G_HEADS * G_HD
CONV_K = 5
BRANCH_W = 512
D_FF = 4 * D_MODEL
CHUNK = 64
Q_BLOCK = 128
ROPE_BASE = 10000.0
EPS = 1e-6
IN_SPLITS = (A_QK, A_QK, A_VW,
             M_QKW, M_QKW, M_VW, M_VW, 4 * M_HEADS,
             G_W, G_W, G_W, G_W, 4 * G_HEADS,
             3 * D_MODEL)
D_IN = sum(IN_SPLITS)

kernel_name = 'hybrid_diffattn_mlstm_gdn_dit_trunk'

def _rmsnorm(x, gain):
    x32 = x.astype(jnp.float32)
    y = x32 * lax.rsqrt(jnp.mean(x32 * x32, axis=-1, keepdims=True) + EPS)
    return (y * gain.astype(jnp.float32)).astype(x.dtype)

def _l2norm(x):
    x32 = x.astype(jnp.float32)
    return (x32 * lax.rsqrt(jnp.sum(x32 * x32, axis=-1, keepdims=True) + EPS)).astype(x.dtype)

def _heads(t, h):
    B, T, _ = t.shape
    return jnp.moveaxis(t.reshape(B, T, h, -1), 2, 1)

def _merge_heads(t):
    B, H, T, d = t.shape
    return jnp.moveaxis(t, 1, 2).reshape(B, T, H * d)

def _flip(t):
    return jnp.flip(t, axis=2)

def _grid_rope_tables(n_lat):
    rows = n_lat // GRID_W
    row = jnp.repeat(jnp.arange(rows, dtype=jnp.float32), GRID_W)
    col = jnp.tile(jnp.arange(GRID_W, dtype=jnp.float32), rows)
    half = A_HD // 2
    inv_freq = ROPE_BASE ** (-jnp.arange(0, half, 2, dtype=jnp.float32) / half)
    ang_r = row[:, None] * inv_freq
    ang_c = col[:, None] * inv_freq
    ang = jnp.concatenate([ang_r, ang_r, ang_c, ang_c], axis=-1)
    return jnp.cos(ang), jnp.sin(ang)

def _apply_rope(x, cos, sin):
    x32 = x.astype(jnp.float32)
    a1, a2, b1, b2 = jnp.split(x32, 4, axis=-1)
    rot = jnp.concatenate([-a2, a1, -b2, b1], axis=-1)
    c = cos[None, :, None, None, :]
    s = sin[None, :, None, None, :]
    return (x32 * c + rot * s).astype(x.dtype)

def _centred_conv(x, w):
    return lax.conv_general_dilated(
        x, w[:, None, :].astype(x.dtype), window_strides=(1,),
        padding=((CONV_K // 2, CONV_K // 2),),
        dimension_numbers=('NWC', 'WIO', 'NWC'),
        feature_group_count=x.shape[-1])

def _diff_attend(q, k, v, lam):
    s = jnp.einsum('bqhmd,bkhmd->bhmqk', q, k).astype(jnp.float32) * (A_HD ** -0.5)
    p = jax.nn.softmax(s, axis=-1)
    w = p[:, :, 0] - lam * p[:, :, 1]
    return jnp.einsum('bhqk,bkhe->bqhe', w.astype(v.dtype), v)

def _diff_attn_branch(lat, ctx, lam_vec, lam_init, gain, cos, sin, need_ctx_out):
    q, k, v = lat
    qc, kc, vc = ctx
    B, n, _ = q.shape
    nc = qc.shape[1]
    q5 = _apply_rope(q.reshape(B, n, A_HEADS, 2, A_HD), cos, sin)
    k5 = _apply_rope(k.reshape(B, n, A_HEADS, 2, A_HD), cos, sin)
    kc5 = kc.reshape(B, nc, A_HEADS, 2, A_HD)
    vc4 = vc.reshape(B, nc, A_HEADS, A_VD)
    lam_vec = lam_vec.astype(jnp.float32)
    lam = (jnp.exp(jnp.sum(lam_vec[0] * lam_vec[1])) -
           jnp.exp(jnp.sum(lam_vec[2] * lam_vec[3])) + lam_init)
    k_all = jnp.concatenate([k5, kc5], axis=1)
    v_all = jnp.concatenate([v.reshape(B, n, A_HEADS, A_VD), vc4], axis=1)
    nb = n // Q_BLOCK
    qb = jnp.moveaxis(q5.reshape(B, nb, Q_BLOCK, A_HEADS, 2, A_HD), 1, 0)
    o = lax.map(lambda blk: _diff_attend(blk, k_all, v_all, lam), qb)
    o = jnp.moveaxis(o, 0, 1).reshape(B, n, A_HEADS, A_VD)

    def post(t):
        return (_rmsnorm(t, gain) * (1.0 - lam_init)).reshape(t.shape[0], t.shape[1], A_VW)

    y = post(o)
    yc = post(_diff_attend(qc.reshape(B, nc, A_HEADS, 2, A_HD), kc5, vc4, lam)) if need_ctx_out else None
    return y, yc

def _to_chunks(t, n_chunks):
    shp = t.shape
    t = t.reshape(shp[0], shp[1], n_chunks, CHUNK, *shp[3:])
    return jnp.moveaxis(t, 2, 0)

def _from_chunks(t):
    t = jnp.moveaxis(t, 0, 2)
    return t.reshape(t.shape[0], t.shape[1], -1, *t.shape[4:])

def _mlstm_scan(q, k, v, log_i, log_f, state, with_output):
    f32 = jnp.float32
    n_chunks = q.shape[2] // CHUNK
    xs = tuple(_to_chunks(t.astype(f32), n_chunks)
               for t in (q, k.astype(f32) * (M_QK ** -0.5), v, log_i, log_f))
    causal = jnp.tril(jnp.ones((CHUNK, CHUNK), dtype=bool))

    def body(carry, blk):
        C, nv, m = carry
        qc, kc, vc, ic, fc = blk
        b = jnp.cumsum(fc, axis=-1)
        b_end = b[..., -1]
        a = b_end[..., None] - b + ic
        m_new = jnp.maximum(b_end + m, jnp.max(a, axis=-1))
        carry_w = jnp.exp(b_end + m - m_new)
        key_w = jnp.exp(a - m_new[..., None])
        C_new = carry_w[..., None, None] * C + jnp.einsum('bhs,bhsk,bhsv->bhkv', key_w, kc, vc)
        n_new = carry_w[..., None] * nv + jnp.einsum('bhs,bhsk->bhk', key_w, kc)
        if not with_output:
            return (C_new, n_new, m_new), None
        d = jnp.where(causal, b[..., :, None] - b[..., None, :] + ic[..., None, :], -jnp.inf)
        inter = b + m[..., None]
        m_row = jnp.maximum(inter, jnp.max(d, axis=-1))
        w = jnp.exp(d - m_row[..., None])
        e_inter = jnp.exp(inter - m_row)
        s = jnp.einsum('bhjk,bhsk->bhjs', qc, kc) * w
        num = (jnp.einsum('bhjs,bhsv->bhjv', s, vc) +
               e_inter[..., None] * jnp.einsum('bhjk,bhkv->bhjv', qc, C))
        den = jnp.sum(s, axis=-1) + e_inter * jnp.einsum('bhjk,bhk->bhj', qc, nv)
        h = num / jnp.maximum(jnp.abs(den), jnp.exp(-m_row))[..., None]
        return (C_new, n_new, m_new), h

    state, h = lax.scan(body, state, xs)
    out = _from_chunks(h).astype(v.dtype) if with_output else None
    return out, state

def _mlstm_branch(lat, ctx, f_bias, gain, need_ctx_out):
    f32 = jnp.float32

    def prep(q, k, v, o, gates):
        gi_f, gf_f, gi_b, gf_b = [jnp.moveaxis(t, 2, 1) for t in jnp.split(gates.astype(f32), 4, axis=-1)]
        lf_f = jax.nn.log_sigmoid(gf_f + f_bias[0][:, None])
        lf_b = jax.nn.log_sigmoid(gf_b + f_bias[1][:, None])
        return _heads(q, M_HEADS), _heads(k, M_HEADS), _heads(v, M_HEADS), gi_f, lf_f, gi_b, lf_b, o

    def post(h_f, h_b_rev, o):
        h = _rmsnorm(h_f + _flip(h_b_rev), gain[:, None, :])
        return _merge_heads(h) * jax.nn.sigmoid(o)

    B = lat[0].shape[0]
    zero = (jnp.zeros((B, M_HEADS, M_QK, M_V), f32), jnp.zeros((B, M_HEADS, M_QK), f32),
            jnp.zeros((B, M_HEADS), f32))
    qc, kc, vc, icf, lfcf, icb, lfcb, oc = prep(*ctx)
    hc_f, st_f = _mlstm_scan(qc, kc, vc, icf, lfcf, zero, need_ctx_out)
    hc_b, st_b = _mlstm_scan(_flip(qc), _flip(kc), _flip(vc), _flip(icb), _flip(lfcb), zero, need_ctx_out)
    q, k, v, i_f, lf_f, i_b, lf_b, o = prep(*lat)
    h_f, _ = _mlstm_scan(q, k, v, i_f, lf_f, st_f, True)
    h_b, _ = _mlstm_scan(_flip(q), _flip(k), _flip(v), _flip(i_b), _flip(lf_b), st_b, True)
    y = post(h_f, h_b, o)
    yc = post(hc_f, hc_b, oc) if need_ctx_out else None
    return y, yc

def _gdn_scan(q, k, v, g, beta, S, with_output):
    f32 = jnp.float32
    n_chunks = q.shape[2] // CHUNK

    def chunk(t):
        shp = t.shape
        return t.astype(f32).reshape(shp[0], shp[1], n_chunks, CHUNK, *shp[3:])

    qc, kc, vc, gcn, bc = [chunk(t) for t in (q, k, v, g, beta)]
    gcum = jnp.cumsum(gcn, axis=-1)
    incl = jnp.tril(jnp.ones((CHUNK, CHUNK), dtype=bool))
    strict = jnp.tril(jnp.ones((CHUNK, CHUNK), dtype=bool), -1)
    diff = gcum[..., :, None] - gcum[..., None, :]
    decay = jnp.where(incl, jnp.exp(jnp.where(incl, diff, 0.0)), 0.0)
    kb = kc * bc[..., None]
    A = jnp.where(strict, jnp.einsum('bhnid,bhnjd->bhnij', kb, kc) * decay, 0.0)
    eye = jnp.eye(CHUNK, dtype=f32)
    T = lax.linalg.triangular_solve(A + eye, jnp.broadcast_to(eye, A.shape),
                                    left_side=True, lower=True, unit_diagonal=True)
    u = jnp.einsum('bhnij,bhnjv->bhniv', T, vc * bc[..., None])
    w = jnp.einsum('bhnij,bhnjk->bhnik', T, kb * jnp.exp(gcum)[..., None])
    g_end = gcum[..., -1]
    k_end = kc * jnp.exp(g_end[..., None] - gcum)[..., None]
    xs = [u, w, k_end, g_end]
    if with_output:
        qk = jnp.where(incl, jnp.einsum('bhnid,bhnjd->bhnij', qc, kc) * decay, 0.0)
        xs += [qc * jnp.exp(gcum)[..., None], qk]
    xs = tuple(jnp.moveaxis(t, 2, 0) for t in xs)

    def body(S, blk):
        u_c, w_c, ke_c, ge_c = blk[:4]
        v_new = u_c - jnp.einsum('bhlk,bhkv->bhlv', w_c, S)
        S_new = S * jnp.exp(ge_c)[..., None, None] + jnp.einsum('bhlk,bhlv->bhkv', ke_c, v_new)
        if not with_output:
            return S_new, None
        q_c, qk_c = blk[4:]
        o = jnp.einsum('bhlk,bhkv->bhlv', q_c, S) + jnp.einsum('bhij,bhjv->bhiv', qk_c, v_new)
        return S_new, o

    S, o = lax.scan(body, S.astype(f32), xs)
    out = _from_chunks(o).astype(v.dtype) if with_output else None
    return out, S

def _gdn_branch(lat, ctx, conv_w, a_log, dt_bias, gain, need_ctx_out):
    f32 = jnp.float32

    def prep(q, k, v, z, gates):
        qkv = jax.nn.silu(_centred_conv(jnp.concatenate([q, k, v], axis=-1), conv_w))
        q, k, v = jnp.split(qkv, 3, axis=-1)
        q = _l2norm(_heads(q, G_HEADS)) * (G_HD ** -0.5)
        k = _l2norm(_heads(k, G_HEADS))
        v = _heads(v, G_HEADS)
        a_f, a_b, b_f, b_b = [jnp.moveaxis(t, 2, 1) for t in jnp.split(gates.astype(f32), 4, axis=-1)]
        g_f = -jnp.exp(a_log[0])[:, None] * jax.nn.softplus(a_f + dt_bias[0][:, None])
        g_b = -jnp.exp(a_log[1])[:, None] * jax.nn.softplus(a_b + dt_bias[1][:, None])
        return q, k, v, g_f, jax.nn.sigmoid(b_f), g_b, jax.nn.sigmoid(b_b), z

    def post(o_f, o_b_rev, z):
        o = _rmsnorm(o_f + _flip(o_b_rev), gain)
        return _merge_heads(o) * jax.nn.silu(z)

    B = lat[0].shape[0]
    zero = jnp.zeros((B, G_HEADS, G_HD, G_HD), f32)
    qc, kc, vc, gcf, bcf, gcb, bcb, zc = prep(*ctx)
    oc_f, st_f = _gdn_scan(qc, kc, vc, gcf, bcf, zero, need_ctx_out)
    oc_b, st_b = _gdn_scan(_flip(qc), _flip(kc), _flip(vc), _flip(gcb), _flip(bcb), zero, need_ctx_out)
    q, k, v, g_f, b_f, g_b, b_b, z = prep(*lat)
    o_f, _ = _gdn_scan(q, k, v, g_f, b_f, st_f, True)
    o_b, _ = _gdn_scan(_flip(q), _flip(k), _flip(v), _flip(g_b), _flip(b_b), st_b, True)
    y = post(o_f, o_b, z)
    yc = post(oc_f, oc_b, zc) if need_ctx_out else None
    return y, yc

def _merge_branches(ya, ym, yg, gates, w_branch, w_out):
    ga, gm, gg = jnp.split(jax.nn.sigmoid(gates), 3, axis=-1)
    y = ga * (ya @ w_branch[0]) + gm * (ym @ w_branch[1]) + gg * (yg @ w_branch[2])
    return y @ w_out

def _sq_relu_mlp(h, w1, w2):
    return jnp.square(jax.nn.relu(h @ w1)) @ w2

def _layer(x, cx, c_silu, cctx_silu, w_ada, b_ada, norm_gains, w_in, b_in, a_lambda, a_norm,
           m_fbias, m_norm, g_conv, g_alog, g_dtbias, g_norm, w_branch, w_out, w_ff1, w_ff2,
           lam_init, cos, sin, need_ctx_out):
    sh1, sc1, gt1, sh2, sc2, gt2 = [t[:, None, :] for t in jnp.split(c_silu @ w_ada + b_ada, 6, axis=-1)]
    sh1c, sc1c, gt1c, sh2c, sc2c, gt2c = jnp.split(cctx_silu @ w_ada + b_ada, 6, axis=-1)
    split_idx = np.cumsum(IN_SPLITS)[:-1].tolist()

    h = _rmsnorm(x, norm_gains[0]) * (1.0 + sc1) + sh1
    hc = _rmsnorm(cx, norm_gains[0]) * (1.0 + sc1c) + sh1c
    p = jnp.split(h @ w_in + b_in, split_idx, axis=-1)
    pc = jnp.split(hc @ w_in + b_in, split_idx, axis=-1)
    ya, yac = _diff_attn_branch(p[0:3], pc[0:3], a_lambda, lam_init, a_norm, cos, sin, need_ctx_out)
    ym, ymc = _mlstm_branch(p[3:8], pc[3:8], m_fbias, m_norm, need_ctx_out)
    yg, ygc = _gdn_branch(p[8:13], pc[8:13], g_conv, g_alog, g_dtbias, g_norm, need_ctx_out)
    x = x + gt1 * _rmsnorm(_merge_branches(ya, ym, yg, p[13], w_branch, w_out), norm_gains[1])

    h2 = _rmsnorm(x, norm_gains[2]) * (1.0 + sc2) + sh2
    x = x + gt2 * _rmsnorm(_sq_relu_mlp(h2, w_ff1, w_ff2), norm_gains[3])

    if need_ctx_out:
        cx = cx + gt1c * _rmsnorm(_merge_branches(yac, ymc, ygc, pc[13], w_branch, w_out), norm_gains[1])
        h2c = _rmsnorm(cx, norm_gains[2]) * (1.0 + sc2c) + sh2c
        cx = cx + gt2c * _rmsnorm(_sq_relu_mlp(h2c, w_ff1, w_ff2), norm_gains[3])
    return x, cx

def setup_inputs(seed: int = 0) -> dict:
    key = jax.random.key(seed)
    ks = jax.random.split(key, 24)
    f32 = jnp.float32

    def nrm(k, shape, scale):
        return jax.random.normal(k, shape, f32) * scale

    dt = jnp.exp(jax.random.uniform(ks[15], (DEPTH, 2, G_HEADS), f32, math.log(1e-3), math.log(1e-1)))
    return {
        'x': nrm(ks[0], (BATCH, SEQ, D_MODEL), 1.0),
        'c': nrm(ks[1], (BATCH, D_MODEL), 1.0),
        'ctx': nrm(ks[2], (BATCH, CTX_LEN, D_MODEL), 1.0),
        'c_ctx': nrm(ks[3], (D_MODEL,), 1.0),
        'w_ada': nrm(ks[4], (DEPTH, D_MODEL, 6 * D_MODEL), 0.5 * D_MODEL ** -0.5),
        'b_ada': nrm(ks[5], (DEPTH, 6 * D_MODEL), 0.02),
        'norm_gains': 1.0 + nrm(ks[6], (DEPTH, 4, D_MODEL), 0.02),
        'w_in': nrm(ks[7], (DEPTH, D_MODEL, D_IN), D_MODEL ** -0.5),
        'b_in': nrm(ks[8], (DEPTH, D_IN), 0.02),
        'a_lambda': nrm(ks[9], (DEPTH, 4, A_HD), 0.1),
        'a_norm': 1.0 + nrm(ks[10], (DEPTH, A_VD), 0.02),
        'm_fbias': jnp.linspace(3.0, 6.0, M_HEADS, dtype=f32)[None, None, :] + nrm(ks[11], (DEPTH, 2, M_HEADS), 0.1),
        'm_norm': 1.0 + nrm(ks[12], (DEPTH, M_HEADS, M_V), 0.02),
        'g_conv': nrm(ks[13], (DEPTH, CONV_K, 3 * G_W), CONV_K ** -0.5),
        'g_alog': jnp.log(jax.random.uniform(ks[14], (DEPTH, 2, G_HEADS), f32, 1.0, 16.0)),
        'g_dtbias': dt + jnp.log(-jnp.expm1(-dt)),
        'g_norm': 1.0 + nrm(ks[16], (DEPTH, G_HD), 0.02),
        'w_branch': nrm(ks[17], (DEPTH, 3, BRANCH_W, D_MODEL), BRANCH_W ** -0.5),
        'w_out': nrm(ks[18], (DEPTH, D_MODEL, D_MODEL), D_MODEL ** -0.5),
        'w_ff1': nrm(ks[19], (DEPTH, D_MODEL, D_FF), D_MODEL ** -0.5),
        'w_ff2': nrm(ks[20], (DEPTH, D_FF, D_MODEL), D_FF ** -0.5),
    }

def reference(x, c, ctx, c_ctx, w_ada, b_ada, norm_gains, w_in, b_in, a_lambda, a_norm,
              m_fbias, m_norm, g_conv, g_alog, g_dtbias, g_norm, w_branch, w_out, w_ff1, w_ff2):
    cos, sin = _grid_rope_tables(x.shape[1])
    c_silu = jax.nn.silu(c)
    cctx_silu = jax.nn.silu(c_ctx)
    cx = ctx
    for i in range(DEPTH):
        lam_init = 0.8 - 0.6 * math.exp(-0.3 * i)
        x, cx = _layer(x, cx, c_silu, cctx_silu, w_ada[i], b_ada[i], norm_gains[i], w_in[i], b_in[i],
                       a_lambda[i], a_norm[i], m_fbias[i], m_norm[i], g_conv[i], g_alog[i],
                       g_dtbias[i], g_norm[i], w_branch[i], w_out[i], w_ff1[i], w_ff2[i],
                       lam_init, cos, sin, i < DEPTH - 1)
    return x


_drawn_inputs = setup_inputs


def setup_inputs(seed=0):
    import zlib

    import numpy as np

    out = dict(_drawn_inputs(seed))
    spreads = {}
    factors = {'a_lambda': 4.987, 'a_norm': 8.0, 'm_norm': 8.0, 'g_norm': 8.0}
    for name, (base, spread) in spreads.items():
        noise = np.random.default_rng([zlib.crc32(name.encode()), seed]).standard_normal(out[name].shape)
        drawn = base * np.exp(spread * noise) if base else spread * noise
        out[name] = __import__('jax').numpy.asarray(drawn.astype(out[name].dtype))
    for name, factor in factors.items():
        out[name] = (out[name] * factor).astype(out[name].dtype)
    return out
```

```python
import math
from contextlib import ExitStack

import numpy as np

import concourse.bass as bass
from concourse import mybir

F32 = mybir.dt.float32
BF16 = mybir.dt.bfloat16
U8 = mybir.dt.uint8
ALU = mybir.AluOpType
ACT = mybir.ActivationFunctionType
AX_X = mybir.AxisListType.X

P = 128
DEPTH, DM, CTX, LAT = 2, 1024, 256, 256
TOK = CTX + LAT
KD = DM // P
NT = TOK // P
HEADS, A_HD, M_QK, M_V, G_HD = 4, 64, 64, 128, 128
CONV_K, D_FF, GRID_W = 5, 4096, 64
FT = D_FF // P
EPS = 1e-6
LEVELS = 7
RING = 3
CW = 4096

A_Q, A_K, A_V = 0, 512, 1024
M_QKC, M_VC, M_O, M_GATES = 1536, 2048, 2560, 3072
G_Q, G_K, G_V, G_Z, G_GATES, BR_G = 3088, 3600, 4112, 4624, 5136, 5152

B_AQ, B_AK, B_MQ, B_MK, B_MO, B_GQ, B_GZ, B_BG, B_ADA, R_C = 0, 4, 8, 10, 12, 16, 28, 32, 56, 104
R_GAIN, R_CONV, R_AN, R_MN, R_GN = 0, 32, 92, 93, 97

UNITS = [(0, 0), (1, 1), (0, 1), (1, 0), (0, 2), (1, 3), (0, 3), (1, 2)]
FIRST_VISIT = {0, 1, 4, 5}


def shape_constants():
    k = np.arange(P)
    ident = np.eye(P, dtype=np.float32)
    tri_f = (k[:, None] <= k[None, :]).astype(np.float32)
    tri_b = (k[:, None] >= k[None, :]).astype(np.float32)
    rope = np.zeros((P, P), np.float32)
    for m in range(P):
        if (m // 16) % 2 == 0:
            rope[m + 16, m] = -1.0
        else:
            rope[m - 16, m] = 1.0
    half = A_HD // 2
    inv_freq = np.float32(10000.0) ** (-np.arange(0, half, 2, dtype=np.float32) / np.float32(half))
    tok = np.arange(LAT)
    row, col = (tok // GRID_W).astype(np.float32), (tok % GRID_W).astype(np.float32)
    ar, ac = row[:, None] * inv_freq, col[:, None] * inv_freq
    ang = np.concatenate([ar, ar, ac, ac] * 2, axis=-1).T.astype(np.float32)
    pair = ((k[:, None] // 2 == k[None, :] // 2) & (k[:, None] < k[None, :])).astype(np.float32)
    sel = np.zeros((P, HEADS, P), np.float32)
    selp = np.zeros((P, 2, P), np.float32)
    for h in range(HEADS):
        sel[h, h, :] = 1.0
        selp[h, h // 2, 64 * (h % 2):64 * (h % 2) + 64] = 1.0
    f = np.concatenate([ident, tri_f, tri_b, rope, np.cos(ang), np.sin(ang),
                        sel.reshape(P, -1), selp.reshape(P, -1), pair, pair.T], axis=1).astype(np.float32)
    b = np.stack([ident, (1 - tri_f) * -1e30, (1 - tri_b) * -1e30], axis=1).astype(np.float32)
    m = np.zeros((P, 2, LEVELS - 1, P), np.float32)
    for lv in range(1, LEVELS):
        blk = k >> lv
        up = (blk[:, None] // 2 == blk[None, :] // 2) & (blk[:, None] % 2 == 0) & (blk[None, :] % 2 == 1)
        m[:, 0, lv - 1], m[:, 1, lv - 1] = up, up.T
    return f, b, m


def plan():
    segs, chunks, where = [], [], {}
    taken = {"act": 0, "dve": 0}

    def chunk(l, kind, i):
        chunks.append([l, kind, i, None])
        return len(chunks) - 1

    def seg(l, kind, i, c, engine, bank=None, evacuated=True):
        n = len(segs)
        if evacuated:
            taken[engine] += 1
        normal = [s for s in segs if s[4] < 2 and s[1] != "ff2"]
        segs.append((l, kind, i, c, len(normal) % 2 if bank is None else bank,
                     engine if evacuated else None, taken[engine]))
        if c is not None:
            chunks[c][3] = n
        where.setdefault((l, kind), []).append(n)

    for l in range(DEPTH):
        for n in range(12):
            seg(l, "ada", n, chunk(l, "ada", n), "act")
        seg(l, "gate", 0, None, "dve")
        for kind, engine in (("gq", "act"), ("gk", "act"), ("gv", "act"), ("gz", "dve"),
                             ("mqk", "dve"), ("mv", "dve"), ("mo", "act"),
                             ("aq", "dve"), ("ak", "dve"), ("av", "dve")):
            c = chunk(l, kind, 0)
            for i in range(4):
                seg(l, kind, i, c, engine)
        for b in (2, 1, 0):
            wb = chunk(l, "wb", b)
            for nb in range(2):
                bg = chunk(l, "bg", (b, nb))
                for i in range(4):
                    seg(l, "bg", (b, 4 * nb + i), bg, "act")
                    seg(l, "by", (b, 4 * nb + i), wb, "dve")
        for nb in range(2):
            c = chunk(l, "wo", nb)
            for i in range(4):
                seg(l, "wo", 4 * nb + i, c, "act")
        for n in range(8):
            c = chunk(l, "ff1", n)
            for i in range(4):
                seg(l, "ff1", 4 * n + i, c, "act")
        for nb in range(2):
            for kc in range(4):
                c = chunk(l, "ff2", (nb, kc))
                for i in range(4):
                    seg(l, "ff2", (nb, kc, i), c, "act", bank=2 + (4 * nb + i) % 6 if nb == 0 or i < 2 else i - 2,
                        evacuated=kc == 3)
    return segs, chunks, where


def hybrid_trunk(nc, x, c, ctx, c_ctx, w_ada, b_ada, norm_gains, w_in, b_in, a_lambda, a_norm,
                 m_fbias, m_norm, g_conv, g_alog, g_dtbias, g_norm, w_branch, w_out, w_ff1, w_ff2,
                 const_f, const_b, const_m, out):
    SEGS, CHUNKS, WHERE = plan()

    def tokens(l):
        return (0, TOK) if l < DEPTH - 1 else (CTX, LAT)

    with ExitStack() as stack:
        def sb(name, shape, dt=F32):
            return stack.enter_context(nc.sbuf_tensor(name, shape, dt))

        def sem(name):
            return stack.enter_context(nc.semaphore(name))

        bank = [stack.enter_context(nc.psum_tensor(f"bank{i}", [P, 512], F32)) for i in range(8)]

        cf = sb("cf", [P, 4 * P + 2 * LAT + 8 * P])
        ident, tri = cf[:, 0:P], [cf[:, P:2 * P], cf[:, 2 * P:3 * P]]
        rope_r = cf[:, 3 * P:4 * P]
        cos_t, sin_t = cf[:, 512:768], cf[:, 768:1024]
        sel = [cf[0:4, 1024 + h * P:1024 + (h + 1) * P] for h in range(HEADS)]
        selp = [cf[0:4, 1536 + i * P:1536 + (i + 1) * P] for i in range(2)]
        pair_mask = [cf[:, 1792 + d * P:1792 + (d + 1) * P] for d in range(2)]
        cb = sb("cb", [P, 3, P], BF16)
        ident_b = cb[:, 0, :]
        mask_b = [cb[:, 1 + d, :].unsqueeze(1).broadcast_to((P, HEADS, P)) for d in range(2)]
        cm = sb("cm", [P, 2, LEVELS - 1, P], U8)
        ones = sb("ones", [P, P])
        cols1 = sb("cols1", [P, DEPTH, P])
        cols2 = sb("cols2", [P, DEPTH, P])
        gate_bias = sb("gate_bias", [P, DEPTH, 32])
        fdt_bias = sb("fdt_bias", [P, DEPTH, 16])
        alog = sb("alog", [P, DEPTH, 8])
        v_bias = sb("v_bias", [P, 2, 512])
        w_gates = sb("w_gates", [P, KD, 32])

        xt = sb("xt", [P, KD, TOK])
        ht = sb("ht", [P, KD, TOK])
        ring = sb("ring", [P, RING, CW])
        arena = sb("arena", [P, 19480])
        work = sb("work", [P, 10, 512])

        def part(at, n):
            return arena[:, at:at + n]

        gq = part(0, 2048).rearrange("p (h t) -> p h t", h=4)
        gk = part(2048, 2048).rearrange("p (h t) -> p h t", h=4)
        gz = part(4096, 2048).rearrange("p (h t) -> p h t", h=4)
        gk_tok = part(6144, 2048).rearrange("p (t c) -> p t c", t=NT)
        gv_tok = part(8192, 2048).rearrange("p (t c) -> p t c", t=NT)
        oacc = part(10240, 2048).rearrange("p (t c) -> p t c", t=NT)
        raw = part(14336, 1560).rearrange("p (r s c) -> p r s c", r=3, s=2)
        mq = part(12288, 1024).rearrange("p (i t) -> p i t", i=2)
        mk = part(13312, 1024).rearrange("p (i t) -> p i t", i=2)
        mo = part(14336, 2048).rearrange("p (h t) -> p h t", h=4)
        mv = part(16384, 2064).rearrange("p (t h c) -> p t h c", t=NT, h=4)
        mk_tok = part(18448, 1024).rearrange("p (t c) -> p t c", t=NT)
        aq, ak, av = gq, gk, gk_tok
        hidden = part(0, 16384).rearrange("p (f t) -> p f t", f=FT)
        ot_of = {1: part(0, 4096).rearrange("p (k t) -> p k t", k=KD), 3: work[:, 0:8, :]}
        level_masks = part(1024, 2 * (LEVELS - 1) * P)
        rows1 = part(0, DEPTH * P).rearrange("p (l c) -> p l c", l=DEPTH)
        rows2 = part(256, DEPTH * P).rearrange("p (l c) -> p l c", l=DEPTH)
        lamv = part(512, DEPTH * 4 * A_HD).rearrange("p (l a c) -> p l a c", l=DEPTH, a=4)
        merged = work[:, 0:8, :]
        gate_sig = [part(12288, 512), part(12800, 512)]
        gated = [part(13312, 512), part(13824, 512)]

        silu_c = sb("silu_c", [P, 2, KD])
        ada = sb("ada", [P, 48, 2])
        mod_scale = sb("mod_scale", [P, 2, KD, 2])
        out_gate = sb("out_gate", [P, 2, KD, 2])
        gates = sb("gates", [P, NT, 32])
        zgate = sb("zgate", [P, NT, 16])
        egate = sb("egate", [P, NT, 16])
        lgate = sb("lgate", [P, NT, 16])
        coef = sb("coef", [P, 16])
        beta = sb("beta", [P, NT, 8])
        nbeta = sb("nbeta", [P, NT, 8])
        lam2 = sb("lam2", [P, DEPTH, 2])
        nlam = sb("nlam", [P, DEPTH])
        gcol = sb("gcol", [P, 12])
        gecol = sb("gecol", [P, 16])
        gstate = sb("gstate", [P, 2, HEADS, G_HD])
        row_buf = sb("row_buf", [P, 8, P])
        mrow = row_buf[0:4, :, :]
        grow = mrow[:, 0:3, :]
        rstd = row_buf[:, 0:4, :].rearrange("p a c -> p (a c)")
        ada_rows = mrow[0:2, :, :].rearrange("p (a b) c -> p a (b c)", a=2)
        mmax = sb("mmax", [4, 2])
        mcol = sb("mcol", [P, 16])
        mden = sb("mden", [P, 8])
        mstate = sb("mstate", [P, 2, 2, M_V + 1])
        amax = sb("amax", [P, 2, 8])
        post_stat = sb("post_stat", [P, NT, HEADS])

        names = (
            "consts_in params_in rows_in x_in chunk_in0 chunk_in1 chunk_in2 gatew_in vbias_in out_stored "
            "ones_set masks_ready pads_set states_zero "
            "dense_ready taken_act taken_dve act_step dve_step pool_step "
            "cols_psum cols_ready csig silu_ready ada_cols ada_ready "
            "xtr_psum xtr_ready lam_sum lam_exp lam_ready "
            "sq_ready sq_used norm_sum norm_root rstd_ready scaled_ready h_ready "
            "gates_z gates_exp gates_ready gate_segment_done "
            "conv_done conv_sig conv_out vt_psum vt_out l2_sq l2_sum l2_root l2_out kt_psum kt_out "
            "gz_sig "
            "gd_small gd_rows gd_cols gd_ecol gd_neg gd_ke gd_arg gd_decay gd_qk gd_b gd_qkd gd_u0 gd_t0 "
            "gd_t1 gd_m gd_mout gd_up gd_uout gd_tout gd_w gd_wout gd_qb gd_qg gd_v gd_vn gd_o gd_oacc "
            "gd_s gd_state "
            "ml_small ml_rows ml_exp ml_cols ml_ecol ml_arg ml_decay ml_qk ml_p ml_qb ml_qg ml_kw ml_num "
            "ml_h ml_c ml_state mkt_psum mkt_out "
            "post_sq post_sum post_root post_norm post_tr post_out "
            "rope_psum rope_out at_s at_max at_e at_w at_wt at_wtout at_o at_oout "
            "y_ready hid_ready res_ready final_psum final_out"
        ).split()
        S = {n: sem(n) for n in names}

        block = stack.enter_context(nc.Block())

        out_units = [[u for u in range(8) if l < DEPTH - 1 or UNITS[u][1] >= 2] for l in range(DEPTH)]

        def sofar(counts, l):
            return sum(counts[:l])

        def evacuated(eng, n):
            eng.wait_ge(S["taken_" + SEGS[n][5]], SEGS[n][6])

        def seg_of(l, kind, i=-1):
            return WHERE[(l, kind)][i]

        def token_tiles(l):
            t0, n = tokens(l)
            return list(range(t0 // P, (t0 + n) // P))

        def seg_tokens(l, kind):
            return (0, TOK) if kind in ("gk", "gv", "mqk", "ak") else tokens(l)

        def post_count(l, b):
            return 3 * NT * l + {2: 0, 1: 1, 0: 2}[b] * len(token_tiles(l))

        def attn_units(l):
            return sum(4 * len(token_tiles(k)) for k in range(l))

        def norm_count(l, which):
            return 4 * l + which

        def scaled_count(l, which):
            return 2 * KD * l + KD * (which // 2)

        def mlstm_c(i):
            return bank[3][:, 129 * i:129 * i + 129]

        @block.sync
        def _(sp):
            sp.dma_start(cf[:, :], const_f).then_inc(S["consts_in"], 16)
            sp.dma_start(work[:, 8, 0:3 * P].rearrange("p (a c) -> p a c", a=3), const_b).then_inc(S["consts_in"], 16)
            sp.dma_start(level_masks, const_m.rearrange("p a b c -> p (a b c)")).then_inc(S["consts_in"], 16)
            rows_of = lambda v: v.rearrange("(j p) -> j p", p=P)
            for l in range(DEPTH):
                table1 = [(0, b_in[l, 0:1024]), (8, b_in[l, 1536:2048]), (12, b_in[l, M_O:M_O + 512]),
                          (16, b_in[l, G_Q:G_Q + 2048]), (B_BG, b_in[l, BR_G:BR_G + 3072]),
                          (B_ADA, b_ada[l, :]), (R_C, c[0, :]), (R_C + 8, c_ctx[:])]
                for r, src in table1:
                    v = rows_of(src)
                    sp.dma_start(rows1[r:r + v.shape[0], l, :], v).then_inc(S["rows_in"], 16)
                sp.dma_start(rows2[0:32, l, :], norm_gains[l].rearrange("g (j p) -> (g j) p", p=P)).then_inc(S["rows_in"], 16)
                sp.dma_start(rows2[R_CONV:R_CONV + 60, l, :],
                             g_conv[l].rearrange("k (j p) -> (k j) p", p=P)).then_inc(S["rows_in"], 16)
                sp.dma_start(rows2[R_AN:R_AN + 1, l, :], a_norm[l:l + 1, :]).then_inc(S["rows_in"], 16)
                sp.dma_start(rows2[R_MN:R_MN + 4, l, :], m_norm[l]).then_inc(S["rows_in"], 16)
                sp.dma_start(rows2[R_GN:R_GN + 1, l, :], g_norm[l:l + 1, :]).then_inc(S["rows_in"], 16)
            sp.dma_start(ht[:, 0:4, :].rearrange("p (t a) c -> p t (a c)", t=2),
                         ctx[0].rearrange("(t p) c -> p t c", p=P)).then_inc(S["x_in"], 16)
            sp.dma_start(ht[:, 4:8, :].rearrange("p (t a) c -> p t (a c)", t=2),
                         x[0].rearrange("(t p) c -> p t c", p=P)).then_inc(S["x_in"], 16)

            def chunk_source(l, kind, i):
                tall = lambda w: w.rearrange("(k p) n -> p k n", p=P)
                cols = {"gq": G_Q, "gk": G_K, "gv": G_V, "gz": G_Z, "mqk": M_QKC, "mv": M_VC, "mo": M_O,
                        "aq": A_Q, "ak": A_K, "av": A_V}
                if kind == "ada":
                    return tall(w_ada[l][:, 512 * i:512 * i + 512]), 8
                if kind in cols:
                    return tall(w_in[l][:, cols[kind]:cols[kind] + 512]), 8
                if kind == "bg":
                    at = BR_G + 1024 * i[0] + 512 * i[1]
                    return tall(w_in[l][:, at:at + 512]), 8
                if kind == "wb":
                    return tall(w_branch[l, i]), 4
                if kind == "wo":
                    return tall(w_out[l][:, 512 * i:512 * i + 512]), 8
                if kind == "ff1":
                    return tall(w_ff1[l][:, 512 * i:512 * i + 512]), 8
                return tall(w_ff2[l][1024 * i[1]:1024 * i[1] + 1024, 512 * i[0]:512 * i[0] + 512]), 8

            for n, (l, kind, i, _) in enumerate(CHUNKS):
                if n >= RING:
                    sp.wait_ge(S["dense_ready"], CHUNKS[n - RING][3] + 1)
                src, k = chunk_source(l, kind, i)
                sp.dma_start(ring[:, n % RING, :].rearrange("p (k n) -> p k n", k=k), src)\
                    .then_inc(S[f"chunk_in{n % RING}"], 16)
                if kind == "ada" and i == 11:
                    if l > 0:
                        sp.wait_ge(S["dense_ready"], seg_of(l - 1, "gate") + 1)
                        evacuated(sp, seg_of(l - 1, "av"))
                    tall = lambda w: w.rearrange("(k p) n -> p k n", p=P)
                    sp.dma_start(w_gates[:, :, 0:16], tall(w_in[l][:, M_GATES:M_GATES + 16])).then_inc(S["gatew_in"], 16)
                    sp.dma_start(w_gates[:, :, 16:32], tall(w_in[l][:, G_GATES:G_GATES + 16])).then_inc(S["gatew_in"], 16)
                    sp.dma_start(v_bias[:, 0, :], b_in[l, A_V:A_V + 512].partition_broadcast(P)).then_inc(S["vbias_in"], 16)
                    sp.dma_start(v_bias[:, 1, :], b_in[l, M_VC:M_VC + 512].partition_broadcast(P)).then_inc(S["vbias_in"], 16)
            for t in range(2):
                sp.wait_ge(S["final_out"], 2 * t + 2)
                sp.dma_start(out[0, t * P:(t + 1) * P, :],
                             work[:, 2 * t:2 * t + 2, :].rearrange("p a c -> p (a c)")).then_inc(S["out_stored"], 16)
            sp.wait_ge(S["out_stored"], 32)

        @block.gpsimd
        def _(pool):
            steps = [0]

            def link(ins):
                steps[0] += 1
                ins.then_inc(S["pool_step"], 1)
                pool.wait_ge(S["pool_step"], steps[0])

            nc.gpsimd.memset(ones[:, :], 1.0).then_inc(S["ones_set"], 1)
            for l in range(DEPTH):
                flat = lambda v: v.rearrange("a b -> (a b)").partition_broadcast(P)
                pool.dma_start(gate_bias[:, l, 0:16], b_in[l, M_GATES:M_GATES + 16].partition_broadcast(P)).then_inc(S["params_in"], 16)
                pool.dma_start(gate_bias[:, l, 16:32], b_in[l, G_GATES:G_GATES + 16].partition_broadcast(P)).then_inc(S["params_in"], 16)
                pool.dma_start(fdt_bias[:, l, 0:8], flat(m_fbias[l])).then_inc(S["params_in"], 16)
                pool.dma_start(fdt_bias[:, l, 8:16], flat(g_dtbias[l])).then_inc(S["params_in"], 16)
                pool.dma_start(alog[:, l, :], flat(g_alog[l])).then_inc(S["params_in"], 16)
                pool.dma_start(lamv[:, l, :, :].rearrange("p a b -> p (a b)"), flat(a_lambda[l])).then_inc(S["params_in"], 16)

            pool.wait_ge(S["consts_in"], 16 * 3)

            for l in range(DEPTH):
                if l > 0:
                    pool.wait_ge(S["res_ready"], 2 * l * KD)
                for r in range(3):
                    for s in range(2):
                        nc.gpsimd.memset(raw[:, r, s, 0:2], 0.0)
                        nc.gpsimd.memset(raw[:, r, s, 258:260], 0.0)
                nc.gpsimd.memset(mv[:, :, :, M_V:M_V + 1], 1.0).then_inc(S["pads_set"], 1)
                nc.gpsimd.memset(gstate[:, :, :, :], 0.0).then_inc(S["states_zero"], 1)
                nc.gpsimd.memset(mstate[:, :, :, :], 0.0).then_inc(S["states_zero"], 1)
                nc.gpsimd.memset(mmax[:, :], 0.0).then_inc(S["states_zero"], 1)

                for j in range(8):
                    t0, n = seg_tokens(l, "gq" if j < 4 else "gk")
                    src = (gq if j < 4 else gk)[:, j % 4, t0:t0 + n]
                    pool.wait_ge(S["vt_psum"], 4 * l + 4)
                    if j >= 2 or l > 0:
                        pool.wait_ge(S["l2_sum"], 8 * l + j - 1)
                    nc.gpsimd.tensor_tensor(work[:, 4 + j % 2, 0:n], src, src, ALU.mult).then_inc(S["l2_sq"], 1)

                for u, (d, t) in enumerate(UNITS):
                    g = 8 * l + u
                    o = sofar([len(v) for v in out_units], l) + len([v for v in out_units[l] if v <= u])
                    pool.wait_ge(S["gd_b"], g + 1)
                    if g > 0:
                        pool.wait_ge(S["gd_o"], sofar([len(v) for v in out_units], l) + len([v for v in out_units[l] if v < u]))
                        pool.wait_ge(S["gd_v"], g)
                        pool.wait_ge(S["gd_s"], g)
                    four = lambda a: a.rearrange("p (h c) -> p h c", h=4)
                    link(nc.gpsimd.tensor_tensor(four(work[:, 3, :]), four(work[:, 1, :]),
                                                 pair_mask[d].unsqueeze(1).broadcast_to((P, 4, P)), ALU.mult))
                    nc.gpsimd.tensor_tensor(four(work[:, 3, :]), four(work[:, 3, :]),
                                            ident.unsqueeze(1).broadcast_to((P, 4, P)), ALU.add).then_inc(S["gd_u0"], 1)
                    pool.wait_ge(S["gd_neg"], g + 1)
                    keys = gk_tok[:, t, :].rearrange("p (h c) -> p h c", h=4)
                    nc.gpsimd.tensor_tensor(four(work[:, 6, :]), keys,
                                            gecol[:, 12:16].unsqueeze(2).broadcast_to((P, 4, P)), ALU.mult).then_inc(S["gd_ke"], 1)
                    nc.gpsimd.tensor_tensor(four(work[:, 7, :]), keys,
                                            gecol[:, 4:8].unsqueeze(2).broadcast_to((P, 4, P)), ALU.mult).then_inc(S["gd_ke"], 1)

                def post_squares(b):
                    for j, t in enumerate(token_tiles(l)):
                        n = post_count(l, b) + j
                        if b == 2:
                            pool.wait_ge(S["gd_oacc"], sofar([len(v) for v in out_units], l + 1))
                        elif b == 1:
                            pool.wait_ge(S["ml_h"], 2 * sofar([len(v) for v in out_units], l + 1))
                        else:
                            pool.wait_ge(S["at_oout"], attn_units(l + 1))
                        if n >= 2:
                            pool.wait_ge(S["post_sum"], n - 1)
                        nc.gpsimd.tensor_tensor(work[:, 8 + j % 2, :], oacc[:, t, :], oacc[:, t, :],
                                                ALU.mult).then_inc(S["post_sq"], 1)
                post_squares(2)
                post_squares(1)
                post_squares(0)

                t0, n = tokens(l)
                for j in range(16):
                    cc = j % 8
                    evacuated(pool, seg_of(l, "by", 8 + j))
                    nc.gpsimd.tensor_tensor(merged[:, cc, 0:n], merged[:, cc, 0:n], gated[j % 2][:, 0:n],
                                            ALU.add).then_inc(S["y_ready"], 1)
                    if cc == 7:
                        pool.wait_ge(S["y_ready"], 16 * l + j + 1)
                for f in range(FT):
                    evacuated(pool, seg_of(l, "ff1", f))
                    nc.gpsimd.tensor_tensor(hidden[:, f, 0:n], work[:, 8 + f % 2, 0:n], work[:, 8 + f % 2, 0:n],
                                            ALU.mult).then_inc(S["hid_ready"], 1)

        @block.scalar
        def _(act):
            steps = [0]

            def link(ins):
                steps[0] += 1
                ins.then_inc(S["act_step"], 1)
                act.wait_ge(S["act_step"], steps[0])

            def dense(l, kind, idx=None):
                for n in WHERE[(l, kind)] if idx is None else [WHERE[(l, kind)][k] for k in idx]:
                    _, _, i, _, bk, engine, o = SEGS[n]
                    if engine != "act" and kind != "gz":
                        continue
                    act.wait_ge(S["dense_ready"], n + 1)
                    ps = bank[bk]
                    t0, tn = seg_tokens(l, kind)
                    if kind == "ada":
                        if i == 0 and l > 0:
                            act.wait_ge(S["res_ready"], 2 * l * KD)
                        if i >= 2:
                            act.wait_ge(S["ada_cols"], 12 * l + i - 1)
                        nc.scalar.copy(ada_rows[:, i % 2, :], ps[0:2, :]).then_inc(S["taken_act"], 1)
                    elif kind in ("gq", "gk", "gv"):
                        j = {"gq": 0, "gk": 4, "gv": 8}[kind] + i
                        if j >= 3:
                            act.wait_ge(S["conv_done"], 12 * l + j - 2)
                        else:
                            act.wait_ge(S["pads_set"], l + 1)
                        s0, sn = t0 // CTX, tn // CTX
                        nc.scalar.activation(raw[:, j % 3, s0:s0 + sn, 2:258],
                                             ps[:, 0:tn].rearrange("p (s c) -> p s c", s=sn), ACT.Identity,
                                             bias=cols1[:, l, B_GQ + j:B_GQ + j + 1]).then_inc(S["taken_act"], 1)
                    elif kind == "gz":
                        if 4 * l + i >= 2:
                            evacuated(act, prev_gz(l, i, 2))
                        nc.scalar.activation(work[:, 8 + i % 2, 0:tn], ps[:, 0:tn], ACT.Sigmoid,
                                             bias=cols1[:, l, B_GZ + i:B_GZ + i + 1]).then_inc(S["gz_sig"], 1)
                    elif kind == "mo":
                        if l > 0:
                            act.wait_ge(S["res_ready"], 2 * l * KD)
                        nc.scalar.activation(mo[:, i, t0:t0 + tn], ps[:, 0:tn], ACT.Sigmoid,
                                             bias=cols1[:, l, B_MO + i:B_MO + i + 1]).then_inc(S["taken_act"], 1)
                    elif kind == "bg":
                        b, cc = i
                        k = WHERE[(l, "bg")].index(n)
                        if k >= 2:
                            evacuated(act, seg_of(l, "by", k - 2))
                        nc.scalar.activation(gate_sig[k % 2][:, 0:tn], ps[:, 0:tn], ACT.Sigmoid,
                                             bias=cols1[:, l, B_BG + 8 * b + cc:B_BG + 8 * b + cc + 1])\
                            .then_inc(S["taken_act"], 1)
                    elif kind == "wo":
                        nc.scalar.copy(ot_of[1][:, i, 0:tn], ps[:, 0:tn]).then_inc(S["taken_act"], 1)
                    elif kind == "ff1":
                        if FT * l + i >= 2:
                            act.wait_ge(S["hid_ready"], FT * l + i - 1)
                        nc.scalar.activation(work[:, 8 + i % 2, 0:tn], ps[:, 0:tn], ACT.Relu).then_inc(S["taken_act"], 1)
                    elif kind == "ff2" and engine == "act":
                        nb, _, q = i
                        nc.scalar.copy(ot_of[3][:, 4 * nb + q, 0:tn], ps[:, 0:tn]).then_inc(S["taken_act"], 1)

            def prev_gz(l, i, back):
                k = 4 * l + i - back
                return seg_of(k // 4, "gz", k % 4)

            act.wait_ge(S["ones_set"], 1)
            act.wait_ge(S["masks_ready"], 1)

            for l in range(DEPTH):
                act.wait_ge(S["cols_psum"], 2 * l + 1)
                nc.scalar.copy(cols1[:, l, 0:120], bank[2 + 2 * l][:, 0:120]).then_inc(S["cols_ready"], 1)
                act.wait_ge(S["cols_psum"], 2 * l + 2)
                nc.scalar.copy(cols2[:, l, 0:98], bank[3 + 2 * l][:, 0:98]).then_inc(S["cols_ready"], 1)
            act.wait_ge(S["cols_ready"], 4)
            nc.scalar.activation(silu_c[:, :, :].rearrange("p a k -> p (a k)"), cols1[:, 0, R_C:R_C + 16],
                                 ACT.Sigmoid).then_inc(S["csig"], 1)
            for k in range(KD):
                act.wait_ge(S["xtr_psum"], k + 1)
                nc.scalar.copy(xt[:, k, :], bank[4 + k % 4][:, :]).then_inc(S["xtr_ready"], 1)
            act.wait_ge(S["lam_sum"], 1)
            nc.scalar.activation(lam2[:, :, :], lam2[:, :, :], ACT.Exp).then_inc(S["lam_exp"], 1)

            def norm(l, which):
                t0, n = (0, TOK) if which == 0 else tokens(l)
                q = norm_count(l, which)
                for k in range(KD):
                    if which in (0, 2):
                        src = xt[:, k, t0:t0 + n]
                        if which == 0 and l == 0:
                            act.wait_ge(S["xtr_ready"], KD)
                        elif k == 0:
                            act.wait_ge(S["res_ready"], KD * (2 * l + which // 2))
                    else:
                        src = ot_of[which][:, k, 0:n]
                        if k == 0:
                            evacuated(act, seg_of(l, "wo" if which == 1 else "ff2"))
                    if KD * q + k >= 2:
                        act.wait_ge(S["sq_used"], KD * q + k - 1)
                    nc.scalar.activation(work[:, 8 + k % 2, 0:n], src, ACT.Square).then_inc(S["sq_ready"], 1)
                act.wait_ge(S["sq_used"], KD * q + KD)
                nc.scalar.activation(rstd[:, 0:n], bank[7][:, 0:n], ACT.Sqrt, bias=eps_col[:, 0:1],
                                     scale=1.0 / DM).then_inc(S["norm_root"], 1)

            def modulate(l, which):
                t0, n = (0, TOK) if which == 0 else tokens(l)
                s = which // 2
                if which == 0:
                    act.wait_ge(S["ada_ready"], l + 1)
                for k in range(KD):
                    act.wait_ge(S["scaled_ready"], scaled_count(l, which) + k + 1)
                    for a in range(t0, t0 + n, CTX):
                        cond = 1 if a < CTX else 0
                        last = nc.scalar.activation(ht[:, k, a:a + CTX], work[:, k, a - t0:a - t0 + CTX], ACT.Identity,
                                                    scale=mod_scale[:, s, k, cond:cond + 1],
                                                    bias=ada[:, 24 * s + k, cond:cond + 1])
                    last.then_inc(S["h_ready"], 1)

            eps_col = sb("eps_col", [P, 2])
            link(nc.scalar.activation(eps_col[:, 0:1], ones[:, 0:1], ACT.Copy, scale=EPS))

            for l in range(DEPTH):
                dense(l, "ada")
                norm(l, 0)
                modulate(l, 0)
                act.wait_ge(S["gates_z"], l + 1)
                link(nc.scalar.activation(egate[:, :, :], egate[:, :, :], ACT.Exp, scale=-1.0))
                nc.scalar.activation(coef[:, 8:16], alog[:, l, :], ACT.Exp)
                nc.scalar.activation(beta[:, :, :], gates[:, :, 24:32], ACT.Exp, scale=-1.0)
                nc.scalar.activation(egate[:, :, :], egate[:, :, :], ACT.Ln, bias=1.0).then_inc(S["gates_exp"], 1)

                def conv_sigmoid(j):
                    t0, n = seg_tokens(l, "gq" if j < 4 else "gk")
                    act.wait_ge(S["conv_done"], 12 * l + j + 1)
                    if j >= 2:
                        act.wait_ge(S["conv_out"], 12 * l + j - 1)
                    nc.scalar.activation(work[:, 2 + j % 2, 0:n], work[:, j % 2, 0:n], ACT.Sigmoid).then_inc(S["conv_sig"], 1)

                for j in range(12):
                    dense(l, ("gq", "gk", "gv")[j // 4], [j % 4])
                    if j >= 1:
                        conv_sigmoid(j - 1)
                conv_sigmoid(11)
                dense(l, "gz")
                for h in range(4):
                    act.wait_ge(S["vt_psum"], 4 * l + h + 1)
                    nc.scalar.copy(gv_tok[:, :, h * P:(h + 1) * P],
                                   bank[4 + h % 2][:, :].rearrange("p (t c) -> p t c", t=NT)).then_inc(S["vt_out"], 1)
                act.wait_ge(S["vt_psum"], 4 * l + 4)
                for j in range(8):
                    t0, n = seg_tokens(l, "gq" if j < 4 else "gk")
                    act.wait_ge(S["l2_sum"], 8 * l + j + 1)
                    if j >= 2 or l > 0:
                        act.wait_ge(S["l2_out"], 8 * l + j - 1)
                    nc.scalar.activation(work[:, 6 + j % 2, 0:n], bank[6 + j % 2][:, 0:n], ACT.Sqrt,
                                         bias=eps_col[:, 0:1]).then_inc(S["l2_root"], 1)
                for h in range(4):
                    act.wait_ge(S["kt_psum"], 4 * l + h + 1)
                    nc.scalar.copy(gk_tok[:, :, h * P:(h + 1) * P],
                                   bank[4 + h % 2][:, :].rearrange("p (t c) -> p t c", t=NT)).then_inc(S["kt_out"], 1)

                for u, (d, t) in enumerate(UNITS):
                    g = 8 * l + u
                    act.wait_ge(S["gd_small"], g + 1)
                    if g > 0:
                        act.wait_ge(S["gd_v"], g)
                    nc.scalar.copy(grow[:, 0, :], bank[5][0:4, 0:P])
                    nc.scalar.activation(grow[:, 1, :], bank[5][0:4, 0:P], ACT.Exp)
                    nc.scalar.mul(grow[:, 2, :], bank[5][0:4, 0:P], -1.0).then_inc(S["gd_rows"], 1)
                    act.wait_ge(S["gd_cols"], g + 1)
                    if g > 0:
                        act.wait_ge(S["gd_state"], g)
                    nc.scalar.activation(gecol[:, 0:12], gcol[:, :], ACT.Exp).then_inc(S["gd_ecol"], 1)
                    act.wait_ge(S["gd_arg"], g + 1)
                    nc.scalar.activation(work[:, 0, :], bank[2][:, :], ACT.Exp).then_inc(S["gd_decay"], 1)
                    act.wait_ge(S["gd_t0"], g + 1)
                    nc.scalar.copy(work[:, 4, :], bank[5][:, :]).then_inc(S["gd_t1"], 1)
                    for lv in range(1, LEVELS):
                        act.wait_ge(S["gd_m"], (LEVELS - 1) * g + lv)
                        nc.scalar.copy(work[:, 5, :], bank[2][:, :]).then_inc(S["gd_mout"], 1)
                    act.wait_ge(S["gd_w"], g + 1)
                    nc.scalar.copy(work[:, 4, :], bank[5][:, :]).then_inc(S["gd_wout"], 1)
                    if u in (4, 5):
                        dense(l, "mo", [2 * (u % 2), 2 * (u % 2) + 1])

                def post_roots(b):
                    for j, t in enumerate(token_tiles(l)):
                        n = post_count(l, b) + j
                        act.wait_ge(S["post_sum"], n + 1)
                        nc.scalar.activation(post_stat[:, t, :], post_stat[:, t, :], ACT.Sqrt, bias=eps_col[:, 0:1],
                                             scale=1.0 / P).then_inc(S["post_root"], 1)
                post_roots(2)

                act.wait_ge(S["mkt_psum"], l + 1)
                nc.scalar.copy(mk_tok[:, 0:2, :].rearrange("p t c -> p (t c)"), bank[2][:, :])
                nc.scalar.copy(mk_tok[:, 2:4, :].rearrange("p t c -> p (t c)"), bank[3][:, :]).then_inc(S["mkt_out"], 1)
                for u, (d, t) in enumerate(UNITS):
                    g = 8 * l + u
                    o = sofar([len(v) for v in out_units], l) + len([v for v in out_units[l] if v <= u])
                    act.wait_ge(S["ml_rows"], g + 1)
                    nc.scalar.activation(mrow[:, 7, :], mrow[:, 4, :], ACT.Exp).then_inc(S["ml_exp"], 1)
                    act.wait_ge(S["ml_cols"], g + 1)
                    nc.scalar.copy(mcol[:, 8:10], bank[5][:, 264:266])
                    nc.scalar.activation(mcol[:, 0:8], bank[5][:, 256:264], ACT.Exp).then_inc(S["ml_ecol"], 1)
                    if u in out_units[l]:
                        act.wait_ge(S["ml_arg"], o)
                        nc.scalar.activation(work[:, 0, :], bank[2][:, :], ACT.Exp).then_inc(S["ml_decay"], 1)
                post_roots(1)

                for k in range(attn_units(l + 1) - attn_units(l)):
                    g = attn_units(l) + k
                    t = token_tiles(l)[k // 4]
                    nk = CTX if t < 2 else TOK
                    act.wait_ge(S["at_max"], g + 1)
                    if g >= 1:
                        act.wait_ge(S["at_w"], g)
                    for m in range(2):
                        last = nc.scalar.activation(work[:, m, 0:nk], bank[2 + m][:, 0:nk], ACT.Exp,
                                                    bias=amax[:, g % 2, m:m + 1], accum_out=amax[:, g % 2, 2 + m:3 + m])
                        last.then_inc(S["at_e"], 1)
                    act.wait_ge(S["at_wt"], g + 1)
                    nc.scalar.copy(work[:, 3, 0:nk], bank[4][:, 0:nk]).then_inc(S["at_wtout"], 1)
                post_roots(0)

                dense(l, "bg")
                dense(l, "wo")
                norm(l, 1)
                norm(l, 2)
                modulate(l, 2)
                dense(l, "ff1")
                dense(l, "ff2")
                norm(l, 3)

        @block.vector
        def _(dve):
            steps = [0]

            def link(ins):
                steps[0] += 1
                ins.then_inc(S["dve_step"], 1)
                dve.wait_ge(S["dve_step"], steps[0])

            four = lambda a: a.rearrange("p (h c) -> p h c", h=4)
            wide = lambda a, n=P: a.unsqueeze(2).broadcast_to((P, 4, n))

            def dense(l, kind, idx=None):
                for n in WHERE[(l, kind)] if idx is None else [WHERE[(l, kind)][k] for k in idx]:
                    _, _, i, _, bk, engine, o = SEGS[n]
                    if engine != "dve":
                        continue
                    dve.wait_ge(S["dense_ready"], n + 1)
                    ps = bank[bk]
                    t0, tn = seg_tokens(l, kind)
                    if kind == "gate":
                        ins = nc.vector.tensor_tensor(gates[:, :, :], ps[:, 0:128].rearrange("p (t c) -> p t c", t=NT),
                                                      gate_bias[:, l, :].unsqueeze(1).broadcast_to((P, NT, 32)), ALU.add)
                    elif kind == "gz":
                        dve.wait_ge(S["gz_sig"], 4 * l + i + 1)
                        ins = nc.vector.scalar_tensor_tensor(out=gz[:, i, t0:t0 + tn], in0=ps[:, 0:tn],
                                                             scalar=cols1[:, l, B_GZ + i:B_GZ + i + 1],
                                                             in1=work[:, 8 + i % 2, 0:tn], op0=ALU.add, op1=ALU.mult)
                    elif kind == "mqk":
                        dst, b, f = (mq, B_MQ, 1.0) if i < 2 else (mk, B_MK, M_QK ** -0.5)
                        ins = nc.vector.tensor_scalar(dst[:, i % 2, :], ps[:, :], cols1[:, l, b + i % 2:b + i % 2 + 1], f,
                                                      ALU.add, ALU.mult)
                    elif kind == "mv":
                        if i == 0:
                            dve.wait_ge(S["vbias_in"], 32 * (l + 1))
                        ins = nc.vector.tensor_tensor(mv[:, i, :, 0:M_V], four(ps[:, :]), four(v_bias[:, 1, :]), ALU.add)
                    elif kind in ("aq", "ak"):
                        dst, b, f = (aq, B_AQ, A_HD ** -0.5) if kind == "aq" else (ak, B_AK, 1.0)
                        ins = nc.vector.tensor_scalar(dst[:, i, t0:t0 + tn], ps[:, 0:tn], cols1[:, l, b + i:b + i + 1], f,
                                                      ALU.add, ALU.mult)
                    elif kind == "av":
                        ins = nc.vector.tensor_tensor(av[:, i, :], ps[:, :], v_bias[:, 0, :], ALU.add)
                    elif kind == "by":
                        k = WHERE[(l, "by")].index(n)
                        evacuated(dve, WHERE[(l, "bg")][k])
                        if k >= 10:
                            dve.wait_ge(S["y_ready"], 16 * l + k - 9)
                        dst = merged[:, i[1], 0:tn] if k < 8 else gated[k % 2][:, 0:tn]
                        ins = nc.vector.tensor_tensor(dst, ps[:, 0:tn], gate_sig[k % 2][:, 0:tn], ALU.mult)
                    ins.then_inc(S["taken_dve"], 1)

            dve.wait_ge(S["consts_in"], 16 * 3)
            dve.wait_ge(S["params_in"], 16 * 12)
            nc.vector.tensor_copy(cm[:, :, :, :].rearrange("p a b c -> p (a b c)"), level_masks)
            nc.vector.tensor_copy(cb[:, :, :].rearrange("p a c -> p (a c)"), work[:, 8, 0:3 * P]).then_inc(S["masks_ready"], 1)
            dve.wait_ge(S["csig"], 1)
            nc.vector.tensor_tensor(silu_c[:, :, :].rearrange("p a k -> p (a k)"),
                                    silu_c[:, :, :].rearrange("p a k -> p (a k)"), cols1[:, 0, R_C:R_C + 16],
                                    ALU.mult).then_inc(S["silu_ready"], 1)
            lam_prod = work[:, 9, 0:DEPTH * 2 * A_HD].rearrange("p (l m c) -> p l m c", l=DEPTH, m=2)
            for l in range(DEPTH):
                for m in range(2):
                    link(nc.vector.tensor_tensor(lam_prod[:, l, m, :], lamv[:, l, 2 * m, :], lamv[:, l, 2 * m + 1, :], ALU.mult))
            nc.vector.tensor_reduce(lam2[:, :, :], lam_prod, op=ALU.add, axis=AX_X).then_inc(S["lam_sum"], 1)
            dve.wait_ge(S["lam_exp"], 1)
            for l in range(DEPTH):
                lam_init = 0.8 - 0.6 * math.exp(-0.3 * l)
                link(nc.vector.tensor_tensor(nlam[:, l:l + 1], lam2[:, l, 1:2], lam2[:, l, 0:1], ALU.subtract))
                link(nc.vector.tensor_scalar(nlam[:, l:l + 1], nlam[:, l:l + 1], -lam_init, None, ALU.add))
            nc.vector.memset(coef[:, 0:8], -1.0)

            def root_to_rstd(l, which):
                t0, n = (0, TOK) if which == 0 else tokens(l)
                dve.wait_ge(S["norm_root"], norm_count(l, which) + 1)
                link(nc.vector.reciprocal(rstd[:, 0:n], rstd[:, 0:n]))

            def normed(l, which):
                t0, n = (0, TOK) if which == 0 else tokens(l)
                root_to_rstd(l, which)
                for k in range(KD):
                    nc.vector.tensor_tensor(work[:, k, 0:n], xt[:, k, t0:t0 + n], rstd[:, 0:n], ALU.mult)\
                        .then_inc(S["scaled_ready"], 1)

            def residual(l, which):
                t0, n = tokens(l)
                root_to_rstd(l, which)
                ot = ot_of[which]
                for k in range(KD):
                    for a in range(0, n, CTX):
                        cond = 1 if a + t0 < CTX else 0
                        link(nc.vector.scalar_tensor_tensor(out=ot[:, k, a:a + CTX], in0=ot[:, k, a:a + CTX],
                                                            scalar=out_gate[:, which // 2, k, cond:cond + 1],
                                                            in1=rstd[:, a:a + CTX], op0=ALU.mult, op1=ALU.mult))
                    nc.vector.tensor_tensor(xt[:, k, t0:t0 + n], xt[:, k, t0:t0 + n], ot[:, k, 0:n], ALU.add)\
                        .then_inc(S["res_ready"], 1)
                dve.wait_ge(S["res_ready"], KD * (2 * l + which // 2 + 1))

            for l in range(DEPTH):
                dve.wait_ge(S["ada_cols"], 12 * (l + 1))
                link(nc.vector.tensor_tensor(ada[:, :, :], bank[6][:, 0:96].rearrange("p (j a) -> p j a", a=2),
                                             cols1[:, l, B_ADA:B_ADA + 48].unsqueeze(2).broadcast_to((P, 48, 2)), ALU.add))
                for s in range(2):
                    gain = lambda r: cols2[:, l, R_GAIN + 8 * r:R_GAIN + 8 * r + 8].unsqueeze(2).broadcast_to((P, KD, 2))
                    link(nc.vector.tensor_scalar(mod_scale[:, s, :, :], ada[:, 24 * s + 8:24 * s + 16, :], 1.0, None, ALU.add))
                    link(nc.vector.tensor_tensor(mod_scale[:, s, :, :], mod_scale[:, s, :, :], gain(2 * s), ALU.mult))
                    ins = nc.vector.tensor_tensor(out_gate[:, s, :, :], ada[:, 24 * s + 16:24 * s + 24, :], gain(2 * s + 1), ALU.mult)
                ins.then_inc(S["ada_ready"], 1)
                normed(l, 0)

                dense(l, "gate")
                evacuated(dve, seg_of(l, "gate"))
                two = lambda a: a.unsqueeze(1).broadcast_to((P, NT, a.shape[1]))
                for d in range(2):
                    link(nc.vector.scalar_tensor_tensor(out=zgate[:, :, 4 * d:4 * d + 4], in0=gates[:, :, 8 * d + 4:8 * d + 8],
                                                        scalar=-1.0, in1=two(fdt_bias[:, l, 4 * d:4 * d + 4]),
                                                        op0=ALU.mult, op1=ALU.subtract))
                link(nc.vector.tensor_tensor(zgate[:, :, 8:16], gates[:, :, 16:24], two(fdt_bias[:, l, 8:16]), ALU.add))
                nc.vector.scalar_tensor_tensor(out=egate[:, :, :], in0=zgate[:, :, :], scalar=-1.0, in1=zgate[:, :, :],
                                               op0=ALU.mult, op1=ALU.max).then_inc(S["gates_z"], 1)
                dve.wait_ge(S["gates_exp"], l + 1)
                link(nc.vector.tensor_scalar(coef[:, 8:16], coef[:, 8:16], -1.0, None, ALU.mult))
                link(nc.vector.scalar_tensor_tensor(out=lgate[:, :, :], in0=zgate[:, :, :], scalar=0.0, in1=egate[:, :, :],
                                                    op0=ALU.max, op1=ALU.add))
                link(nc.vector.tensor_tensor(lgate[:, :, :], lgate[:, :, :], two(coef[:, :]), ALU.mult))
                link(nc.vector.tensor_scalar(beta[:, :, :], beta[:, :, :], 1.0, None, ALU.add))
                link(nc.vector.reciprocal(beta[:, :, :], beta[:, :, :]))
                nc.vector.tensor_scalar(nbeta[:, :, :], beta[:, :, :], -1.0, None, ALU.mult).then_inc(S["gates_ready"], 1)
                dve.wait_ge(S["gates_ready"], l + 1)

                def conv(j):
                    t0, n = seg_tokens(l, "gq" if j < 4 else "gk")
                    s0, sn = t0 // CTX, n // CTX
                    seg = seg_of(l, ("gq", "gk", "gv")[j // 4], j % 4)
                    evacuated(dve, seg)
                    if j == 0:
                        dve.wait_ge(S["h_ready"], 2 * KD * l + KD)
                    if j >= 2:
                        dve.wait_ge(S["conv_out"], 12 * l + j - 1)
                    acc = work[:, j % 2, 0:n].rearrange("p (s c) -> p s c", s=sn)
                    tap = lambda k: cols2[:, l, R_CONV + 12 * k + j:R_CONV + 12 * k + j + 1]
                    src = lambda k: raw[:, j % 3, s0:s0 + sn, k:k + CTX]
                    link(nc.vector.tensor_scalar(acc, src(0), tap(0), None, ALU.mult))
                    for k in range(1, CONV_K):
                        ins = nc.vector.scalar_tensor_tensor(out=acc, in0=src(k), scalar=tap(k), in1=acc,
                                                             op0=ALU.mult, op1=ALU.add)
                        if k < CONV_K - 1:
                            link(ins)
                    ins.then_inc(S["conv_done"], 1)

                def conv_silu(j):
                    t0, n = seg_tokens(l, "gq" if j < 4 else "gk")
                    dve.wait_ge(S["conv_sig"], 12 * l + j + 1)
                    dst = (gq[:, j % 4, t0:t0 + n], gk[:, j % 4, t0:t0 + n], work[:, 4 + j % 4, 0:n])[j // 4]
                    nc.vector.tensor_tensor(dst, work[:, j % 2, 0:n], work[:, 2 + j % 2, 0:n], ALU.mult)\
                        .then_inc(S["conv_out"], 1)

                for j in range(12):
                    conv(j)
                    if j >= 1:
                        conv_silu(j - 1)
                conv_silu(11)
                dense(l, "gz")
                dve.wait_ge(S["vt_psum"], 4 * l + 4)
                for j in range(8):
                    t0, n = seg_tokens(l, "gq" if j < 4 else "gk")
                    dst = (gq if j < 4 else gk)[:, j % 4, t0:t0 + n]
                    r = work[:, 6 + j % 2, 0:n]
                    dve.wait_ge(S["l2_root"], 8 * l + j + 1)
                    link(nc.vector.reciprocal(r, r))
                    nc.vector.scalar_tensor_tensor(out=dst, in0=dst, scalar=G_HD ** -0.5 if j < 4 else 1.0, in1=r,
                                                   op0=ALU.mult, op1=ALU.mult).then_inc(S["l2_out"], 1)

                for u, (d, t) in enumerate(UNITS):
                    g = 8 * l + u
                    gives = u in out_units[l]
                    o = sofar([len(v) for v in out_units], l) + len([v for v in out_units[l] if v <= u])
                    dve.wait_ge(S["gd_rows"], g + 1)
                    if g > 0:
                        dve.wait_ge(S["gd_ecol"], g)
                    link(nc.vector.tensor_copy(gcol[:, 0:4], bank[5][:, 128:132]))
                    link(nc.vector.tensor_tensor(gcol[:, 4:8], bank[5][:, 132:136], gcol[:, 0:4], ALU.subtract))
                    nc.vector.tensor_copy(gcol[:, 8:12], bank[5][:, 132:136]).then_inc(S["gd_cols"], 1)
                    dve.wait_ge(S["gd_ecol"], g + 1)
                    if g > 0:
                        dve.wait_ge(S["gd_ke"], 2 * g)
                    nc.vector.tensor_scalar(gecol[:, 12:16], gecol[:, 0:4], -1.0, None, ALU.mult).then_inc(S["gd_neg"], 1)
                    dve.wait_ge(S["gd_decay"], g + 1)
                    dve.wait_ge(S["gd_qk"], g + 1)
                    for h in range(HEADS):
                        hs = slice(h * P, (h + 1) * P)
                        ins = nc.vector.scalar_tensor_tensor(out=work[:, 1, hs], in0=bank[3][:, hs],
                                                             scalar=nbeta[:, t, 4 * d + h:4 * d + h + 1],
                                                             in1=work[:, 0, hs], op0=ALU.mult, op1=ALU.mult)
                    ins.then_inc(S["gd_b"], 1)
                    if gives:
                        nc.vector.tensor_tensor(work[:, 2, :], bank[4][:, :], work[:, 0, :], ALU.mult).then_inc(S["gd_qkd"], 1)
                        dve.wait_ge(S["gd_qb"], o)
                        nc.vector.tensor_tensor(four(work[:, 8, :]), gq[:, :, t * P:(t + 1) * P], four(bank[7][:, :]),
                                                ALU.mult).then_inc(S["gd_qg"], 1)
                    dve.wait_ge(S["gd_t1"], g + 1)
                    for lv in range(1, LEVELS):
                        k = (LEVELS - 1) * g + lv
                        dve.wait_ge(S["gd_up"], 2 * k - 1)
                        mask = lambda side: cm[:, side, lv - 1, :].unsqueeze(1).broadcast_to((P, 4, P))
                        dve.wait_ge(S["gd_up"], 2 * k)
                        nc.vector.copy_predicated(four(work[:, 3, :]), mask(d), four(bank[3][:, :])).then_inc(S["gd_uout"], 1)
                        if lv < LEVELS - 1:
                            nc.vector.copy_predicated(four(work[:, 4, :]), mask(1 - d), four(bank[4][:, :])).then_inc(S["gd_tout"], 1)
                    if u < 6:
                        dense(l, "mqk" if u < 2 else "mv" if u < 4 else "mo", [2 * (u % 2), 2 * (u % 2) + 1])
                    dve.wait_ge(S["gd_v"], g + 1)
                    nc.vector.tensor_tensor(four(work[:, 5, :]), four(bank[6][:, :]), wide(beta[:, t, 4 * d:4 * d + 4]),
                                            ALU.mult).then_inc(S["gd_vn"], 1)
                    if gives:
                        dve.wait_ge(S["gd_o"], o)
                        if u in FIRST_VISIT:
                            ins = nc.vector.tensor_copy(oacc[:, t, :], bank[7][:, :])
                        else:
                            ins = nc.vector.tensor_tensor(oacc[:, t, :], bank[7][:, :], oacc[:, t, :], ALU.add)
                        ins.then_inc(S["gd_oacc"], 1)
                    dve.wait_ge(S["gd_s"], g + 1)
                    for h in range(HEADS):
                        ins = nc.vector.scalar_tensor_tensor(out=gstate[:, d, h, :], in0=gstate[:, d, h, :],
                                                             scalar=gecol[:, 8 + h:9 + h], in1=bank[6][:, h * P:(h + 1) * P],
                                                             op0=ALU.mult, op1=ALU.add)
                    ins.then_inc(S["gd_state"], 1)
                    if gives:
                        dve.wait_ge(S["gd_oacc"], o)

                def post(b):
                    tiles = token_tiles(l)
                    for j, t in enumerate(tiles):
                        dve.wait_ge(S["post_sq"], post_count(l, b) + j + 1)
                        nc.vector.tensor_reduce(post_stat[:, t, :], four(work[:, 8 + j % 2, :]), op=ALU.add, axis=AX_X)\
                            .then_inc(S["post_sum"], 1)
                    for j, t in enumerate(tiles):
                        n = post_count(l, b) + j
                        dve.wait_ge(S["post_root"], n + 1)
                        link(nc.vector.reciprocal(post_stat[:, t, :], post_stat[:, t, :]))
                        nc.vector.tensor_tensor(four(oacc[:, t, :]), four(oacc[:, t, :]), wide(post_stat[:, t, :]), ALU.mult)\
                            .then_inc(S["post_norm"], 1)
                    for j, t in enumerate(tiles):
                        n = post_count(l, b) + j
                        dve.wait_ge(S["post_tr"], n + 1)
                        ps = bank[6 + j % 2]
                        ts = slice(t * P, (t + 1) * P)
                        if b == 2:
                            ins = nc.vector.scalar_tensor_tensor(out=gz[:, :, ts], in0=four(ps[:, :]),
                                                                 scalar=cols2[:, l, R_GN:R_GN + 1], in1=gz[:, :, ts],
                                                                 op0=ALU.mult, op1=ALU.mult)
                        elif b == 1:
                            for h in range(HEADS):
                                ins = nc.vector.scalar_tensor_tensor(out=mo[:, h, ts], in0=ps[:, h * P:(h + 1) * P],
                                                                     scalar=cols2[:, l, R_MN + h:R_MN + h + 1],
                                                                     in1=mo[:, h, ts], op0=ALU.mult, op1=ALU.mult)
                        else:
                            lam_init = 0.8 - 0.6 * math.exp(-0.3 * l)
                            ins = nc.vector.tensor_scalar(aq[:, :, ts], four(ps[:, :]), cols2[:, l, R_AN:R_AN + 1],
                                                          1.0 - lam_init, ALU.mult, ALU.mult)
                        ins.then_inc(S["post_out"], 1)
                post(2)

                for u, (d, t) in enumerate(UNITS):
                    g = 8 * l + u
                    gives = u in out_units[l]
                    o = sofar([len(v) for v in out_units], l) + len([v for v in out_units[l] if v <= u])
                    end = P - 1 if d == 0 else 0
                    R = lambda r: mrow[:, r, :]
                    fwd = lambda a: a if d == 0 else a[:, ::-1]
                    dve.wait_ge(S["ml_small"], g + 1)
                    if g > 0:
                        dve.wait_ge(S["ml_c"], g)
                    if l > 0 and u == 0:
                        dve.wait_ge(S["states_zero"], 3 * l + 3)
                    link(nc.vector.tensor_copy(R(0), bank[5][0:4, 128:256]))
                    link(nc.vector.tensor_tensor(R(1), bank[5][0:4, 0:128], R(0), ALU.subtract))
                    link(nc.vector.tensor_tensor_scan(fwd(R(2)), fwd(R(1)), fwd(R(1)), mmax[:, d:d + 1], ALU.max, ALU.max))
                    nc.vector.tensor_scalar(R(3), R(2), -1.0, None, ALU.mult)
                    nc.vector.tensor_scalar(R(4), R(2), -1.0, mmax[:, d:d + 1], ALU.mult, ALU.add)
                    link(nc.vector.scalar_tensor_tensor(out=R(5), in0=R(2), scalar=-1.0, in1=R(0), op0=ALU.mult, op1=ALU.subtract))
                    link(nc.vector.tensor_tensor(mmax[:, d:d + 1], R(0)[:, end:end + 1], R(2)[:, end:end + 1], ALU.add))
                    nc.vector.tensor_scalar(R(6), R(1), R(2)[:, end:end + 1], None, ALU.subtract).then_inc(S["ml_rows"], 1)
                    dve.wait_ge(S["ml_ecol"], g + 1)
                    if u == 0:
                        dve.wait_ge(S["mkt_out"], l + 1)
                    keys = mk_tok[:, t, :].rearrange("p (h c) -> p h c", h=4)
                    kw = work[:, 3, 0:256].rearrange("p (h c) -> p h c", h=4)
                    nc.vector.tensor_tensor(kw, keys, wide(mcol[:, 4:8], M_QK), ALU.mult).then_inc(S["ml_kw"], 1)
                    if gives:
                        dve.wait_ge(S["ml_qb"], o)
                        nc.vector.tensor_tensor(work[:, 2, 0:256].rearrange("p (i c) -> p i c", i=2),
                                                mq[:, :, t * P:(t + 1) * P],
                                                bank[7][:, 0:256].rearrange("p (i c) -> p i c", i=2), ALU.mult)\
                            .then_inc(S["ml_qg"], 1)
                        dve.wait_ge(S["ml_decay"], o)
                        dve.wait_ge(S["ml_qk"], o)
                        nc.vector.tensor_tensor(work[:, 1, 0:256], bank[3][:, 0:256], work[:, 0, 0:256], ALU.mult)
                        nc.vector.tensor_tensor(work[:, 1, 256:512], bank[6][:, 0:256], work[:, 0, 256:512], ALU.mult)\
                            .then_inc(S["ml_p"], 1)
                        dve.wait_ge(S["ml_num"], o)
                        num = [bank[4 + 2 * i][:, 0:258].rearrange("p (h c) -> p h c", h=2) for i in range(2)]
                        nc.vector.tensor_copy(mden[:, 0:2], num[0][:, :, M_V])
                        link(nc.vector.tensor_copy(mden[:, 2:4], num[1][:, :, M_V]))
                        link(nc.vector.scalar_tensor_tensor(out=mden[:, 4:8], in0=mden[:, 0:4], scalar=-1.0, in1=mden[:, 0:4],
                                                            op0=ALU.mult, op1=ALU.max))
                        link(nc.vector.tensor_tensor(mden[:, 4:8], mden[:, 4:8], mcol[:, 0:4], ALU.max))
                        link(nc.vector.reciprocal(mden[:, 4:8], mden[:, 4:8]))
                        for i in range(2):
                            r = mden[:, 4 + 2 * i:6 + 2 * i].unsqueeze(2).broadcast_to((P, 2, P))
                            acc = oacc[:, t, :].rearrange("p (k r c) -> p r k c", k=2, r=2)[:, i]
                            if u in FIRST_VISIT:
                                ins = nc.vector.tensor_tensor(acc, num[i][:, :, 0:M_V], r, ALU.mult)
                            else:
                                tmp = work[:, 4, 256 * i:256 * i + 256].rearrange("p (h c) -> p h c", h=2)
                                link(nc.vector.tensor_tensor(tmp, num[i][:, :, 0:M_V], r, ALU.mult))
                                ins = nc.vector.tensor_tensor(acc, acc, tmp, ALU.add)
                            ins.then_inc(S["ml_h"], 1)
                    dve.wait_ge(S["ml_c"], g + 1)
                    for i in range(2):
                        ins = nc.vector.scalar_tensor_tensor(out=mstate[:, d, i, :], in0=mstate[:, d, i, :],
                                                             scalar=mcol[:, 8 + i:9 + i],
                                                             in1=mlstm_c(i),
                                                             op0=ALU.mult, op1=ALU.add)
                    ins.then_inc(S["ml_state"], 1)
                    if gives:
                        dve.wait_ge(S["ml_h"], 2 * o)
                    dve.wait_ge(S["ml_state"], g + 1)
                    if u < 6:
                        dense(l, ("aq", "ak", "av")[u // 2], [2 * (u % 2), 2 * (u % 2) + 1])
                post(1)

                for j in range(8):
                    dst = (aq if j < 4 else ak)[:, j % 4, CTX:TOK]
                    n = 8 * l + j
                    dve.wait_ge(S["rope_psum"], n + 1)
                    link(nc.vector.tensor_tensor(dst, dst, cos_t, ALU.mult))
                    link(nc.vector.tensor_tensor(work[:, 4, 0:256], bank[4 + j % 2][:, 0:256], sin_t, ALU.mult))
                    nc.vector.tensor_tensor(dst, dst, work[:, 4, 0:256], ALU.add).then_inc(S["rope_out"], 1)

                for k in range(attn_units(l + 1) - attn_units(l)):
                    g = attn_units(l) + k
                    t = token_tiles(l)[k // 4]
                    h = k % 4
                    nk = CTX if t < 2 else TOK
                    st = amax[:, g % 2, :]
                    dve.wait_ge(S["at_s"], g + 1)
                    for m in range(2):
                        ins = nc.vector.tensor_reduce(st[:, m:m + 1], bank[2 + m][:, 0:nk], op=ALU.max, axis=AX_X, negate=True)
                    ins.then_inc(S["at_max"], 1)
                    dve.wait_ge(S["at_e"], 2 * g + 2)
                    link(nc.vector.reciprocal(st[:, 4:6], st[:, 2:4]))
                    link(nc.vector.tensor_tensor(st[:, 6:7], st[:, 5:6], nlam[:, l:l + 1], ALU.mult))
                    link(nc.vector.tensor_scalar(work[:, 1, 0:nk], work[:, 1, 0:nk], st[:, 6:7], None, ALU.mult))
                    if g >= 1:
                        dve.wait_ge(S["at_wt"], g)
                    nc.vector.scalar_tensor_tensor(out=work[:, 2, 0:nk], in0=work[:, 0, 0:nk], scalar=st[:, 4:5],
                                                   in1=work[:, 1, 0:nk], op0=ALU.mult, op1=ALU.add).then_inc(S["at_w"], 1)
                    dve.wait_ge(S["at_o"], g + 1)
                    nc.vector.tensor_copy(oacc[:, t, h * P:(h + 1) * P], bank[5][:, 0:P]).then_inc(S["at_oout"], 1)
                dve.wait_ge(S["at_oout"], attn_units(l + 1))
                post(0)

                dense(l, "by")
                residual(l, 1)
                normed(l, 2)
                residual(l, 3)

            for t in range(2):
                for hf in range(2):
                    n = 2 * t + hf
                    dve.wait_ge(S["final_psum"], n + 1)
                    nc.vector.tensor_copy(work[:, n, :], bank[2 + n][:, :]).then_inc(S["final_out"], 1)

        @block.tensor
        def _(pe):
            mm = nc.tensor.matmul

            def chunk_arrived(n):
                pe.wait_ge(S[f"chunk_in{n % RING}"], 16 * (n // RING + 1))

            def bank_free(n):
                for m in range(n - 1, -1, -1):
                    if SEGS[m][4] == SEGS[n][4]:
                        if SEGS[m][5] is not None:
                            evacuated(pe, m)
                        return

            def dense(l, kind, idx=None):
                for n in WHERE[(l, kind)] if idx is None else [WHERE[(l, kind)][k] for k in idx]:
                    _, _, i, ch, bk, engine, _ = SEGS[n]
                    ps = bank[bk]
                    t0, tn = seg_tokens(l, kind)
                    bank_free(n)
                    if ch is not None:
                        chunk_arrived(ch)
                        k_of = 4 if kind == "by" else 8
                        w = ring[:, ch % RING, :].rearrange("p (k n) -> p k n", k=k_of)
                    if kind == "ada":
                        for k in range(KD):
                            last = mm(ps[0:2, :], silu_c[:, :, k], w[:, k, :], start=k == 0, stop=k == KD - 1)
                    elif kind == "gate":
                        pe.wait_ge(S["gatew_in"], 32 * (l + 1))
                        for t in range(NT):
                            for k in range(KD):
                                last = mm(ps[:, 32 * t:32 * t + 32], ht[:, k, t * P:(t + 1) * P], w_gates[:, k, :],
                                          start=k == 0, stop=k == KD - 1)
                    elif kind in ("mv", "av"):
                        for k in range(KD):
                            last = mm(ps[:, :], ht[:, k, i * P:(i + 1) * P], w[:, k, :], start=k == 0, stop=k == KD - 1)
                    elif kind in ("gq", "gk", "gv", "gz", "mqk", "mo", "aq", "ak", "bg", "ff1"):
                        q = (i[1] if kind == "bg" else i) % 4
                        for k in range(KD):
                            last = mm(ps[:, 0:tn], w[:, k, q * P:(q + 1) * P], ht[:, k, t0:t0 + tn],
                                      start=k == 0, stop=k == KD - 1)
                    elif kind == "by":
                        b, cc = i
                        y = {2: gz, 1: mo, 0: aq}[b]
                        pe.wait_ge(S["post_out"], post_count(l, b) + len(token_tiles(l)))
                        for k in range(4):
                            last = mm(ps[:, 0:tn], w[:, k, cc * P:(cc + 1) * P], y[:, k, t0:t0 + tn],
                                      start=k == 0, stop=k == 3)
                    elif kind == "wo":
                        q = i % 4
                        pe.wait_ge(S["y_ready"], 16 * (l + 1))
                        for k in range(KD):
                            last = mm(ps[:, 0:tn], w[:, k, q * P:(q + 1) * P], merged[:, k, 0:tn],
                                      start=k == 0, stop=k == KD - 1)
                    elif kind == "ff2":
                        nb, kc, q = i
                        pe.wait_ge(S["hid_ready"], FT * l + 8 * kc + 8)
                        for k in range(KD):
                            last = mm(ps[:, 0:tn], w[:, k, q * P:(q + 1) * P], hidden[:, 8 * kc + k, 0:tn],
                                      start=kc == 0 and k == 0, stop=kc == 3 and k == KD - 1)
                    last.then_inc(S["dense_ready"], 1)

            pe.wait_ge(S["consts_in"], 16 * 3)
            pe.wait_ge(S["rows_in"], 16 * 26)
            for l in range(DEPTH):
                nc.tensor.transpose(bank[2 + 2 * l][:, 0:120], rows1[0:120, l, :], ident[0:120, 0:120]).then_inc(S["cols_psum"], 1)
                nc.tensor.transpose(bank[3 + 2 * l][:, 0:98], rows2[0:98, l, :], ident[0:98, 0:98]).then_inc(S["cols_psum"], 1)
            pe.wait_ge(S["x_in"], 32)
            pe.wait_ge(S["cols_ready"], 4)
            x_tok = ht[:, :, :].rearrange("p (t a) c -> p t (a c)", t=NT)
            for k in range(KD):
                if k >= 4:
                    pe.wait_ge(S["xtr_ready"], k - 3)
                for t in range(NT):
                    last = nc.tensor.transpose(bank[4 + k % 4][:, t * P:(t + 1) * P], x_tok[:, t, k * P:(k + 1) * P], ident)
                last.then_inc(S["xtr_psum"], 1)
            pe.wait_ge(S["xtr_ready"], KD)
            pe.wait_ge(S["masks_ready"], 1)
            pe.wait_ge(S["silu_ready"], 1)
            pe.wait_ge(S["ones_set"], 1)

            def norm(l, which):
                t0, n = (0, TOK) if which == 0 else tokens(l)
                q = norm_count(l, which)
                for k in range(KD):
                    pe.wait_ge(S["sq_ready"], KD * q + k + 1)
                    mm(bank[7][:, 0:n], ones[:, :], work[:, 8 + k % 2, 0:n], start=k == 0, stop=k == KD - 1)\
                        .then_inc(S["sq_used"], 1)

            for l in range(DEPTH):
                def ada_transposes(n):
                    evacuated(pe, seg_of(l, "ada", n))
                    for q in range(4):
                        j = 4 * n + q
                        last = mm(bank[6][:, 2 * j:2 * j + 2], ada_rows[:, n % 2, q * P:(q + 1) * P], ident[0:2, 0:2],
                                  start=True, stop=True)
                    last.then_inc(S["ada_cols"], 1)

                for n in range(12):
                    dense(l, "ada", [n])
                    if n > 0:
                        ada_transposes(n - 1)
                ada_transposes(11)
                norm(l, 0)
                pe.wait_ge(S["h_ready"], 2 * KD * l + KD)
                dense(l, "gate")
                for j in range(12):
                    dense(l, ("gq", "gk", "gv")[j // 4], [j % 4])
                dense(l, "gz")
                for h in range(4):
                    pe.wait_ge(S["conv_out"], 12 * l + 9 + h)
                    if h >= 2:
                        pe.wait_ge(S["vt_out"], 4 * l + h - 1)
                    for t in range(NT):
                        last = nc.tensor.transpose(bank[4 + h % 2][:, t * P:(t + 1) * P], work[:, 4 + h, t * P:(t + 1) * P], ident)
                    last.then_inc(S["vt_psum"], 1)
                for j in range(8):
                    n = seg_tokens(l, "gq" if j < 4 else "gk")[1]
                    pe.wait_ge(S["l2_sq"], 8 * l + j + 1)
                    if j >= 2:
                        pe.wait_ge(S["l2_root"], 8 * l + j - 1)
                    mm(bank[6 + j % 2][:, 0:n], ones[:, :], work[:, 4 + j % 2, 0:n], start=True, stop=True).then_inc(S["l2_sum"], 1)
                for h in range(4):
                    pe.wait_ge(S["l2_out"], 8 * l + 5 + h)
                    pe.wait_ge(S["vt_out"], 4 * l + 4)
                    if h >= 2:
                        pe.wait_ge(S["kt_out"], 4 * l + h - 1)
                    for t in range(NT):
                        last = nc.tensor.transpose(bank[4 + h % 2][:, t * P:(t + 1) * P], gk[:, h, t * P:(t + 1) * P], ident)
                    last.then_inc(S["kt_psum"], 1)
                pe.wait_ge(S["kt_out"], 4 * l + 4)
                pe.wait_ge(S["gates_ready"], l + 1)
                pe.wait_ge(S["states_zero"], 3 * l + 3)

                H = lambda h: slice(h * P, (h + 1) * P)
                for u, (d, t) in enumerate(UNITS):
                    g = 8 * l + u
                    gives = u in out_units[l]
                    o = sofar([len(v) for v in out_units], l) + len([v for v in out_units[l] if v <= u])
                    ts = slice(t * P, (t + 1) * P)
                    log_g = lgate[:, t, 8 + 4 * d:12 + 4 * d]
                    mm(bank[5][0:4, 0:P], log_g, tri[d], start=True, stop=True)
                    mm(bank[5][:, 128:132], tri[d], log_g, start=True, stop=True)
                    mm(bank[5][:, 132:136], ones[:, :], log_g, start=True, stop=True).then_inc(S["gd_small"], 1)
                    for h in range(HEADS):
                        last = mm(bank[3][:, H(h)], gk[:, h, ts], gk[:, h, ts], start=True, stop=True)
                    if gives:
                        for h in range(HEADS):
                            last = mm(bank[4][:, H(h)], gk[:, h, ts], gq[:, h, ts], start=True, stop=True)
                    last.then_inc(S["gd_qk"], 1)
                    pe.wait_ge(S["gd_rows"], g + 1)
                    mm(bank[2][:, :], ident_b, mask_b[d], start=True, stop=False)
                    for h in range(HEADS):
                        mm(bank[2][:, H(h)], sel[h], grow[:, 0, :], start=False, stop=False)
                        last = mm(bank[2][:, H(h)], grow[:, 2, :], sel[h], start=False, stop=h == HEADS - 1)
                    last.then_inc(S["gd_arg"], 1)
                    if gives:
                        for h in range(HEADS):
                            last = mm(bank[7][:, H(h)], sel[h], grow[:, 1, :], start=True, stop=True)
                        last.then_inc(S["gd_qb"], 1)
                    pe.wait_ge(S["gd_u0"], g + 1)
                    pe.wait_ge(S["gd_cols"], g + 1)
                    for h in range(HEADS):
                        last = nc.tensor.transpose(bank[5][:, H(h)], work[:, 3, H(h)], ident)
                    last.then_inc(S["gd_t0"], 1)
                    pe.wait_ge(S["gd_t1"], g + 1)
                    pe.wait_ge(S["gd_decay"], g + 1)
                    if gives:
                        pe.wait_ge(S["gd_qkd"], o)
                    for lv in range(1, LEVELS):
                        k = (LEVELS - 1) * g + lv
                        if lv > 1:
                            pe.wait_ge(S["gd_tout"], (LEVELS - 2) * g + lv - 1)
                        for h in range(HEADS):
                            last = mm(bank[2][:, H(h)], work[:, 1, H(h)], work[:, 4, H(h)], start=True, stop=True)
                        last.then_inc(S["gd_m"], 1)
                        pe.wait_ge(S["gd_mout"], k)
                        if lv > 1:
                            pe.wait_ge(S["gd_uout"], k - 1)
                        for h in range(HEADS):
                            last = mm(bank[3][:, H(h)], work[:, 5, H(h)], work[:, 3, H(h)], start=True, stop=True)
                        last.then_inc(S["gd_up"], 1)
                        for h in range(HEADS):
                            last = mm(bank[4][:, H(h)], work[:, 3, H(h)], work[:, 5, H(h)], start=True, stop=True)
                        last.then_inc(S["gd_up"], 1)
                    pe.wait_ge(S["gd_uout"], (LEVELS - 1) * (g + 1))
                    pe.wait_ge(S["gd_ke"], 2 * g + 2)
                    for h in range(HEADS):
                        last = mm(bank[5][:, H(h)], work[:, 6, H(h)], work[:, 3, H(h)], start=True, stop=True)
                    last.then_inc(S["gd_w"], 1)
                    if u < 6:
                        if l > 0 and u == 0:
                            pe.wait_ge(S["res_ready"], 2 * l * KD)
                        dense(l, "mqk" if u < 2 else "mv" if u < 4 else "mo", [2 * (u % 2), 2 * (u % 2) + 1])
                    pe.wait_ge(S["gd_wout"], g + 1)
                    if u >= 2:
                        pe.wait_ge(S["gd_state"], g - 1)
                    if g >= 1:
                        pe.wait_ge(S["gd_state"], g)
                    for h in range(HEADS):
                        mm(bank[6][:, H(h)], work[:, 3, H(h)], gv_tok[:, t, H(h)], start=True, stop=False)
                        last = mm(bank[6][:, H(h)], work[:, 4, H(h)], gstate[:, d, h, :], start=False, stop=True)
                    last.then_inc(S["gd_v"], 1)
                    pe.wait_ge(S["gd_vn"], g + 1)
                    if gives:
                        pe.wait_ge(S["gd_qg"], o)
                        for h in range(HEADS):
                            mm(bank[7][:, H(h)], work[:, 2, H(h)], work[:, 5, H(h)], start=True, stop=False)
                            last = mm(bank[7][:, H(h)], work[:, 8, H(h)], gstate[:, d, h, :], start=False, stop=True)
                        last.then_inc(S["gd_o"], 1)
                    for h in range(HEADS):
                        last = mm(bank[6][:, H(h)], work[:, 7, H(h)], work[:, 5, H(h)], start=True, stop=True)
                    last.then_inc(S["gd_s"], 1)
                    if gives:
                        pe.wait_ge(S["gd_oacc"], o)

                def post(b):
                    for j, t in enumerate(token_tiles(l)):
                        n = post_count(l, b) + j
                        pe.wait_ge(S["post_norm"], n + 1)
                        if j >= 2:
                            pe.wait_ge(S["post_out"], n - 1)
                        for h in range(HEADS):
                            last = nc.tensor.transpose(bank[6 + j % 2][:, H(h)], oacc[:, t, H(h)], ident)
                        last.then_inc(S["post_tr"], 1)
                    pe.wait_ge(S["post_out"], post_count(l, b) + len(token_tiles(l)))
                pe.wait_ge(S["gd_state"], 8 * (l + 1))
                post(2)

                evacuated(pe, seg_of(l, "mqk"))
                evacuated(pe, seg_of(l, "mv"))
                for t in range(NT):
                    for i in range(2):
                        at = (t % 2) * 256 + i * P
                        last = nc.tensor.transpose(bank[2 + t // 2][:, at:at + P], mk[:, i, t * P:(t + 1) * P], ident)
                last.then_inc(S["mkt_psum"], 1)
                pe.wait_ge(S["mkt_out"], l + 1)
                pe.wait_ge(S["pads_set"], l + 1)
                for u, (d, t) in enumerate(UNITS):
                    g = 8 * l + u
                    gives = u in out_units[l]
                    o = sofar([len(v) for v in out_units], l) + len([v for v in out_units[l] if v <= u])
                    ts = slice(t * P, (t + 1) * P)
                    if g > 0:
                        pe.wait_ge(S["ml_ecol"], g)
                    mm(bank[5][0:4, 0:P], gates[:, t, 8 * d:8 * d + 4], ident, start=True, stop=True)
                    mm(bank[5][0:4, P:2 * P], lgate[:, t, 4 * d:4 * d + 4], tri[d], start=True, stop=True)\
                        .then_inc(S["ml_small"], 1)
                    if g > 0:
                        pe.wait_ge(S["ml_state"], g)
                    if gives:
                        for h in range(HEADS):
                            i, r = h // 2, 64 * (h % 2)
                            last = mm(bank[3 + 3 * (h % 2)][:, H(i)], mk[r:r + 64, i, ts], mq[r:r + 64, i, ts],
                                      start=True, stop=True)
                        last.then_inc(S["ml_qk"], 1)
                    pe.wait_ge(S["ml_rows"], g + 1)
                    pe.wait_ge(S["ml_exp"], g + 1)
                    mm(bank[5][:, 256:260], mrow[:, 5, :], ident[0:4, 0:4].rearrange("p (i r) -> p r i", r=2),
                       start=True, stop=True)
                    mm(bank[5][:, 260:264], mrow[:, 6, :], ident[0:4, 0:4], start=True, stop=True)
                    end = P - 1 if d == 0 else 0
                    for i in range(2):
                        last = mm(bank[5][:, 264 + i:265 + i], selp[i], mrow[:, 7, end:end + 1], start=True, stop=True)
                    last.then_inc(S["ml_cols"], 1)
                    if gives:
                        mm(bank[2][:, :], ident_b, mask_b[d], start=True, stop=False)
                        for q in range(HEADS):
                            h = 2 * (q % 2) + q // 2
                            mm(bank[2][:, H(q)], mrow[:, 1, :], sel[h], start=False, stop=False)
                            last = mm(bank[2][:, H(q)], sel[h], mrow[:, 3, :], start=False, stop=q == HEADS - 1)
                        last.then_inc(S["ml_arg"], 1)
                        for i in range(2):
                            last = mm(bank[7][:, i * P:(i + 1) * P], selp[i], mrow[:, 7, :], start=True, stop=True)
                        last.then_inc(S["ml_qb"], 1)
                    if gives:
                        pe.wait_ge(S["ml_p"], o)
                        pe.wait_ge(S["ml_qg"], o)
                        for h in range(HEADS):
                            i, r = h // 2, 64 * (h % 2)
                            dst = bank[4 + 2 * (h % 2)][:, 129 * i:129 * i + 129]
                            mm(dst, work[:, 1, H(2 * (h % 2) + i)], mv[:, t, h, :], start=True, stop=False)
                            last = mm(dst, work[r:r + 64, 2, i * P:(i + 1) * P], mstate[r:r + 64, d, i, :],
                                      start=False, stop=True)
                        last.then_inc(S["ml_num"], 1)
                    pe.wait_ge(S["ml_kw"], g + 1)
                    for h in range(HEADS):
                        i, r = h // 2, 64 * (h % 2)
                        last = mm(mlstm_c(i)[r:r + 64, :], work[:, 3, 64 * h:64 * h + 64], mv[:, t, h, :], start=True, stop=True)
                    last.then_inc(S["ml_c"], 1)
                    if gives:
                        pe.wait_ge(S["ml_h"], 2 * o)
                    if u < 6:
                        dense(l, ("aq", "ak", "av")[u // 2], [2 * (u % 2), 2 * (u % 2) + 1])
                post(1)

                evacuated(pe, seg_of(l, "av"))
                for j in range(8):
                    src = (aq if j < 4 else ak)[:, j % 4, CTX:TOK]
                    if j >= 2:
                        pe.wait_ge(S["rope_out"], 8 * l + j - 1)
                    mm(bank[4 + j % 2][:, 0:LAT], rope_r, src, start=True, stop=True).then_inc(S["rope_psum"], 1)
                pe.wait_ge(S["rope_out"], 8 * l + 8)
                for k in range(attn_units(l + 1) - attn_units(l)):
                    g = attn_units(l) + k
                    t = token_tiles(l)[k // 4]
                    h = k % 4
                    nk = CTX if t < 2 else TOK
                    if g >= 1:
                        pe.wait_ge(S["at_e"], 2 * g)
                    for m in range(2):
                        r = 64 * m
                        last = mm(bank[2 + m][:, 0:nk], aq[r:r + 64, h, t * P:(t + 1) * P], ak[r:r + 64, h, 0:nk],
                                  start=True, stop=True)
                    last.then_inc(S["at_s"], 1)
                    pe.wait_ge(S["at_w"], g + 1)
                    if g >= 1:
                        pe.wait_ge(S["at_wtout"], g)
                    for kt in range(nk // P):
                        last = nc.tensor.transpose(bank[4][:, H(kt)], work[:, 2, H(kt)], ident)
                    last.then_inc(S["at_wt"], 1)
                    pe.wait_ge(S["at_wtout"], g + 1)
                    if g >= 1:
                        pe.wait_ge(S["at_oout"], g)
                    for kt in range(nk // P):
                        last = mm(bank[5][:, 0:P], work[:, 3, H(kt)], av[:, kt, H(h)], start=kt == 0, stop=kt == nk // P - 1)
                    last.then_inc(S["at_o"], 1)
                post(0)
                for j in range(24):
                    dense(l, "bg", [j])
                    dense(l, "by", [j])
                dense(l, "wo")
                norm(l, 1)
                norm(l, 2)
                pe.wait_ge(S["h_ready"], 2 * KD * l + 2 * KD)
                dense(l, "ff1")
                dense(l, "ff2")
                norm(l, 3)

            pe.wait_ge(S["res_ready"], 2 * DEPTH * KD)
            for t in range(2):
                for hf in range(2):
                    for q in range(4):
                        last = nc.tensor.transpose(bank[2 + 2 * t + hf][:, q * P:(q + 1) * P],
                                                   xt[:, 4 * hf + q, CTX + t * P:CTX + (t + 1) * P], ident)
                    last.then_inc(S["final_psum"], 1)


_INS = ["x", "c", "ctx", "c_ctx", "w_ada", "b_ada", "norm_gains", "w_in", "b_in", "a_lambda", "a_norm",
        "m_fbias", "m_norm", "g_conv", "g_alog", "g_dtbias", "g_norm", "w_branch", "w_out", "w_ff1", "w_ff2"]


def kernel(**inputs):
    import numpy as _np
    import concourse.bacc as _bacc
    from concourse import mybir as _mybir
    from concourse.bass_utils import run_bass_kernel_spmd as _run

    nc = _bacc.Bacc("TRN2", target_bir_lowering=False, num_devices=1)
    arrays, args = {}, []
    const_f, const_b, const_m = shape_constants()
    every = [(n, _np.ascontiguousarray(inputs[n])) for n in _INS]
    every += [("const_f", const_f), ("const_b", const_b), ("const_m", const_m)]
    for name, a in every:
        arrays[f"in_{name}"] = a
        args.append(nc.dram_tensor(f"in_{name}", a.shape, _mybir.dt.from_np(a.dtype), kind="ExternalInput").ap())
    args.append(nc.dram_tensor("out_0", (1, LAT, DM), F32, kind="ExternalOutput").ap())
    hybrid_trunk(nc, *args)
    r = _run(nc, [arrays], core_ids=[0])
    return r.results[0]["out_0"]
```

```python
import math
from contextlib import ExitStack

import numpy as np

import concourse.bass as bass
from concourse import mybir

F32 = mybir.dt.float32
BF16 = mybir.dt.bfloat16
U8 = mybir.dt.uint8
ALU = mybir.AluOpType
ACT = mybir.ActivationFunctionType
AX_X = mybir.AxisListType.X

P = 128
DEPTH, DM, CTX, LAT = 2, 1024, 256, 256
TOK = CTX + LAT
KD = DM // P
NT = TOK // P
HEADS, A_HD, M_QK, M_V, G_HD = 4, 64, 64, 128, 128
CONV_K, D_FF, GRID_W = 5, 4096, 64
FT = D_FF // P
EPS = 1e-6
LEVELS = 7
RING = 4
CW = 2048

A_Q, A_K, A_V = 0, 512, 1024
M_QKC, M_VC, M_O, M_GATES = 1536, 2048, 2560, 3072
G_Q, G_K, G_V, G_Z, G_GATES, BR_G = 3088, 3600, 4112, 4624, 5136, 5152

B_AQ, B_AK, B_AV, B_MQ, B_MK, B_MV, B_MO, B_GQ, B_GZ, B_BG = 0, 4, 8, 12, 14, 16, 20, 24, 36, 40
B_ADA, R_C = 64, 112
R_GAIN, R_CONV, R_AN, R_MN, R_GN = 0, 32, 92, 93, 97

UNITS = [(0, 0), (1, 1), (0, 1), (1, 0), (0, 2), (1, 3), (0, 3), (1, 2)]
FIRST_VISIT = {0, 1, 4, 5}


GAPS = 2 * (LEVELS - 1)


def shape_constants():
    k = np.arange(P)
    ident = np.eye(P, dtype=np.float32)
    tri_f = (k[:, None] <= k[None, :]).astype(np.float32)
    tri_b = (k[:, None] >= k[None, :]).astype(np.float32)
    rope = np.zeros((P, P), np.float32)
    for m in range(P):
        if (m // 16) % 2 == 0:
            rope[m + 16, m] = -1.0
        else:
            rope[m - 16, m] = 1.0
    half = A_HD // 2
    inv_freq = np.float32(10000.0) ** (-np.arange(0, half, 2, dtype=np.float32) / np.float32(half))
    tok = np.arange(LAT)
    row, col = (tok // GRID_W).astype(np.float32), (tok % GRID_W).astype(np.float32)
    ar, ac = row[:, None] * inv_freq, col[:, None] * inv_freq
    ang = np.concatenate([ar, ar, ac, ac] * 2, axis=-1).T.astype(np.float32)
    sel = np.zeros((P, HEADS, P), np.float32)
    selp = np.zeros((P, 2, P), np.float32)
    for h in range(HEADS):
        sel[h, h, :] = 1.0
        selp[h, h // 2, 64 * (h % 2):64 * (h % 2) + 64] = 1.0
    f = np.concatenate([ident, tri_f, tri_b, rope, np.cos(ang), np.sin(ang),
                        sel.reshape(P, -1), selp.reshape(P, -1)], axis=1).astype(np.float32)
    b = np.stack([ident, (1 - tri_f) * -1e30, (1 - tri_b) * -1e30], axis=1).astype(np.float32)
    m = np.zeros((P, 2, LEVELS, P), np.float32)
    for lv in range(LEVELS):
        blk = k >> lv
        up = (blk[:, None] // 2 == blk[None, :] // 2) & (blk[:, None] % 2 == 0) & (blk[None, :] % 2 == 1)
        m[:, 0, lv], m[:, 1, lv] = up, up.T
    return f, b, m


def plan():
    segs, chunks, where, gaps, beside = [], [], {}, {}, {}
    taken = {"act": 0, "dve": 0}

    def chunk(l, kind, i):
        chunks.append([l, kind, i, None])
        return len(chunks) - 1

    def seg(l, kind, i, c, engine, bank=None, evacuated=True):
        n = len(segs)
        if evacuated:
            taken[engine] += 1
        if bank is None:
            bank = len([s for s in segs if s[4] < 2 and s[1] != "ff2"]) % 2
        segs.append((l, kind, i, c, bank,
                     engine if evacuated else None, taken[engine]))
        if c is not None:
            chunks[c][3] = n
        where.setdefault((l, kind), []).append(n)
        return n

    def group(l, kind, engine, order=range(4), bank=None):
        for i in order:
            if i % 2 == 0:
                group.chunk = chunk(l, kind, i // 2)
            n = seg(l, kind, i, group.chunk, engine, bank)
        return n

    def modulation(l, n, banks=(None, None)):
        got = [seg(l, "ada", n, chunk(l, "ada", n), "act", banks[0])]
        if n > 0:
            got.append(seg(l, "adat", n - 1, None, "dve", banks[1]))
        return got

    for l in range(DEPTH):
        if l == 0:
            for n in range(24):
                modulation(l, n)
            seg(l, "adat", 23, None, "dve")
        seg(l, "gate", 0, None, "dve")
        group(l, "gq", "act")
        group(l, "gk", "act")
        group(l, "gv", "act")
        group(l, "gz", "dve")
        count = 0
        for p in range(4):
            pieces = []
            for q in range(4):
                if q < 3:
                    kind, i = (("mqk", "mv", "mo")[(3 * p + q) // 4], (3 * p + q) % 4)
                    n = group(l, kind, "act" if kind == "mo" else "dve", [i], 2 + 4 * (count % 2))
                    count += 1
                    pieces += [[(n, k, k + 1)] for k in range(4)]
                if l + 1 < DEPTH:
                    got = modulation(l + 1, 4 * p + q, (2 + 4 * (count % 2), 2 + 4 * ((count + 1) % 2)))
                    count += len(got)
                    pieces += [[(got[0], 0, 2)], [(got[0], 2, 4)] + [(n, 0, 4) for n in got[1:]]]
            for x in range(GAPS):
                gaps[(l, p, x)] = sum(pieces[x * len(pieces) // GAPS:(x + 1) * len(pieces) // GAPS], [])
        for u in range(8):
            beside[(l, u)] = [group(l, ("aq", "ak", "av")[m // 4], "dve", [m % 4])
                              for m in range(12 * u // 8, 12 * (u + 1) // 8)]
            if l + 1 < DEPTH:
                beside[(l, u)] += modulation(l + 1, 16 + u)
                if u == 7:
                    beside[(l, u)].append(seg(l + 1, "adat", 23, None, "dve"))
        for b in (2, 1, 0):
            for half in range(2):
                wb = chunk(l, "wb", (b, half))
                for nb in range(2):
                    bg = chunk(l, "bg", (b, 2 * half + nb))
                    for i in range(2):
                        cc = 4 * half + 2 * nb + i
                        seg(l, "bg", (b, cc), bg, "act")
                        seg(l, "by", (b, cc), wb, "dve")
        for nb in range(4):
            c = chunk(l, "wo", nb)
            for i in range(2):
                seg(l, "wo", 2 * nb + i, c, "act")
        for n in range(16):
            c = chunk(l, "ff1", n)
            for i in range(2):
                seg(l, "ff1", 2 * n + i, c, "act")
        for nb in range(4):
            for kc in range(4):
                c = chunk(l, "ff2", (nb, kc))
                for i in range(2):
                    seg(l, "ff2", (nb, kc, i), c, "act", bank=2 + (2 * nb + i) % 6, evacuated=kc == 3)
    return segs, chunks, where, gaps, beside


def hybrid_trunk(nc, x, c, ctx, c_ctx, w_ada, b_ada, norm_gains, w_in, b_in, a_lambda, a_norm,
                 m_fbias, m_norm, g_conv, g_alog, g_dtbias, g_norm, w_branch, w_out, w_ff1, w_ff2,
                 const_f, const_b, const_m, out):
    SEGS, CHUNKS, WHERE, IN_GAP, BESIDE = plan()

    def tokens(l):
        return (0, TOK) if l < DEPTH - 1 else (CTX, LAT)

    with ExitStack() as stack:
        def sb(name, shape, dt=F32):
            return stack.enter_context(nc.sbuf_tensor(name, shape, dt))

        def sem(name):
            return stack.enter_context(nc.semaphore(name))

        bank = [stack.enter_context(nc.psum_tensor(f"bank{i}", [P, 512], F32)) for i in range(8)]

        cf = sb("cf", [P, 4 * P + 2 * LAT + 6 * P])
        ident, tri = cf[:, 0:P], [cf[:, P:2 * P], cf[:, 2 * P:3 * P]]
        rope_r = cf[:, 3 * P:4 * P]
        cos_t, sin_t = cf[:, 512:768], cf[:, 768:1024]
        sel = [cf[0:4, 1024 + h * P:1024 + (h + 1) * P] for h in range(HEADS)]
        selp = [cf[0:4, 1536 + i * P:1536 + (i + 1) * P] for i in range(2)]
        cb = sb("cb", [P, 3, P], BF16)
        ident_b = cb[:, 0, :]
        mask_b = [cb[:, 1 + d, :].unsqueeze(1).broadcast_to((P, HEADS, P)) for d in range(2)]
        cm = sb("cm", [P, 2, LEVELS, P], U8)
        ones = sb("ones", [P, P])
        cols1 = sb("cols1", [P, DEPTH, P])
        cols2 = sb("cols2", [P, DEPTH, P])
        gate_bias = sb("gate_bias", [P, DEPTH, 32])
        fdt_bias = sb("fdt_bias", [P, DEPTH, 16])
        alog = sb("alog", [P, DEPTH, 8])
        v_bias = sb("v_bias", [P, 2, 512])
        w_gates = sb("w_gates", [P, KD, 32])

        xt = sb("xt", [P, KD, TOK])
        ht = sb("ht", [P, KD, TOK])
        ring = sb("ring", [P, RING, CW])
        arena = sb("arena", [P, 19480])
        work = sb("work", [P, 18, 512])

        def part(at, n):
            return arena[:, at:at + n]

        gq = part(0, 2048).rearrange("p (h t) -> p h t", h=4)
        gk = part(2048, 2048).rearrange("p (h t) -> p h t", h=4)
        gz = part(4096, 2048).rearrange("p (h t) -> p h t", h=4)
        gk_tok = part(6144, 2048).rearrange("p (t c) -> p t c", t=NT)
        gv_tok = part(8192, 2048).rearrange("p (t c) -> p t c", t=NT)
        oacc = part(10240, 2048).rearrange("p (t c) -> p t c", t=NT)
        raw = part(14336, 1560).rearrange("p (r s c) -> p r s c", r=3, s=2)
        mq = part(12288, 1024).rearrange("p (i t) -> p i t", i=2)
        mk = part(13312, 1024).rearrange("p (i t) -> p i t", i=2)
        mo = part(14336, 2048).rearrange("p (h t) -> p h t", h=4)
        mv = part(16384, 2064).rearrange("p (t h c) -> p t h c", t=NT, h=4)
        mk_tok = part(18448, 1024).rearrange("p (t c) -> p t c", t=NT)
        aq, ak, av = gq, gk, gk_tok
        hidden = part(0, 16384).rearrange("p (f t) -> p f t", f=FT)
        ot_of = {1: part(0, 4096).rearrange("p (k t) -> p k t", k=KD), 3: work[:, 0:8, :]}
        level_masks = part(1024, 2 * LEVELS * P)
        rows1 = part(0, DEPTH * P).rearrange("p (l c) -> p l c", l=DEPTH)
        rows2 = part(256, DEPTH * P).rearrange("p (l c) -> p l c", l=DEPTH)
        lamv = part(512, DEPTH * 4 * A_HD).rearrange("p (l a c) -> p l a c", l=DEPTH, a=4)
        merged = work[:, 10:18, :]
        gate_sig = [part(12288, 512), part(12800, 512)]
        gated = [part(13312, 512), part(13824, 512)]

        silu_c = sb("silu_c", [P, 2, KD])
        ada = sb("ada", [P, 2, 48, 2])
        mod_scale = sb("mod_scale", [P, 2, KD, 2])
        out_gate = sb("out_gate", [P, 2, KD, 2])
        gates = sb("gates", [P, NT, 32])
        zgate = sb("zgate", [P, NT, 16])
        egate = sb("egate", [P, NT, 16])
        lgate = sb("lgate", [P, NT, 16])
        coef = sb("coef", [P, 16])
        beta = sb("beta", [P, NT, 8])
        nbeta = sb("nbeta", [P, NT, 8])
        lam2 = sb("lam2", [P, DEPTH, 2])
        nlam = sb("nlam", [P, DEPTH])
        gcol = [sb(f"gcol{d}", [P, 12]) for d in range(2)]
        gecol = [sb(f"gecol{d}", [P, 16]) for d in range(2)]
        gstate = sb("gstate", [P, 2, HEADS, G_HD])
        row_buf = sb("row_buf", [P, 8, P])
        mrow = row_buf[0:4, :, :]
        grow = [mrow[:, 4 * d:4 * d + 3, :] for d in range(2)]
        rstd = row_buf[:, 0:4, :].rearrange("p a c -> p (a c)")
        ada_rows = sb("ada_rows", [2, 2, 256])
        mmax = sb("mmax", [4, 2])
        mcol = sb("mcol", [P, 16])
        mden = sb("mden", [P, 8])
        mstate = gstate[:, :, :, :].rearrange("p d h c -> p (d h c)")[:, 0:4 * (M_V + 1)]\
            .rearrange("p (d i c) -> p d i c", d=2, i=2)
        amax = sb("amax", [P, 2, 8])
        post_stat = sb("post_stat", [P, NT, HEADS])

        names = (
            "consts_in params_in rows_in x_in chunk_in0 chunk_in1 chunk_in2 chunk_in3 gatew_in out_stored "
            "ones_set masks_ready pads_set states_zero "
            "dense_ready taken_act taken_dve act_step dve_step pool_step "
            "vbias_in cols_psum cols_ready csig silu_ready ada_ready "
            "xtr_psum xtr_ready lam_sum lam_exp lam_ready "
            "sq_ready sq_used norm_sum norm_root rstd_ready scaled_ready h_ready "
            "gates_z gates_exp gates_ready gate_segment_done "
            "conv_done conv_sig conv_out vt_psum vt_out l2_sq l2_sum l2_root l2_out kt_psum kt_out "
            "gz_sig "
            "slots_set "
            "ml_small ml_rows ml_exp ml_cols ml_ecol ml_arg ml_decay ml_qk ml_p ml_qb ml_qg ml_kw ml_num "
            "ml_h ml_c ml_state mkt_psum mkt_out "
            "post_sq post_sum post_root post_norm post_tr post_out "
            "rope_psum rope_out at_s at_max at_e at_w at_wt at_wtout at_o at_oout "
            "y_ready hid_ready res_ready final_psum final_out"
        ).split()
        S = {n: sem(n) for n in names}
        gd_names = ("small rows cols ecol neg ke arg decay qk b qkd eye u0 t0 t1 m mout u uout t tout w wout qb qg "
                    "v vn o oacc s state").split()
        G = [{n: sem(f"gd_{n}_{way}") for n in gd_names} for way in ("forward", "backward")]

        block = stack.enter_context(nc.Block())

        out_units = [[u for u in range(8) if l < DEPTH - 1 or UNITS[u][1] >= 2] for l in range(DEPTH)]

        CHUNK_OF = [[0, 1, 2, 3], [1, 0, 3, 2]]

        def gd_gives(l, p):
            return l < DEPTH - 1 or p >= 2

        def gd_outs(l, p):
            return sum(4 if k < DEPTH - 1 else 2 for k in range(l)) + (p + 1 if l < DEPTH - 1 else max(p - 1, 0))

        def slot(d, i):
            return work[:, 9 * d + i, :]

        def parity(a, lv, q):
            return a.rearrange("p (h b q s) -> p h b q s", h=HEADS, q=2, s=2 ** lv)[:, :, :, q, :]

        def compact(a, lv):
            return a.rearrange("p (h b s) -> p h b s", h=HEADS, s=2 ** lv)

        def sofar(counts, l):
            return sum(counts[:l])

        def evacuated(eng, n):
            eng.wait_ge(S["taken_" + SEGS[n][5]], SEGS[n][6])

        def completed(fill):
            return [n for n, _, to in fill if to == 4]

        def seg_of(l, kind, i=-1):
            return WHERE[(l, kind)][i]

        def token_tiles(l):
            t0, n = tokens(l)
            return list(range(t0 // P, (t0 + n) // P))

        def seg_tokens(l, kind):
            return (0, TOK) if kind in ("gk", "gv", "mqk", "mv", "ak", "av") else tokens(l)

        def post_count(l, b):
            return 3 * NT * l + {2: 0, 1: 1, 0: 2}[b] * len(token_tiles(l))

        def attn_units(l):
            return sum(4 * len(token_tiles(k)) for k in range(l))

        def norm_count(l, which):
            return 4 * l + which

        def scaled_count(l, which):
            return 2 * KD * l + KD * (which // 2)

        def mlstm_c(i):
            return bank[3][:, 129 * i:129 * i + 129]

        @block.sync
        def _(sp):
            sp.dma_start(cf[:, :], const_f).then_inc(S["consts_in"], 16)
            sp.dma_start(work[:, 8, 0:3 * P].rearrange("p (a c) -> p a c", a=3), const_b).then_inc(S["consts_in"], 16)
            sp.dma_start(level_masks, const_m.rearrange("p a b c -> p (a b c)")).then_inc(S["consts_in"], 16)
            rows_of = lambda v: v.rearrange("(j p) -> j p", p=P)
            for l in range(DEPTH):
                table1 = [(B_AQ, b_in[l, 0:3072]), (B_GQ, b_in[l, G_Q:G_Q + 2048]), (B_BG, b_in[l, BR_G:BR_G + 3072]),
                          (B_ADA, b_ada[l, :]), (R_C, c[0, :]), (R_C + 8, c_ctx[:])]
                for r, src in table1:
                    v = rows_of(src)
                    sp.dma_start(rows1[r:r + v.shape[0], l, :], v).then_inc(S["rows_in"], 16)
                sp.dma_start(rows2[0:32, l, :], norm_gains[l].rearrange("g (j p) -> (g j) p", p=P)).then_inc(S["rows_in"], 16)
                sp.dma_start(rows2[R_CONV:R_CONV + 60, l, :],
                             g_conv[l].rearrange("k (j p) -> (k j) p", p=P)).then_inc(S["rows_in"], 16)
                sp.dma_start(rows2[R_AN:R_AN + 1, l, :], a_norm[l:l + 1, :]).then_inc(S["rows_in"], 16)
                sp.dma_start(rows2[R_MN:R_MN + 4, l, :], m_norm[l]).then_inc(S["rows_in"], 16)
                sp.dma_start(rows2[R_GN:R_GN + 1, l, :], g_norm[l:l + 1, :]).then_inc(S["rows_in"], 16)
            sp.dma_start(ht[:, 0:4, :].rearrange("p (t a) c -> p t (a c)", t=2),
                         ctx[0].rearrange("(t p) c -> p t c", p=P)).then_inc(S["x_in"], 16)
            sp.dma_start(ht[:, 4:8, :].rearrange("p (t a) c -> p t (a c)", t=2),
                         x[0].rearrange("(t p) c -> p t c", p=P)).then_inc(S["x_in"], 16)

            def chunk_source(l, kind, i):
                tall = lambda w: w.rearrange("(k p) n -> p k n", p=P)
                cols = {"gq": G_Q, "gk": G_K, "gv": G_V, "gz": G_Z, "mqk": M_QKC, "mv": M_VC, "mo": M_O,
                        "aq": A_Q, "ak": A_K, "av": A_V}
                if kind == "ada":
                    return tall(w_ada[l][:, 256 * i:256 * i + 256]), 8
                if kind in cols:
                    at = cols[kind] + 256 * i
                    return tall(w_in[l][:, at:at + 256]), 8
                if kind == "bg":
                    at = BR_G + 1024 * i[0] + 256 * i[1]
                    return tall(w_in[l][:, at:at + 256]), 8
                if kind == "wb":
                    return tall(w_branch[l, i[0]][:, 512 * i[1]:512 * i[1] + 512]), 4
                if kind == "wo":
                    return tall(w_out[l][:, 256 * i:256 * i + 256]), 8
                if kind == "ff1":
                    return tall(w_ff1[l][:, 256 * i:256 * i + 256]), 8
                return tall(w_ff2[l][1024 * i[1]:1024 * i[1] + 1024, 256 * i[0]:256 * i[0] + 256]), 8

            for n, (l, kind, i, _) in enumerate(CHUNKS):
                if n >= RING:
                    sp.wait_ge(S["dense_ready"], CHUNKS[n - RING][3] + 1)
                src, k = chunk_source(l, kind, i)
                sp.dma_start(ring[:, n % RING, :].rearrange("p (k n) -> p k n", k=k), src)\
                    .then_inc(S[f"chunk_in{n % RING}"], 16)
                if kind == "gq" and i == 0:
                    if l > 0:
                        sp.wait_ge(S["dense_ready"], seg_of(l - 1, "gate") + 1)
                    tall = lambda w: w.rearrange("(k p) n -> p k n", p=P)
                    sp.dma_start(w_gates[:, :, 0:16], tall(w_in[l][:, M_GATES:M_GATES + 16])).then_inc(S["gatew_in"], 16)
                    sp.dma_start(w_gates[:, :, 16:32], tall(w_in[l][:, G_GATES:G_GATES + 16])).then_inc(S["gatew_in"], 16)
            for t in range(2):
                sp.wait_ge(S["final_out"], 2 * t + 2)
                sp.dma_start(out[0, t * P:(t + 1) * P, :],
                             work[:, 2 * t:2 * t + 2, :].rearrange("p a c -> p (a c)")).then_inc(S["out_stored"], 16)
            sp.wait_ge(S["out_stored"], 32)

        @block.gpsimd
        def _(pool):
            steps = [0]

            def link(ins):
                steps[0] += 1
                ins.then_inc(S["pool_step"], 1)
                pool.wait_ge(S["pool_step"], steps[0])

            nc.gpsimd.memset(ones[:, :], 1.0).then_inc(S["ones_set"], 1)
            for d in range(2):
                nc.gpsimd.memset(slot(d, 5), 0.0).then_inc(S["slots_set"], 1)
            for l in range(DEPTH):
                flat = lambda v: v.rearrange("a b -> (a b)").partition_broadcast(P)
                pool.dma_start(gate_bias[:, l, 0:16], b_in[l, M_GATES:M_GATES + 16].partition_broadcast(P)).then_inc(S["params_in"], 16)
                pool.dma_start(gate_bias[:, l, 16:32], b_in[l, G_GATES:G_GATES + 16].partition_broadcast(P)).then_inc(S["params_in"], 16)
                pool.dma_start(fdt_bias[:, l, 0:8], flat(m_fbias[l])).then_inc(S["params_in"], 16)
                pool.dma_start(fdt_bias[:, l, 8:16], flat(g_dtbias[l])).then_inc(S["params_in"], 16)
                pool.dma_start(alog[:, l, :], flat(g_alog[l])).then_inc(S["params_in"], 16)
                pool.dma_start(lamv[:, l, :, :].rearrange("p a b -> p (a b)"), flat(a_lambda[l])).then_inc(S["params_in"], 16)

            pool.wait_ge(S["consts_in"], 16 * 3)

            for l in range(DEPTH):
                if l > 0:
                    evacuated(pool, seg_of(l - 1, "av"))
                for a, at in ((0, M_VC), (1, A_V)):
                    pool.dma_start(v_bias[:, a, :], b_in[l, at:at + 512].partition_broadcast(P)).then_inc(S["vbias_in"], 16)
                if l > 0:
                    pool.wait_ge(S["res_ready"], 2 * l * KD)
                for r in range(3):
                    for s in range(2):
                        nc.gpsimd.memset(raw[:, r, s, 0:2], 0.0)
                        nc.gpsimd.memset(raw[:, r, s, 258:260], 0.0)
                nc.gpsimd.memset(mv[:, :, :, M_V:M_V + 1], 1.0).then_inc(S["pads_set"], 1)
                nc.gpsimd.memset(gstate[:, :, :, :], 0.0).then_inc(S["states_zero"], 1)
                nc.gpsimd.memset(mmax[:, :], 0.0).then_inc(S["states_zero"], 1)

                for j in range(8):
                    t0, n = seg_tokens(l, "gq" if j < 4 else "gk")
                    src = (gq if j < 4 else gk)[:, j % 4, t0:t0 + n]
                    pool.wait_ge(S["conv_out"], 12 * l + j + 1)
                    if j >= 2 or l > 0:
                        pool.wait_ge(S["l2_sum"], 8 * l + j - 1)
                    nc.gpsimd.tensor_tensor(work[:, 10 + j % 2, 0:n], src, src, ALU.mult).then_inc(S["l2_sq"], 1)

                four = lambda a: a.rearrange("p (h c) -> p h c", h=4)
                pool.wait_ge(S["conv_out"], 12 * (l + 1))
                pool.wait_ge(S["l2_out"], 8 * (l + 1))
                for p in range(4):
                    g = 4 * l + p
                    for d in range(2):
                        if g > 0:
                            pool.wait_ge(G[d]["v"], g)
                        nc.gpsimd.tensor_copy(four(slot(d, 3)), ident.unsqueeze(1).broadcast_to((P, 4, P)))\
                            .then_inc(G[d]["eye"], 1)
                    for d in range(2):
                        pool.wait_ge(G[d]["neg"], g + 1)
                        keys = four(gk_tok[:, CHUNK_OF[d][p], :])
                        for tile, at in ((6, 12), (7, 4)):
                            nc.gpsimd.tensor_tensor(four(slot(d, tile)), keys,
                                                    gecol[d][:, at:at + 4].unsqueeze(2).broadcast_to((P, 4, P)), ALU.mult)\
                                .then_inc(G[d]["ke"], 1)

                def post_squares(b):
                    for j, t in enumerate(token_tiles(l)):
                        n = post_count(l, b) + j
                        if b == 2:
                            for d in range(2):
                                pool.wait_ge(G[d]["oacc"], gd_outs(l, 3))
                        elif b == 1:
                            pool.wait_ge(S["ml_h"], 2 * sofar([len(v) for v in out_units], l + 1))
                        else:
                            pool.wait_ge(S["at_oout"], attn_units(l + 1))
                        if n >= 2:
                            pool.wait_ge(S["post_sum"], n - 1)
                        nc.gpsimd.tensor_tensor(work[:, 8 + j % 2, :], oacc[:, t, :], oacc[:, t, :],
                                                ALU.mult).then_inc(S["post_sq"], 1)
                post_squares(2)
                post_squares(1)

                t0, n = tokens(l)
                for j in range(16):
                    cc = j % 8
                    if j == 8:
                        post_squares(0)
                    evacuated(pool, seg_of(l, "by", 8 + j))
                    nc.gpsimd.tensor_tensor(merged[:, cc, 0:n], merged[:, cc, 0:n], gated[j % 2][:, 0:n],
                                            ALU.add).then_inc(S["y_ready"], 1)
                    if cc == 7:
                        pool.wait_ge(S["y_ready"], 16 * l + j + 1)
                for f in range(FT):
                    evacuated(pool, seg_of(l, "ff1", f))
                    nc.gpsimd.tensor_tensor(hidden[:, f, 0:n], work[:, 8 + f % 2, 0:n], work[:, 8 + f % 2, 0:n],
                                            ALU.mult).then_inc(S["hid_ready"], 1)

        @block.scalar
        def _(act):
            steps = [0]

            def link(ins):
                steps[0] += 1
                ins.then_inc(S["act_step"], 1)
                act.wait_ge(S["act_step"], steps[0])

            def dense(l, kind, idx=None):
                for n in WHERE[(l, kind)] if idx is None else [WHERE[(l, kind)][k] for k in idx]:
                    take(n)

            def take(n):
                l, kind, i, _, bk, engine, o = SEGS[n]
                if engine != "act" and kind != "gz":
                    return
                act.wait_ge(S["dense_ready"], n + 1)
                ps = bank[bk]
                t0, tn = seg_tokens(l, kind)
                if kind == "ada":
                    if 24 * l + i >= 2:
                        k = 24 * l + i - 2
                        act.wait_ge(S["dense_ready"], seg_of(k // 24, "adat", k % 24) + 1)
                    nc.scalar.copy(ada_rows[:, i % 2, :], ps[0:2, 0:256]).then_inc(S["taken_act"], 1)
                elif kind in ("gq", "gk", "gv"):
                    j = {"gq": 0, "gk": 4, "gv": 8}[kind] + i
                    if j >= 3:
                        act.wait_ge(S["conv_done"], 12 * l + j - 2)
                    else:
                        act.wait_ge(S["pads_set"], l + 1)
                    s0, sn = t0 // CTX, tn // CTX
                    nc.scalar.activation(raw[:, j % 3, s0:s0 + sn, 2:258],
                                         ps[:, 0:tn].rearrange("p (s c) -> p s c", s=sn), ACT.Identity,
                                         bias=cols1[:, l, B_GQ + j:B_GQ + j + 1]).then_inc(S["taken_act"], 1)
                elif kind == "gz":
                    if 4 * l + i >= 2:
                        evacuated(act, prev_gz(l, i, 2))
                    nc.scalar.activation(work[:, 8 + i % 2, 0:tn], ps[:, 0:tn], ACT.Sigmoid,
                                         bias=cols1[:, l, B_GZ + i:B_GZ + i + 1]).then_inc(S["gz_sig"], 1)
                elif kind == "mo":
                    if i == 0:
                        act.wait_ge(S["conv_done"], 12 * (l + 1))
                    nc.scalar.activation(mo[:, i, t0:t0 + tn], ps[:, 0:tn], ACT.Sigmoid,
                                         bias=cols1[:, l, B_MO + i:B_MO + i + 1]).then_inc(S["taken_act"], 1)
                elif kind == "bg":
                    b, cc = i
                    k = WHERE[(l, "bg")].index(n)
                    if k >= 2:
                        evacuated(act, seg_of(l, "by", k - 2))
                    nc.scalar.activation(gate_sig[k % 2][:, 0:tn], ps[:, 0:tn], ACT.Sigmoid,
                                         bias=cols1[:, l, B_BG + 8 * b + cc:B_BG + 8 * b + cc + 1])\
                        .then_inc(S["taken_act"], 1)
                elif kind == "wo":
                    nc.scalar.copy(ot_of[1][:, i, 0:tn], ps[:, 0:tn]).then_inc(S["taken_act"], 1)
                elif kind == "ff1":
                    if FT * l + i >= 2:
                        act.wait_ge(S["hid_ready"], FT * l + i - 1)
                    nc.scalar.activation(work[:, 8 + i % 2, 0:tn], ps[:, 0:tn], ACT.Relu).then_inc(S["taken_act"], 1)
                elif kind == "ff2" and engine == "act":
                    nb, _, q = i
                    nc.scalar.copy(ot_of[3][:, 2 * nb + q, 0:tn], ps[:, 0:tn]).then_inc(S["taken_act"], 1)

            def prev_gz(l, i, back):
                k = 4 * l + i - back
                return seg_of(k // 4, "gz", k % 4)

            act.wait_ge(S["ones_set"], 1)
            act.wait_ge(S["masks_ready"], 1)

            for l in range(DEPTH):
                act.wait_ge(S["cols_psum"], 2 * l + 1)
                nc.scalar.copy(cols1[:, l, :], bank[2 + 2 * l][:, 0:P]).then_inc(S["cols_ready"], 1)
                act.wait_ge(S["cols_psum"], 2 * l + 2)
                nc.scalar.copy(cols2[:, l, 0:98], bank[3 + 2 * l][:, 0:98]).then_inc(S["cols_ready"], 1)
            act.wait_ge(S["cols_ready"], 4)
            nc.scalar.activation(silu_c[:, :, :].rearrange("p a k -> p (a k)"), cols1[:, 0, R_C:R_C + 16],
                                 ACT.Sigmoid).then_inc(S["csig"], 1)
            for k in range(KD):
                act.wait_ge(S["xtr_psum"], k + 1)
                nc.scalar.copy(xt[:, k, :], bank[4 + k % 4][:, :]).then_inc(S["xtr_ready"], 1)
            act.wait_ge(S["lam_sum"], 1)
            nc.scalar.activation(lam2[:, :, :], lam2[:, :, :], ACT.Exp).then_inc(S["lam_exp"], 1)

            def norm(l, which):
                t0, n = (0, TOK) if which == 0 else tokens(l)
                q = norm_count(l, which)
                for k in range(KD):
                    if which in (0, 2):
                        src = xt[:, k, t0:t0 + n]
                        if which == 0 and l == 0:
                            act.wait_ge(S["xtr_ready"], KD)
                        elif k == 0:
                            act.wait_ge(S["res_ready"], KD * (2 * l + which // 2))
                    else:
                        src = ot_of[which][:, k, 0:n]
                        if k == 0:
                            evacuated(act, seg_of(l, "wo" if which == 1 else "ff2"))
                    if KD * q + k >= 2:
                        act.wait_ge(S["sq_used"], KD * q + k - 1)
                    nc.scalar.activation(work[:, 8 + k % 2, 0:n], src, ACT.Square).then_inc(S["sq_ready"], 1)
                act.wait_ge(S["sq_used"], KD * q + KD)
                nc.scalar.activation(rstd[:, 0:n], bank[7][:, 0:n], ACT.Sqrt, bias=eps_col[:, 0:1],
                                     scale=1.0 / DM).then_inc(S["norm_root"], 1)

            def modulate(l, which):
                t0, n = (0, TOK) if which == 0 else tokens(l)
                s = which // 2
                if which == 0:
                    act.wait_ge(S["ada_ready"], l + 1)
                for k in range(KD):
                    act.wait_ge(S["scaled_ready"], scaled_count(l, which) + k + 1)
                    for a in range(t0, t0 + n, CTX):
                        cond = 1 if a < CTX else 0
                        last = nc.scalar.activation(ht[:, k, a:a + CTX], work[:, k, a - t0:a - t0 + CTX], ACT.Identity,
                                                    scale=mod_scale[:, s, k, cond:cond + 1],
                                                    bias=ada[:, l % 2, 24 * s + k, cond:cond + 1])
                    last.then_inc(S["h_ready"], 1)

            eps_col = sb("eps_col", [P, 2])
            link(nc.scalar.activation(eps_col[:, 0:1], ones[:, 0:1], ACT.Copy, scale=EPS))

            for l in range(DEPTH):
                if l == 0:
                    dense(l, "ada")
                norm(l, 0)
                modulate(l, 0)
                act.wait_ge(S["gates_z"], l + 1)
                link(nc.scalar.activation(egate[:, :, :], egate[:, :, :], ACT.Exp, scale=-1.0))
                nc.scalar.activation(coef[:, 8:16], alog[:, l, :], ACT.Exp)
                nc.scalar.activation(beta[:, :, :], gates[:, :, 24:32], ACT.Exp, scale=-1.0)
                nc.scalar.activation(egate[:, :, :], egate[:, :, :], ACT.Ln, bias=1.0).then_inc(S["gates_exp"], 1)

                def conv_sigmoid(j):
                    t0, n = seg_tokens(l, "gq" if j < 4 else "gk")
                    act.wait_ge(S["conv_done"], 12 * l + j + 1)
                    if j >= 2:
                        act.wait_ge(S["conv_out"], 12 * l + j - 1)
                    nc.scalar.activation(work[:, 2 + j % 2, 0:n], work[:, j % 2, 0:n], ACT.Sigmoid).then_inc(S["conv_sig"], 1)

                def l2_root(j):
                    t0, n = seg_tokens(l, "gq" if j < 4 else "gk")
                    act.wait_ge(S["l2_sum"], 8 * l + j + 1)
                    if j >= 2:
                        act.wait_ge(S["l2_out"], 8 * l + j - 1)
                    nc.scalar.activation(work[:, 12 + j % 2, 0:n], bank[6 + j % 2][:, 0:n], ACT.Sqrt,
                                         bias=eps_col[:, 0:1]).then_inc(S["l2_root"], 1)

                for j in range(12):
                    dense(l, ("gq", "gk", "gv")[j // 4], [j % 4])
                    if j >= 1:
                        conv_sigmoid(j - 1)
                    if j >= 4:
                        l2_root(j - 4)
                conv_sigmoid(11)
                for h in range(4):
                    dense(l, "gz", [h])
                    act.wait_ge(S["vt_psum"], 4 * l + h + 1)
                    nc.scalar.copy(gv_tok[:, :, h * P:(h + 1) * P],
                                   bank[4 + h % 2][:, :].rearrange("p (t c) -> p t c", t=NT)).then_inc(S["vt_out"], 1)
                    act.wait_ge(S["kt_psum"], 4 * l + h + 1)
                    nc.scalar.copy(gk_tok[:, :, h * P:(h + 1) * P],
                                   bank[2 + h % 2][:, :].rearrange("p (t c) -> p t c", t=NT)).then_inc(S["kt_out"], 1)

                for p in range(4):
                    g = 4 * l + p
                    for d in range(2):
                        act.wait_ge(G[d]["small"], g + 1)
                        if g > 0:
                            act.wait_ge(G[d]["state"], g)
                        nc.scalar.copy(grow[d][:, 0, :], bank[4 * d + 3][0:4, 0:P])
                        nc.scalar.activation(grow[d][:, 1, :], bank[4 * d + 3][0:4, 0:P], ACT.Exp)
                        nc.scalar.mul(grow[d][:, 2, :], bank[4 * d + 3][0:4, 0:P], -1.0).then_inc(G[d]["rows"], 1)
                    for d in range(2):
                        act.wait_ge(G[d]["cols"], g + 1)
                        nc.scalar.activation(gecol[d][:, 0:12], gcol[d][:, :], ACT.Exp).then_inc(G[d]["ecol"], 1)
                    for d in range(2):
                        act.wait_ge(G[d]["arg"], g + 1)
                        nc.scalar.activation(slot(d, 0), bank[4 * d][:, :], ACT.Exp).then_inc(G[d]["decay"], 1)
                    for d in range(2):
                        act.wait_ge(G[d]["t0"], g + 1)
                        nc.scalar.copy(slot(d, 4), bank[4 * d + 3][:, :]).then_inc(G[d]["t1"], 1)
                    for lv in range(1, LEVELS):
                        for d in range(2):
                            act.wait_ge(G[d]["m"], (LEVELS - 1) * g + lv)
                            nc.scalar.copy(parity(slot(d, 5), lv, d), compact(bank[4 * d][:, 0:256], lv))\
                                .then_inc(G[d]["mout"], 1)
                        for x in (2 * lv - 2, 2 * lv - 1):
                            for n in completed(IN_GAP[(l, p, x)]):
                                take(n)
                    for d in range(2):
                        act.wait_ge(G[d]["w"], g + 1)
                        nc.scalar.copy(slot(d, 4), bank[4 * d + 3][:, :]).then_inc(G[d]["wout"], 1)

                def post_roots(b):
                    for j, t in enumerate(token_tiles(l)):
                        n = post_count(l, b) + j
                        act.wait_ge(S["post_sum"], n + 1)
                        nc.scalar.activation(post_stat[:, t, :], post_stat[:, t, :], ACT.Sqrt, bias=eps_col[:, 0:1],
                                             scale=1.0 / P).then_inc(S["post_root"], 1)
                post_roots(2)

                act.wait_ge(S["mkt_psum"], l + 1)
                nc.scalar.copy(mk_tok[:, 0:2, :].rearrange("p t c -> p (t c)"), bank[2][:, :])
                nc.scalar.copy(mk_tok[:, 2:4, :].rearrange("p t c -> p (t c)"), bank[3][:, :]).then_inc(S["mkt_out"], 1)
                for u, (d, t) in enumerate(UNITS):
                    g = 8 * l + u
                    o = sofar([len(v) for v in out_units], l) + len([v for v in out_units[l] if v <= u])
                    act.wait_ge(S["ml_rows"], g + 1)
                    nc.scalar.activation(mrow[:, 7, :], mrow[:, 4, :], ACT.Exp).then_inc(S["ml_exp"], 1)
                    act.wait_ge(S["ml_cols"], g + 1)
                    nc.scalar.copy(mcol[:, 8:10], bank[5][:, 264:266])
                    nc.scalar.activation(mcol[:, 0:8], bank[5][:, 256:264], ACT.Exp).then_inc(S["ml_ecol"], 1)
                    if u in out_units[l]:
                        act.wait_ge(S["ml_arg"], o)
                        nc.scalar.activation(work[:, 0, :], bank[2][:, :], ACT.Exp).then_inc(S["ml_decay"], 1)
                    for n in BESIDE[(l, u)]:
                        take(n)
                post_roots(1)

                steps_a = attn_units(l + 1) - attn_units(l)

                def at_exp(k):
                    g = attn_units(l) + k
                    nk = CTX if token_tiles(l)[k // 4] < 2 else TOK
                    q = g % 2
                    act.wait_ge(S["at_max"], g + 1)
                    if g >= 2:
                        act.wait_ge(S["at_w"], g - 1)
                    for m in range(2):
                        nc.scalar.activation(work[:, 4 * q + m, 0:nk], bank[2 + 4 * q + m][:, 0:nk], ACT.Exp,
                                             bias=amax[:, q, m:m + 1],
                                             accum_out=amax[:, q, 2 + m:3 + m]).then_inc(S["at_e"], 1)

                at_exp(0)
                for k in range(steps_a):
                    g = attn_units(l) + k
                    nk = CTX if token_tiles(l)[k // 4] < 2 else TOK
                    if k + 1 < steps_a:
                        at_exp(k + 1)
                    for j in range(32 // steps_a // 2 * k, 32 // steps_a // 2 * (k + 1)):
                        dense(l, "bg", [j])
                    act.wait_ge(S["at_wt"], g + 1)
                    nc.scalar.copy(work[:, 4 * (g % 2) + 3, 0:nk], bank[4][:, 0:nk]).then_inc(S["at_wtout"], 1)
                post_roots(0)

                dense(l, "bg", range(16, 24))
                dense(l, "wo")
                norm(l, 1)
                norm(l, 2)
                modulate(l, 2)
                dense(l, "ff1")
                dense(l, "ff2")
                norm(l, 3)

        @block.vector
        def _(dve):
            steps = [0]

            def link(ins):
                steps[0] += 1
                ins.then_inc(S["dve_step"], 1)
                dve.wait_ge(S["dve_step"], steps[0])

            four = lambda a: a.rearrange("p (h c) -> p h c", h=4)
            wide = lambda a, n=P: a.unsqueeze(2).broadcast_to((P, 4, n))

            def dense(l, kind, idx=None):
                for n in WHERE[(l, kind)] if idx is None else [WHERE[(l, kind)][k] for k in idx]:
                    take(n)

            def take(n):
                l, kind, i, _, bk, engine, o = SEGS[n]
                if engine != "dve":
                    return
                dve.wait_ge(S["dense_ready"], n + 1)
                ps = bank[bk]
                t0, tn = seg_tokens(l, kind)
                if kind == "adat":
                    at = B_ADA + 2 * i
                    ins = nc.vector.tensor_tensor(ada[:, l % 2, 2 * i:2 * i + 2, :],
                                                  ps[:, 0:4].rearrange("p (j a) -> p j a", a=2),
                                                  cols1[:, l, at:at + 2].unsqueeze(2).broadcast_to((P, 2, 2)), ALU.add)
                elif kind == "gate":
                    ins = nc.vector.tensor_tensor(gates[:, :, :], ps[:, 0:128].rearrange("p (t c) -> p t c", t=NT),
                                                  gate_bias[:, l, :].unsqueeze(1).broadcast_to((P, NT, 32)), ALU.add)
                elif kind == "gz":
                    dve.wait_ge(S["gz_sig"], 4 * l + i + 1)
                    ins = nc.vector.scalar_tensor_tensor(out=gz[:, i, t0:t0 + tn], in0=ps[:, 0:tn],
                                                         scalar=cols1[:, l, B_GZ + i:B_GZ + i + 1],
                                                         in1=work[:, 8 + i % 2, 0:tn], op0=ALU.add, op1=ALU.mult)
                elif kind == "mqk":
                    dst, b, f = (mq, B_MQ, 1.0) if i < 2 else (mk, B_MK, M_QK ** -0.5)
                    ins = nc.vector.tensor_scalar(dst[:, i % 2, :], ps[:, :], cols1[:, l, b + i % 2:b + i % 2 + 1], f,
                                                  ALU.add, ALU.mult)
                elif kind in ("mv", "av"):
                    c, tp = i // 2, i % 2
                    if kind == "mv" and i == 0:
                        dve.wait_ge(S["vbias_in"], 32 * (l + 1))
                        dve.wait_ge(S["conv_done"], 12 * (l + 1))
                    if kind == "mv":
                        dst = mv[:, 2 * tp:2 * tp + 2, 2 * c:2 * c + 2, 0:M_V]
                    else:
                        dst = av[:, 2 * tp:2 * tp + 2, 256 * c:256 * c + 256].rearrange("p t (h c) -> p t h c", h=2)
                    b = v_bias[:, 0 if kind == "mv" else 1, 256 * c:256 * c + 256].rearrange("p (h c) -> p h c", h=2)
                    ins = nc.vector.tensor_tensor(dst, ps[:, :].rearrange("p (t h c) -> p t h c", t=2, h=2),
                                                  b.unsqueeze(1).broadcast_to((P, 2, 2, P)), ALU.add)
                elif kind in ("aq", "ak"):
                    dst, b, f = (aq, B_AQ, A_HD ** -0.5) if kind == "aq" else (ak, B_AK, 1.0)
                    ins = nc.vector.tensor_scalar(dst[:, i, t0:t0 + tn], ps[:, 0:tn], cols1[:, l, b + i:b + i + 1], f,
                                                  ALU.add, ALU.mult)
                elif kind == "by":
                    k = WHERE[(l, "by")].index(n)
                    evacuated(dve, WHERE[(l, "bg")][k])
                    if k >= 10:
                        dve.wait_ge(S["y_ready"], 16 * l + k - 9)
                    dst = merged[:, i[1], 0:tn] if k < 8 else gated[k % 2][:, 0:tn]
                    ins = nc.vector.tensor_tensor(dst, ps[:, 0:tn], gate_sig[k % 2][:, 0:tn], ALU.mult)
                ins.then_inc(S["taken_dve"], 1)

            dve.wait_ge(S["consts_in"], 16 * 3)
            dve.wait_ge(S["params_in"], 16 * 12)
            nc.vector.tensor_copy(cm[:, :, :, :].rearrange("p a b c -> p (a b c)"), level_masks)
            nc.vector.tensor_copy(cb[:, :, :].rearrange("p a c -> p (a c)"), work[:, 8, 0:3 * P]).then_inc(S["masks_ready"], 1)
            dve.wait_ge(S["slots_set"], 2)
            dve.wait_ge(S["csig"], 1)
            nc.vector.tensor_tensor(silu_c[:, :, :].rearrange("p a k -> p (a k)"),
                                    silu_c[:, :, :].rearrange("p a k -> p (a k)"), cols1[:, 0, R_C:R_C + 16],
                                    ALU.mult).then_inc(S["silu_ready"], 1)
            lam_prod = work[:, 9, 0:DEPTH * 2 * A_HD].rearrange("p (l m c) -> p l m c", l=DEPTH, m=2)
            for l in range(DEPTH):
                for m in range(2):
                    link(nc.vector.tensor_tensor(lam_prod[:, l, m, :], lamv[:, l, 2 * m, :], lamv[:, l, 2 * m + 1, :], ALU.mult))
            nc.vector.tensor_reduce(lam2[:, :, :], lam_prod, op=ALU.add, axis=AX_X).then_inc(S["lam_sum"], 1)
            dve.wait_ge(S["lam_exp"], 1)
            for l in range(DEPTH):
                lam_init = 0.8 - 0.6 * math.exp(-0.3 * l)
                link(nc.vector.tensor_tensor(nlam[:, l:l + 1], lam2[:, l, 1:2], lam2[:, l, 0:1], ALU.subtract))
                link(nc.vector.tensor_scalar(nlam[:, l:l + 1], nlam[:, l:l + 1], -lam_init, None, ALU.add))
            nc.vector.memset(coef[:, 0:8], -1.0)

            def root_to_rstd(l, which):
                t0, n = (0, TOK) if which == 0 else tokens(l)
                dve.wait_ge(S["norm_root"], norm_count(l, which) + 1)
                link(nc.vector.reciprocal(rstd[:, 0:n], rstd[:, 0:n]))

            def normed(l, which):
                t0, n = (0, TOK) if which == 0 else tokens(l)
                root_to_rstd(l, which)
                for k in range(KD):
                    nc.vector.tensor_tensor(work[:, k, 0:n], xt[:, k, t0:t0 + n], rstd[:, 0:n], ALU.mult)\
                        .then_inc(S["scaled_ready"], 1)

            def residual(l, which):
                t0, n = tokens(l)
                root_to_rstd(l, which)
                ot = ot_of[which]
                for k in range(KD):
                    for a in range(0, n, CTX):
                        cond = 1 if a + t0 < CTX else 0
                        link(nc.vector.scalar_tensor_tensor(out=ot[:, k, a:a + CTX], in0=ot[:, k, a:a + CTX],
                                                            scalar=out_gate[:, which // 2, k, cond:cond + 1],
                                                            in1=rstd[:, a:a + CTX], op0=ALU.mult, op1=ALU.mult))
                    nc.vector.tensor_tensor(xt[:, k, t0:t0 + n], xt[:, k, t0:t0 + n], ot[:, k, 0:n], ALU.add)\
                        .then_inc(S["res_ready"], 1)
                dve.wait_ge(S["res_ready"], KD * (2 * l + which // 2 + 1))

            for l in range(DEPTH):
                if l == 0:
                    dense(l, "adat")
                evacuated(dve, seg_of(l, "adat"))
                for s in range(2):
                    gain = lambda r: cols2[:, l, R_GAIN + 8 * r:R_GAIN + 8 * r + 8].unsqueeze(2).broadcast_to((P, KD, 2))
                    link(nc.vector.tensor_scalar(mod_scale[:, s, :, :], ada[:, l % 2, 24 * s + 8:24 * s + 16, :], 1.0, None, ALU.add))
                    link(nc.vector.tensor_tensor(mod_scale[:, s, :, :], mod_scale[:, s, :, :], gain(2 * s), ALU.mult))
                    ins = nc.vector.tensor_tensor(out_gate[:, s, :, :], ada[:, l % 2, 24 * s + 16:24 * s + 24, :], gain(2 * s + 1), ALU.mult)
                ins.then_inc(S["ada_ready"], 1)
                normed(l, 0)

                dense(l, "gate")
                evacuated(dve, seg_of(l, "gate"))
                two = lambda a: a.unsqueeze(1).broadcast_to((P, NT, a.shape[1]))
                for d in range(2):
                    link(nc.vector.scalar_tensor_tensor(out=zgate[:, :, 4 * d:4 * d + 4], in0=gates[:, :, 8 * d + 4:8 * d + 8],
                                                        scalar=-1.0, in1=two(fdt_bias[:, l, 4 * d:4 * d + 4]),
                                                        op0=ALU.mult, op1=ALU.subtract))
                link(nc.vector.tensor_tensor(zgate[:, :, 8:16], gates[:, :, 16:24], two(fdt_bias[:, l, 8:16]), ALU.add))
                nc.vector.scalar_tensor_tensor(out=egate[:, :, :], in0=zgate[:, :, :], scalar=-1.0, in1=zgate[:, :, :],
                                               op0=ALU.mult, op1=ALU.max).then_inc(S["gates_z"], 1)
                dve.wait_ge(S["gates_exp"], l + 1)
                link(nc.vector.tensor_scalar(coef[:, 8:16], coef[:, 8:16], -1.0, None, ALU.mult))
                link(nc.vector.scalar_tensor_tensor(out=lgate[:, :, :], in0=zgate[:, :, :], scalar=0.0, in1=egate[:, :, :],
                                                    op0=ALU.max, op1=ALU.add))
                link(nc.vector.tensor_tensor(lgate[:, :, :], lgate[:, :, :], two(coef[:, :]), ALU.mult))
                link(nc.vector.tensor_scalar(beta[:, :, :], beta[:, :, :], 1.0, None, ALU.add))
                link(nc.vector.reciprocal(beta[:, :, :], beta[:, :, :]))
                nc.vector.tensor_scalar(nbeta[:, :, :], beta[:, :, :], -1.0, None, ALU.mult).then_inc(S["gates_ready"], 1)
                dve.wait_ge(S["gates_ready"], l + 1)

                def conv(j):
                    t0, n = seg_tokens(l, "gq" if j < 4 else "gk")
                    s0, sn = t0 // CTX, n // CTX
                    seg = seg_of(l, ("gq", "gk", "gv")[j // 4], j % 4)
                    evacuated(dve, seg)
                    if j == 0:
                        dve.wait_ge(S["h_ready"], 2 * KD * l + KD)
                    if j >= 2:
                        dve.wait_ge(S["conv_out"], 12 * l + j - 1)
                    acc = work[:, j % 2, 0:n].rearrange("p (s c) -> p s c", s=sn)
                    tap = lambda k: cols2[:, l, R_CONV + 12 * k + j:R_CONV + 12 * k + j + 1]
                    src = lambda k: raw[:, j % 3, s0:s0 + sn, k:k + CTX]
                    link(nc.vector.tensor_scalar(acc, src(0), tap(0), None, ALU.mult))
                    for k in range(1, CONV_K):
                        ins = nc.vector.scalar_tensor_tensor(out=acc, in0=src(k), scalar=tap(k), in1=acc,
                                                             op0=ALU.mult, op1=ALU.add)
                        if k < CONV_K - 1:
                            link(ins)
                    ins.then_inc(S["conv_done"], 1)

                def conv_silu(j):
                    t0, n = seg_tokens(l, "gq" if j < 4 else "gk")
                    dve.wait_ge(S["conv_sig"], 12 * l + j + 1)
                    dst = (gq[:, j % 4, t0:t0 + n], gk[:, j % 4, t0:t0 + n], work[:, 4 + j % 4, 0:n])[j // 4]
                    nc.vector.tensor_tensor(dst, work[:, j % 2, 0:n], work[:, 2 + j % 2, 0:n], ALU.mult)\
                        .then_inc(S["conv_out"], 1)

                def l2_scale(j):
                    t0, n = seg_tokens(l, "gq" if j < 4 else "gk")
                    dst = (gq if j < 4 else gk)[:, j % 4, t0:t0 + n]
                    r = work[:, 12 + j % 2, 0:n]
                    dve.wait_ge(S["l2_root"], 8 * l + j + 1)
                    link(nc.vector.reciprocal(r, r))
                    nc.vector.scalar_tensor_tensor(out=dst, in0=dst, scalar=G_HD ** -0.5 if j < 4 else 1.0, in1=r,
                                                   op0=ALU.mult, op1=ALU.mult).then_inc(S["l2_out"], 1)

                for j in range(12):
                    conv(j)
                    if j >= 1:
                        conv_silu(j - 1)
                    if j >= 4:
                        l2_scale(j - 4)
                conv_silu(11)
                dense(l, "gz")

                for p in range(4):
                    g = 4 * l + p
                    o = gd_outs(l, p)
                    for d in range(2):
                        small = bank[4 * d + 3]
                        dve.wait_ge(G[d]["rows"], g + 1)
                        link(nc.vector.tensor_copy(gcol[d][:, 0:4], small[:, 128:132]))
                        nc.vector.tensor_copy(gcol[d][:, 8:12], small[:, 132:136])
                        nc.vector.tensor_tensor(gcol[d][:, 4:8], small[:, 132:136], gcol[d][:, 0:4], ALU.subtract)\
                            .then_inc(G[d]["cols"], 1)
                    for d in range(2):
                        dve.wait_ge(G[d]["ecol"], g + 1)
                        nc.vector.tensor_scalar(gecol[d][:, 12:16], gecol[d][:, 0:4], -1.0, None, ALU.mult)\
                            .then_inc(G[d]["neg"], 1)
                    for d in range(2):
                        t = CHUNK_OF[d][p]
                        dve.wait_ge(G[d]["decay"], g + 1)
                        dve.wait_ge(G[d]["qk"], g + 1)
                        for h in range(HEADS):
                            hs = slice(h * P, (h + 1) * P)
                            ins = nc.vector.scalar_tensor_tensor(out=slot(d, 1)[:, hs], in0=bank[4 * d + 1][:, hs],
                                                                 scalar=nbeta[:, t, 4 * d + h:4 * d + h + 1],
                                                                 in1=slot(d, 0)[:, hs], op0=ALU.mult, op1=ALU.mult)
                        ins.then_inc(G[d]["b"], 1)
                    for d in range(2):
                        dve.wait_ge(G[d]["eye"], g + 1)
                        dve.wait_ge(G[d]["b"], g + 1)
                        nc.vector.copy_predicated(four(slot(d, 3)), cm[:, d, 0, :].unsqueeze(1).broadcast_to((P, HEADS, P)),
                                                  four(slot(d, 1))).then_inc(G[d]["u0"], 1)
                    if gd_gives(l, p):
                        for d in range(2):
                            nc.vector.tensor_tensor(slot(d, 2), bank[4 * d + 2][:, :], slot(d, 0), ALU.mult)\
                                .then_inc(G[d]["qkd"], 1)
                    if gd_gives(l, p):
                        for d in range(2):
                            t = CHUNK_OF[d][p]
                            dve.wait_ge(G[d]["qb"], o)
                            nc.vector.tensor_tensor(four(slot(d, 8)), gq[:, :, t * P:(t + 1) * P],
                                                    four(bank[4 * d + 2][:, :]), ALU.mult).then_inc(G[d]["qg"], 1)
                    for d in range(2):
                        dve.wait_ge(G[d]["t1"], g + 1)
                    for lv in range(1, LEVELS):
                        k = (LEVELS - 1) * g + lv
                        for n in completed(IN_GAP[(l, p, 2 * lv - 2)]):
                            take(n)
                        for d in range(2):
                            mask = lambda side, q: cm[:, side, lv, :].rearrange(
                                "p (b q s) -> p b q s", q=2, s=2 ** lv)[:, :, q, :].unsqueeze(1)\
                                .broadcast_to((P, HEADS, P >> (lv + 1), 2 ** lv))
                            if lv < LEVELS - 1:
                                dve.wait_ge(G[d]["t"], (LEVELS - 2) * g + lv)
                                nc.vector.copy_predicated(parity(slot(d, 4), lv, d), mask(1 - d, d),
                                                          compact(bank[4 * d + 3][:, 0:256], lv)).then_inc(G[d]["tout"], 1)
                            dve.wait_ge(G[d]["u"], k)
                            nc.vector.copy_predicated(parity(slot(d, 3), lv, 1 - d), mask(d, 1 - d),
                                                      compact(bank[4 * d + 1][:, 0:256], lv)).then_inc(G[d]["uout"], 1)
                        for n in completed(IN_GAP[(l, p, 2 * lv - 1)]):
                            take(n)
                    for d in range(2):
                        t = CHUNK_OF[d][p]
                        dve.wait_ge(G[d]["v"], g + 1)
                        nc.vector.tensor_tensor(four(slot(d, 5)), four(bank[4 * d][:, :]), wide(beta[:, t, 4 * d:4 * d + 4]),
                                                ALU.mult).then_inc(G[d]["vn"], 1)
                    for d in range(2):
                        t = CHUNK_OF[d][p]
                        if gd_gives(l, p):
                            dve.wait_ge(G[d]["o"], o)
                            if p % 2 == 0:
                                ins = nc.vector.tensor_copy(oacc[:, t, :], bank[4 * d + 2][:, :])
                            else:
                                dve.wait_ge(G[1 - d]["oacc"], o - 1)
                                ins = nc.vector.tensor_tensor(oacc[:, t, :], bank[4 * d + 2][:, :], oacc[:, t, :], ALU.add)
                            ins.then_inc(G[d]["oacc"], 1)
                        dve.wait_ge(G[d]["s"], g + 1)
                        for h in range(HEADS):
                            ins = nc.vector.scalar_tensor_tensor(out=gstate[:, d, h, :], in0=gstate[:, d, h, :],
                                                                 scalar=gecol[d][:, 8 + h:9 + h],
                                                                 in1=bank[4 * d][:, h * P:(h + 1) * P],
                                                                 op0=ALU.mult, op1=ALU.add)
                        ins.then_inc(G[d]["state"], 1)
                        dve.wait_ge(G[d]["state"], g + 1)
                for d in range(2):
                    dve.wait_ge(G[d]["oacc"], gd_outs(l, 3))

                def post(b):
                    tiles = token_tiles(l)
                    for j, t in enumerate(tiles):
                        dve.wait_ge(S["post_sq"], post_count(l, b) + j + 1)
                        nc.vector.tensor_reduce(post_stat[:, t, :], four(work[:, 8 + j % 2, :]), op=ALU.add, axis=AX_X)\
                            .then_inc(S["post_sum"], 1)
                    for j, t in enumerate(tiles):
                        n = post_count(l, b) + j
                        dve.wait_ge(S["post_root"], n + 1)
                        link(nc.vector.reciprocal(post_stat[:, t, :], post_stat[:, t, :]))
                        nc.vector.tensor_tensor(four(oacc[:, t, :]), four(oacc[:, t, :]), wide(post_stat[:, t, :]), ALU.mult)\
                            .then_inc(S["post_norm"], 1)
                    for j, t in enumerate(tiles):
                        n = post_count(l, b) + j
                        dve.wait_ge(S["post_tr"], n + 1)
                        ps = bank[6 + j % 2]
                        ts = slice(t * P, (t + 1) * P)
                        if b == 2:
                            ins = nc.vector.scalar_tensor_tensor(out=gz[:, :, ts], in0=four(ps[:, :]),
                                                                 scalar=cols2[:, l, R_GN:R_GN + 1], in1=gz[:, :, ts],
                                                                 op0=ALU.mult, op1=ALU.mult)
                        elif b == 1:
                            for h in range(HEADS):
                                ins = nc.vector.scalar_tensor_tensor(out=mo[:, h, ts], in0=ps[:, h * P:(h + 1) * P],
                                                                     scalar=cols2[:, l, R_MN + h:R_MN + h + 1],
                                                                     in1=mo[:, h, ts], op0=ALU.mult, op1=ALU.mult)
                        else:
                            lam_init = 0.8 - 0.6 * math.exp(-0.3 * l)
                            ins = nc.vector.tensor_scalar(aq[:, :, ts], four(ps[:, :]), cols2[:, l, R_AN:R_AN + 1],
                                                          1.0 - lam_init, ALU.mult, ALU.mult)
                        ins.then_inc(S["post_out"], 1)
                post(2)

                link(nc.vector.memset(mstate, 0.0))
                for u, (d, t) in enumerate(UNITS):
                    g = 8 * l + u
                    gives = u in out_units[l]
                    o = sofar([len(v) for v in out_units], l) + len([v for v in out_units[l] if v <= u])
                    end = P - 1 if d == 0 else 0
                    R = lambda r: mrow[:, r, :]
                    fwd = lambda a: a if d == 0 else a[:, ::-1]
                    dve.wait_ge(S["ml_small"], g + 1)
                    if g > 0:
                        dve.wait_ge(S["ml_c"], g)
                    if l > 0 and u == 0:
                        dve.wait_ge(S["states_zero"], 2 * l + 2)
                    link(nc.vector.tensor_copy(R(0), bank[5][0:4, 128:256]))
                    link(nc.vector.tensor_tensor(R(1), bank[5][0:4, 0:128], R(0), ALU.subtract))
                    link(nc.vector.tensor_tensor_scan(fwd(R(2)), fwd(R(1)), fwd(R(1)), mmax[:, d:d + 1], ALU.max, ALU.max))
                    nc.vector.tensor_scalar(R(3), R(2), -1.0, None, ALU.mult)
                    nc.vector.tensor_scalar(R(4), R(2), -1.0, mmax[:, d:d + 1], ALU.mult, ALU.add)
                    link(nc.vector.scalar_tensor_tensor(out=R(5), in0=R(2), scalar=-1.0, in1=R(0), op0=ALU.mult, op1=ALU.subtract))
                    link(nc.vector.tensor_tensor(mmax[:, d:d + 1], R(0)[:, end:end + 1], R(2)[:, end:end + 1], ALU.add))
                    nc.vector.tensor_scalar(R(6), R(1), R(2)[:, end:end + 1], None, ALU.subtract).then_inc(S["ml_rows"], 1)
                    dve.wait_ge(S["ml_ecol"], g + 1)
                    if u == 0:
                        dve.wait_ge(S["mkt_out"], l + 1)
                    keys = mk_tok[:, t, :].rearrange("p (h c) -> p h c", h=4)
                    kw = work[:, 3, 0:256].rearrange("p (h c) -> p h c", h=4)
                    nc.vector.tensor_tensor(kw, keys, wide(mcol[:, 4:8], M_QK), ALU.mult).then_inc(S["ml_kw"], 1)
                    if gives:
                        dve.wait_ge(S["ml_qb"], o)
                        nc.vector.tensor_tensor(work[:, 2, 0:256].rearrange("p (i c) -> p i c", i=2),
                                                mq[:, :, t * P:(t + 1) * P],
                                                bank[7][:, 0:256].rearrange("p (i c) -> p i c", i=2), ALU.mult)\
                            .then_inc(S["ml_qg"], 1)
                        dve.wait_ge(S["ml_decay"], o)
                        dve.wait_ge(S["ml_qk"], o)
                        nc.vector.tensor_tensor(work[:, 1, 0:256], bank[3][:, 0:256], work[:, 0, 0:256], ALU.mult)
                        nc.vector.tensor_tensor(work[:, 1, 256:512], bank[6][:, 0:256], work[:, 0, 256:512], ALU.mult)\
                            .then_inc(S["ml_p"], 1)
                    for n in BESIDE[(l, u)]:
                        take(n)
                    if gives:
                        dve.wait_ge(S["ml_num"], o)
                        num = [bank[4 + 2 * i][:, 0:258].rearrange("p (h c) -> p h c", h=2) for i in range(2)]
                        nc.vector.tensor_copy(mden[:, 0:2], num[0][:, :, M_V])
                        link(nc.vector.tensor_copy(mden[:, 2:4], num[1][:, :, M_V]))
                        link(nc.vector.scalar_tensor_tensor(out=mden[:, 4:8], in0=mden[:, 0:4], scalar=-1.0, in1=mden[:, 0:4],
                                                            op0=ALU.mult, op1=ALU.max))
                        link(nc.vector.tensor_tensor(mden[:, 4:8], mden[:, 4:8], mcol[:, 0:4], ALU.max))
                        link(nc.vector.reciprocal(mden[:, 4:8], mden[:, 4:8]))
                        for i in range(2):
                            r = mden[:, 4 + 2 * i:6 + 2 * i].unsqueeze(2).broadcast_to((P, 2, P))
                            acc = oacc[:, t, :].rearrange("p (k r c) -> p r k c", k=2, r=2)[:, i]
                            if u in FIRST_VISIT:
                                ins = nc.vector.tensor_tensor(acc, num[i][:, :, 0:M_V], r, ALU.mult)
                            else:
                                tmp = work[:, 4, 256 * i:256 * i + 256].rearrange("p (h c) -> p h c", h=2)
                                link(nc.vector.tensor_tensor(tmp, num[i][:, :, 0:M_V], r, ALU.mult))
                                ins = nc.vector.tensor_tensor(acc, acc, tmp, ALU.add)
                            ins.then_inc(S["ml_h"], 1)
                    dve.wait_ge(S["ml_c"], g + 1)
                    for i in range(2):
                        ins = nc.vector.scalar_tensor_tensor(out=mstate[:, d, i, :], in0=mstate[:, d, i, :],
                                                             scalar=mcol[:, 8 + i:9 + i],
                                                             in1=mlstm_c(i),
                                                             op0=ALU.mult, op1=ALU.add)
                    ins.then_inc(S["ml_state"], 1)
                    if gives:
                        dve.wait_ge(S["ml_h"], 2 * o)
                    dve.wait_ge(S["ml_state"], g + 1)
                post(1)

                for j in range(8):
                    dst = (aq if j < 4 else ak)[:, j % 4, CTX:TOK]
                    n = 8 * l + j
                    dve.wait_ge(S["rope_psum"], n + 1)
                    link(nc.vector.tensor_tensor(dst, dst, cos_t, ALU.mult))
                    link(nc.vector.tensor_tensor(work[:, 4, 0:256], bank[4 + j % 2][:, 0:256], sin_t, ALU.mult))
                    nc.vector.tensor_tensor(dst, dst, work[:, 4, 0:256], ALU.add).then_inc(S["rope_out"], 1)

                steps_a = attn_units(l + 1) - attn_units(l)

                def at_max(k):
                    g = attn_units(l) + k
                    nk = CTX if token_tiles(l)[k // 4] < 2 else TOK
                    q = g % 2
                    dve.wait_ge(S["at_s"], g + 1)
                    for m in range(2):
                        ins = nc.vector.tensor_reduce(amax[:, q, m:m + 1], bank[2 + 4 * q + m][:, 0:nk], op=ALU.max,
                                                      axis=AX_X, negate=True)
                    ins.then_inc(S["at_max"], 1)

                def at_take(k):
                    g = attn_units(l) + k
                    t, h = token_tiles(l)[k // 4], k % 4
                    dve.wait_ge(S["at_o"], g + 1)
                    nc.vector.tensor_copy(oacc[:, t, h * P:(h + 1) * P], bank[5][:, 0:P]).then_inc(S["at_oout"], 1)

                at_max(0)
                for k in range(steps_a):
                    g = attn_units(l) + k
                    nk = CTX if token_tiles(l)[k // 4] < 2 else TOK
                    q = g % 2
                    st = amax[:, q, :]
                    e0, e1, w = work[:, 4 * q, 0:nk], work[:, 4 * q + 1, 0:nk], work[:, 4 * q + 2, 0:nk]
                    if k + 1 < steps_a:
                        at_max(k + 1)
                    dve.wait_ge(S["at_e"], 2 * g + 2)
                    link(nc.vector.reciprocal(st[:, 4:6], st[:, 2:4]))
                    link(nc.vector.tensor_tensor(st[:, 6:7], st[:, 5:6], nlam[:, l:l + 1], ALU.mult))
                    link(nc.vector.tensor_scalar(e1, e1, st[:, 6:7], None, ALU.mult))
                    if g >= 2:
                        dve.wait_ge(S["at_wt"], g - 1)
                    nc.vector.scalar_tensor_tensor(out=w, in0=e0, scalar=st[:, 4:5], in1=e1,
                                                   op0=ALU.mult, op1=ALU.add).then_inc(S["at_w"], 1)
                    for j in range(32 // steps_a // 2 * k, 32 // steps_a // 2 * (k + 1)):
                        dense(l, "by", [j])
                    at_take(k)
                dve.wait_ge(S["at_oout"], attn_units(l + 1))
                post(0)

                dense(l, "by", range(16, 24))
                residual(l, 1)
                normed(l, 2)
                residual(l, 3)

            for t in range(2):
                for hf in range(2):
                    n = 2 * t + hf
                    dve.wait_ge(S["final_psum"], n + 1)
                    nc.vector.tensor_copy(work[:, n, :], bank[2 + n][:, :]).then_inc(S["final_out"], 1)

        @block.tensor
        def _(pe):
            mm = nc.tensor.matmul

            def chunk_arrived(n):
                pe.wait_ge(S[f"chunk_in{n % RING}"], 16 * (n // RING + 1))

            def bank_free(n):
                for m in range(n - 1, -1, -1):
                    if SEGS[m][4] == SEGS[n][4]:
                        if SEGS[m][5] is not None:
                            evacuated(pe, m)
                        return

            def dense(l, kind, idx=None):
                for n in WHERE[(l, kind)] if idx is None else [WHERE[(l, kind)][k] for k in idx]:
                    segment(n)

            def segment(n, start=0, end=4):
                l, kind, i, ch, bk, engine, _ = SEGS[n]
                ps = bank[bk]
                t0, tn = seg_tokens(l, kind)
                if start == 0:
                    bank_free(n)
                if ch is not None:
                    chunk_arrived(ch)
                    k_of = 4 if kind == "by" else 8
                    w = ring[:, ch % RING, :].rearrange("p (k n) -> p k n", k=k_of)
                if kind == "ada":
                    for k in range(2 * start, 2 * end):
                        last = mm(ps[0:2, 0:256], silu_c[:, :, k], w[:, k, :], start=k == 0, stop=k == KD - 1)
                elif kind == "adat":
                    evacuated(pe, seg_of(l, "ada", i))
                    for q in range(2):
                        last = mm(ps[:, 2 * q:2 * q + 2], ada_rows[:, i % 2, q * P:(q + 1) * P], ident[0:2, 0:2],
                                  start=True, stop=True)
                elif kind == "gate":
                    pe.wait_ge(S["gatew_in"], 32 * (l + 1))
                    for t in range(NT):
                        for k in range(KD):
                            last = mm(ps[:, 32 * t:32 * t + 32], ht[:, k, t * P:(t + 1) * P], w_gates[:, k, :],
                                      start=k == 0, stop=k == KD - 1)
                elif kind in ("mv", "av"):
                    for a in range(2):
                        t = 2 * (i % 2) + a
                        for k in range(KD):
                            if not 4 * start <= a * KD + k < 4 * end:
                                continue
                            last = mm(ps[:, a * 256:(a + 1) * 256], ht[:, k, t * P:(t + 1) * P], w[:, k, :],
                                      start=k == 0, stop=k == KD - 1)
                elif kind in ("gq", "gk", "gv", "gz", "mqk", "mo", "aq", "ak", "bg", "ff1"):
                    q = (i[1] if kind == "bg" else i) % 2
                    for k in range(2 * start, 2 * end):
                        last = mm(ps[:, 0:tn], w[:, k, q * P:(q + 1) * P], ht[:, k, t0:t0 + tn],
                                  start=k == 0, stop=k == KD - 1)
                elif kind == "by":
                    b, cc = i
                    y = {2: gz, 1: mo, 0: aq}[b]
                    pe.wait_ge(S["post_out"], post_count(l, b) + len(token_tiles(l)))
                    for k in range(4):
                        last = mm(ps[:, 0:tn], w[:, k, (cc % 4) * P:(cc % 4 + 1) * P], y[:, k, t0:t0 + tn],
                                  start=k == 0, stop=k == 3)
                elif kind == "wo":
                    q = i % 2
                    pe.wait_ge(S["y_ready"], 16 * (l + 1))
                    for k in range(KD):
                        last = mm(ps[:, 0:tn], w[:, k, q * P:(q + 1) * P], merged[:, k, 0:tn],
                                  start=k == 0, stop=k == KD - 1)
                elif kind == "ff2":
                    nb, kc, q = i
                    pe.wait_ge(S["hid_ready"], FT * l + 8 * kc + 8)
                    for k in range(KD):
                        last = mm(ps[:, 0:tn], w[:, k, q * P:(q + 1) * P], hidden[:, 8 * kc + k, 0:tn],
                                  start=kc == 0 and k == 0, stop=kc == 3 and k == KD - 1)
                if end == 4:
                    last.then_inc(S["dense_ready"], 1)

            pe.wait_ge(S["consts_in"], 16 * 3)
            pe.wait_ge(S["rows_in"], 16 * 22)
            for l in range(DEPTH):
                nc.tensor.transpose(bank[2 + 2 * l][:, 0:P], rows1[:, l, :], ident).then_inc(S["cols_psum"], 1)
                nc.tensor.transpose(bank[3 + 2 * l][:, 0:98], rows2[0:98, l, :], ident[0:98, 0:98]).then_inc(S["cols_psum"], 1)
            pe.wait_ge(S["x_in"], 32)
            pe.wait_ge(S["cols_ready"], 4)
            x_tok = ht[:, :, :].rearrange("p (t a) c -> p t (a c)", t=NT)
            for k in range(KD):
                if k >= 4:
                    pe.wait_ge(S["xtr_ready"], k - 3)
                for t in range(NT):
                    last = nc.tensor.transpose(bank[4 + k % 4][:, t * P:(t + 1) * P], x_tok[:, t, k * P:(k + 1) * P], ident)
                last.then_inc(S["xtr_psum"], 1)
            pe.wait_ge(S["xtr_ready"], KD)
            pe.wait_ge(S["masks_ready"], 1)
            pe.wait_ge(S["silu_ready"], 1)
            pe.wait_ge(S["ones_set"], 1)

            def norm(l, which):
                t0, n = (0, TOK) if which == 0 else tokens(l)
                q = norm_count(l, which)
                for k in range(KD):
                    pe.wait_ge(S["sq_ready"], KD * q + k + 1)
                    mm(bank[7][:, 0:n], ones[:, :], work[:, 8 + k % 2, 0:n], start=k == 0, stop=k == KD - 1)\
                        .then_inc(S["sq_used"], 1)

            for l in range(DEPTH):
                if l == 0:
                    for n in range(WHERE[(0, "gate")][0]):
                        segment(n)
                norm(l, 0)
                pe.wait_ge(S["h_ready"], 2 * KD * l + KD)
                dense(l, "gate")
                def l2_sum(j):
                    n = seg_tokens(l, "gq" if j < 4 else "gk")[1]
                    pe.wait_ge(S["l2_sq"], 8 * l + j + 1)
                    if j >= 2:
                        pe.wait_ge(S["l2_root"], 8 * l + j - 1)
                    mm(bank[6 + j % 2][:, 0:n], ones[:, :], work[:, 10 + j % 2, 0:n], start=True, stop=True).then_inc(S["l2_sum"], 1)

                for j in range(12):
                    dense(l, ("gq", "gk", "gv")[j // 4], [j % 4])
                    if 3 <= j < 11:
                        l2_sum(j - 3)
                for h in range(4):
                    dense(l, "gz", [h])
                    pe.wait_ge(S["conv_out"], 12 * l + 9 + h)
                    if h >= 2:
                        pe.wait_ge(S["vt_out"], 4 * l + h - 1)
                    for t in range(NT):
                        last = nc.tensor.transpose(bank[4 + h % 2][:, t * P:(t + 1) * P], work[:, 4 + h, t * P:(t + 1) * P], ident)
                    last.then_inc(S["vt_psum"], 1)
                    pe.wait_ge(S["l2_out"], 8 * l + 5 + h)
                    if h >= 2:
                        pe.wait_ge(S["kt_out"], 4 * l + h - 1)
                    for t in range(NT):
                        last = nc.tensor.transpose(bank[2 + h % 2][:, t * P:(t + 1) * P], gk[:, h, t * P:(t + 1) * P], ident)
                    last.then_inc(S["kt_psum"], 1)
                pe.wait_ge(S["kt_out"], 4 * l + 4)
                pe.wait_ge(S["vt_out"], 4 * l + 4)
                pe.wait_ge(S["gates_ready"], l + 1)
                pe.wait_ge(S["states_zero"], 2 * l + 2)
                pe.wait_ge(S["slots_set"], 2)
                evacuated(pe, seg_of(l, "gz", 2))
                evacuated(pe, seg_of(l, "gz", 3))

                H = lambda h: slice(h * P, (h + 1) * P)
                C = lambda h: slice(h * 64, (h + 1) * 64)
                half = lambda a, lv, q: a.rearrange("p (b q s) -> p b q s", q=2, s=2 ** lv)[:, :, q, :]
                for p in range(4):
                    g = 4 * l + p
                    o = gd_outs(l, p)
                    gives = gd_gives(l, p)
                    for d in range(2):
                        t = CHUNK_OF[d][p]
                        ts = slice(t * P, (t + 1) * P)
                        log_g = lgate[:, t, 8 + 4 * d:12 + 4 * d]
                        small = bank[4 * d + 3]
                        mm(small[0:4, 0:P], log_g, tri[d], start=True, stop=True)
                        mm(small[:, 128:132], tri[d], log_g, start=True, stop=True)
                        mm(small[:, 132:136], ones[:, :], log_g, start=True, stop=True).then_inc(G[d]["small"], 1)
                        for h in range(HEADS):
                            last = mm(bank[4 * d + 1][:, H(h)], gk[:, h, ts], gk[:, h, ts], start=True, stop=True)
                        if gives:
                            if o > 1:
                                pe.wait_ge(G[d]["oacc"], o - 1)
                            for h in range(HEADS):
                                last = mm(bank[4 * d + 2][:, H(h)], gk[:, h, ts], gq[:, h, ts], start=True, stop=True)
                        last.then_inc(G[d]["qk"], 1)
                    for d in range(2):
                        pe.wait_ge(G[d]["rows"], g + 1)
                        if g > 0:
                            pe.wait_ge(G[d]["state"], g)
                        mm(bank[4 * d][:, :], ident_b, mask_b[d], start=True, stop=False)
                        for h in range(HEADS):
                            mm(bank[4 * d][:, H(h)], sel[h], grow[d][:, 0, :], start=False, stop=False)
                            last = mm(bank[4 * d][:, H(h)], grow[d][:, 2, :], sel[h], start=False, stop=h == HEADS - 1)
                        last.then_inc(G[d]["arg"], 1)
                    for d in range(2):
                        pe.wait_ge(G[d]["u0"], g + 1)
                        pe.wait_ge(G[d]["cols"], g + 1)
                        for h in range(HEADS):
                            last = nc.tensor.transpose(bank[4 * d + 3][:, H(h)], slot(d, 3)[:, H(h)], ident)
                        last.then_inc(G[d]["t0"], 1)
                    if gives:
                        for d in range(2):
                            pe.wait_ge(G[d]["qkd"], o)
                            for h in range(HEADS):
                                last = mm(bank[4 * d + 2][:, H(h)], sel[h], grow[d][:, 1, :], start=True, stop=True)
                            last.then_inc(G[d]["qb"], 1)
                    for lv in range(1, LEVELS):
                        k = (LEVELS - 1) * g + lv
                        kt = (LEVELS - 2) * g + lv
                        for d in range(2):
                            if lv == 1:
                                pe.wait_ge(G[d]["t1"], g + 1)
                                pe.wait_ge(G[d]["decay"], g + 1)
                                pe.wait_ge(G[d]["b"], g + 1)
                            else:
                                pe.wait_ge(G[d]["tout"], kt - 1)
                            for h in range(HEADS):
                                last = mm(bank[4 * d][:, C(h)], slot(d, 1)[:, H(h)], half(slot(d, 4)[:, H(h)], lv, d),
                                          start=True, stop=True)
                            last.then_inc(G[d]["m"], 1)
                        if lv == 1 and gives:
                            for d in range(2):
                                pe.wait_ge(G[d]["qg"], o)
                        for n, start, end in IN_GAP[(l, p, 2 * lv - 2)]:
                            segment(n, start, end)
                        for d in range(2):
                            pe.wait_ge(G[d]["mout"], k)
                            if lv > 1:
                                pe.wait_ge(G[d]["uout"], k - 1)
                            if lv < LEVELS - 1:
                                for h in range(HEADS):
                                    last = mm(bank[4 * d + 3][:, C(h)], slot(d, 3)[:, H(h)], half(slot(d, 5)[:, H(h)], lv, d),
                                              start=True, stop=True)
                                last.then_inc(G[d]["t"], 1)
                            for h in range(HEADS):
                                last = mm(bank[4 * d + 1][:, C(h)], slot(d, 5)[:, H(h)], half(slot(d, 3)[:, H(h)], lv, 1 - d),
                                          start=True, stop=True)
                            last.then_inc(G[d]["u"], 1)
                        for n, start, end in IN_GAP[(l, p, 2 * lv - 1)]:
                            segment(n, start, end)
                    for bk in (2, 6):
                        evacuated(pe, [n for x in range(GAPS) for n in completed(IN_GAP[(l, p, x)]) if SEGS[n][4] == bk][-1])
                    for d in range(2):
                        pe.wait_ge(G[d]["uout"], (LEVELS - 1) * (g + 1))
                        pe.wait_ge(G[d]["ke"], 2 * g + 2)
                        for h in range(HEADS):
                            last = mm(bank[4 * d + 3][:, H(h)], slot(d, 6)[:, H(h)], slot(d, 3)[:, H(h)], start=True, stop=True)
                        last.then_inc(G[d]["w"], 1)
                    for d in range(2):
                        t = CHUNK_OF[d][p]
                        pe.wait_ge(G[d]["wout"], g + 1)
                        for h in range(HEADS):
                            mm(bank[4 * d][:, H(h)], slot(d, 3)[:, H(h)], gv_tok[:, t, H(h)], start=True, stop=False)
                            last = mm(bank[4 * d][:, H(h)], slot(d, 4)[:, H(h)], gstate[:, d, h, :], start=False, stop=True)
                        last.then_inc(G[d]["v"], 1)
                    for d in range(2):
                        pe.wait_ge(G[d]["vn"], g + 1)
                        if gives:
                            pe.wait_ge(G[d]["qg"], o)
                            for h in range(HEADS):
                                mm(bank[4 * d + 2][:, H(h)], slot(d, 2)[:, H(h)], slot(d, 5)[:, H(h)], start=True, stop=False)
                                last = mm(bank[4 * d + 2][:, H(h)], slot(d, 8)[:, H(h)], gstate[:, d, h, :],
                                          start=False, stop=True)
                            last.then_inc(G[d]["o"], 1)
                        for h in range(HEADS):
                            last = mm(bank[4 * d][:, H(h)], slot(d, 7)[:, H(h)], slot(d, 5)[:, H(h)], start=True, stop=True)
                        last.then_inc(G[d]["s"], 1)
                for d in range(2):
                    pe.wait_ge(G[d]["state"], 4 * (l + 1))
                    pe.wait_ge(G[d]["oacc"], gd_outs(l, 3))

                def post(b):
                    for j, t in enumerate(token_tiles(l)):
                        n = post_count(l, b) + j
                        pe.wait_ge(S["post_norm"], n + 1)
                        if j >= 2:
                            pe.wait_ge(S["post_out"], n - 1)
                        for h in range(HEADS):
                            last = nc.tensor.transpose(bank[6 + j % 2][:, H(h)], oacc[:, t, H(h)], ident)
                        last.then_inc(S["post_tr"], 1)
                    pe.wait_ge(S["post_out"], post_count(l, b) + len(token_tiles(l)))
                post(2)

                evacuated(pe, seg_of(l, "mqk"))
                evacuated(pe, seg_of(l, "mv"))
                for t in range(NT):
                    for i in range(2):
                        at = (t % 2) * 256 + i * P
                        last = nc.tensor.transpose(bank[2 + t // 2][:, at:at + P], mk[:, i, t * P:(t + 1) * P], ident)
                last.then_inc(S["mkt_psum"], 1)
                pe.wait_ge(S["mkt_out"], l + 1)
                pe.wait_ge(S["pads_set"], l + 1)
                for u, (d, t) in enumerate(UNITS):
                    g = 8 * l + u
                    gives = u in out_units[l]
                    o = sofar([len(v) for v in out_units], l) + len([v for v in out_units[l] if v <= u])
                    ts = slice(t * P, (t + 1) * P)
                    if g > 0:
                        pe.wait_ge(S["ml_ecol"], g)
                    mm(bank[5][0:4, 0:P], gates[:, t, 8 * d:8 * d + 4], ident, start=True, stop=True)
                    mm(bank[5][0:4, P:2 * P], lgate[:, t, 4 * d:4 * d + 4], tri[d], start=True, stop=True)\
                        .then_inc(S["ml_small"], 1)
                    if g > 0:
                        pe.wait_ge(S["ml_state"], g)
                    if gives:
                        for h in range(HEADS):
                            i, r = h // 2, 64 * (h % 2)
                            last = mm(bank[3 + 3 * (h % 2)][:, H(i)], mk[r:r + 64, i, ts], mq[r:r + 64, i, ts],
                                      start=True, stop=True)
                        last.then_inc(S["ml_qk"], 1)
                    pe.wait_ge(S["ml_rows"], g + 1)
                    pe.wait_ge(S["ml_exp"], g + 1)
                    mm(bank[5][:, 256:260], mrow[:, 5, :], ident[0:4, 0:4].rearrange("p (i r) -> p r i", r=2),
                       start=True, stop=True)
                    mm(bank[5][:, 260:264], mrow[:, 6, :], ident[0:4, 0:4], start=True, stop=True)
                    end = P - 1 if d == 0 else 0
                    for i in range(2):
                        last = mm(bank[5][:, 264 + i:265 + i], selp[i], mrow[:, 7, end:end + 1], start=True, stop=True)
                    last.then_inc(S["ml_cols"], 1)
                    if gives:
                        mm(bank[2][:, :], ident_b, mask_b[d], start=True, stop=False)
                        for q in range(HEADS):
                            h = 2 * (q % 2) + q // 2
                            mm(bank[2][:, H(q)], mrow[:, 1, :], sel[h], start=False, stop=False)
                            last = mm(bank[2][:, H(q)], sel[h], mrow[:, 3, :], start=False, stop=q == HEADS - 1)
                        last.then_inc(S["ml_arg"], 1)
                        for i in range(2):
                            last = mm(bank[7][:, i * P:(i + 1) * P], selp[i], mrow[:, 7, :], start=True, stop=True)
                        last.then_inc(S["ml_qb"], 1)
                    for n in BESIDE[(l, u)]:
                        segment(n)
                    if gives:
                        pe.wait_ge(S["ml_p"], o)
                        pe.wait_ge(S["ml_qg"], o)
                        for h in range(HEADS):
                            i, r = h // 2, 64 * (h % 2)
                            dst = bank[4 + 2 * (h % 2)][:, 129 * i:129 * i + 129]
                            mm(dst, work[:, 1, H(2 * (h % 2) + i)], mv[:, t, h, :], start=True, stop=False)
                            last = mm(dst, work[r:r + 64, 2, i * P:(i + 1) * P], mstate[r:r + 64, d, i, :],
                                      start=False, stop=True)
                        last.then_inc(S["ml_num"], 1)
                    pe.wait_ge(S["ml_kw"], g + 1)
                    for h in range(HEADS):
                        i, r = h // 2, 64 * (h % 2)
                        last = mm(mlstm_c(i)[r:r + 64, :], work[:, 3, 64 * h:64 * h + 64], mv[:, t, h, :], start=True, stop=True)
                    last.then_inc(S["ml_c"], 1)
                    if gives:
                        pe.wait_ge(S["ml_h"], 2 * o)
                post(1)

                evacuated(pe, seg_of(l, "ak"))
                evacuated(pe, seg_of(l, "av"))
                for j in range(8):
                    src = (aq if j < 4 else ak)[:, j % 4, CTX:TOK]
                    if j >= 2:
                        pe.wait_ge(S["rope_out"], 8 * l + j - 1)
                    mm(bank[4 + j % 2][:, 0:LAT], rope_r, src, start=True, stop=True).then_inc(S["rope_psum"], 1)
                pe.wait_ge(S["rope_out"], 8 * l + 8)
                steps_a = attn_units(l + 1) - attn_units(l)

                def scores(k):
                    g = attn_units(l) + k
                    t, h = token_tiles(l)[k // 4], k % 4
                    nk = CTX if t < 2 else TOK
                    if g >= 2:
                        pe.wait_ge(S["at_e"], 2 * g - 2)
                    for m in range(2):
                        r = 64 * m
                        last = mm(bank[2 + 4 * (g % 2) + m][:, 0:nk], aq[r:r + 64, h, t * P:(t + 1) * P],
                                  ak[r:r + 64, h, 0:nk], start=True, stop=True)
                    last.then_inc(S["at_s"], 1)

                scores(0)
                for k in range(steps_a):
                    g = attn_units(l) + k
                    t, h = token_tiles(l)[k // 4], k % 4
                    nk = CTX if t < 2 else TOK
                    q = g % 2
                    if k + 1 < steps_a:
                        scores(k + 1)
                    for j in range(32 // steps_a // 2 * k, 32 // steps_a // 2 * (k + 1)):
                        dense(l, "bg", [j])
                        dense(l, "by", [j])
                    pe.wait_ge(S["at_w"], g + 1)
                    if g >= 1:
                        pe.wait_ge(S["at_wtout"], g)
                    for kt in range(nk // P):
                        last = nc.tensor.transpose(bank[4][:, H(kt)], work[:, 4 * q + 2, H(kt)], ident)
                    last.then_inc(S["at_wt"], 1)
                    pe.wait_ge(S["at_wtout"], g + 1)
                    if g >= 1:
                        pe.wait_ge(S["at_oout"], g)
                    for kt in range(nk // P):
                        last = mm(bank[5][:, 0:P], work[:, 4 * q + 3, H(kt)], av[:, kt, H(h)], start=kt == 0,
                                  stop=kt == nk // P - 1)
                    last.then_inc(S["at_o"], 1)
                post(0)
                for j in range(16, 24):
                    dense(l, "bg", [j])
                    dense(l, "by", [j])
                dense(l, "wo")
                norm(l, 1)
                norm(l, 2)
                pe.wait_ge(S["h_ready"], 2 * KD * l + 2 * KD)
                dense(l, "ff1")
                dense(l, "ff2")
                norm(l, 3)

            pe.wait_ge(S["res_ready"], 2 * DEPTH * KD)
            for t in range(2):
                for hf in range(2):
                    for q in range(4):
                        last = nc.tensor.transpose(bank[2 + 2 * t + hf][:, q * P:(q + 1) * P],
                                                   xt[:, 4 * hf + q, CTX + t * P:CTX + (t + 1) * P], ident)
                    last.then_inc(S["final_psum"], 1)


_INS = ["x", "c", "ctx", "c_ctx", "w_ada", "b_ada", "norm_gains", "w_in", "b_in", "a_lambda", "a_norm",
        "m_fbias", "m_norm", "g_conv", "g_alog", "g_dtbias", "g_norm", "w_branch", "w_out", "w_ff1", "w_ff2"]


def kernel(**inputs):
    import numpy as _np
    import concourse.bacc as _bacc
    from concourse import mybir as _mybir
    from concourse.bass_utils import run_bass_kernel_spmd as _run

    nc = _bacc.Bacc("TRN2", target_bir_lowering=False, num_devices=1)
    arrays, args = {}, []
    const_f, const_b, const_m = shape_constants()
    every = [(n, _np.ascontiguousarray(inputs[n])) for n in _INS]
    every += [("const_f", const_f), ("const_b", const_b), ("const_m", const_m)]
    for name, a in every:
        arrays[f"in_{name}"] = a
        args.append(nc.dram_tensor(f"in_{name}", a.shape, _mybir.dt.from_np(a.dtype), kind="ExternalInput").ap())
    args.append(nc.dram_tensor("out_0", (1, LAT, DM), F32, kind="ExternalOutput").ap())
    hybrid_trunk(nc, *args)
    r = _run(nc, [arrays], core_ids=[0])
    return r.results[0]["out_0"]
```

```python
import math
from contextlib import ExitStack

import numpy as np

import concourse.bass as bass
from concourse import mybir

F32 = mybir.dt.float32
BF16 = mybir.dt.bfloat16
U8 = mybir.dt.uint8
ALU = mybir.AluOpType
ACT = mybir.ActivationFunctionType
AX_X = mybir.AxisListType.X

P = 128
DEPTH, DM, CTX, LAT = 2, 1024, 256, 256
TOK = CTX + LAT
KD = DM // P
NT = TOK // P
HEADS, A_HD, M_QK, M_V, G_HD = 4, 64, 64, 128, 128
CONV_K, D_FF, GRID_W = 5, 4096, 64
FT = D_FF // P
EPS = 1e-6
LEVELS = 7
RING = 4
CW = 2048

A_Q, A_K, A_V = 0, 512, 1024
M_QKC, M_VC, M_O, M_GATES = 1536, 2048, 2560, 3072
G_Q, G_K, G_V, G_Z, G_GATES, BR_G = 3088, 3600, 4112, 4624, 5136, 5152

B_AQ, B_AK, B_AV, B_MQ, B_MK, B_MV, B_MO, B_GQ, B_GZ, B_BG = 0, 4, 8, 12, 14, 16, 20, 24, 36, 40
B_ADA, R_C = 64, 112
R_GAIN, R_CONV, R_AN, R_MN, R_GN = 0, 32, 92, 93, 97

UNITS = [(0, 0), (1, 1), (0, 1), (1, 0), (0, 2), (1, 3), (0, 3), (1, 2)]
FIRST_VISIT = {0, 1, 4, 5}


ADA_NOW = 8
GAPS = 2 * (LEVELS - 1)


def shape_constants():
    k = np.arange(P)
    ident = np.eye(P, dtype=np.float32)
    tri_f = (k[:, None] <= k[None, :]).astype(np.float32)
    tri_b = (k[:, None] >= k[None, :]).astype(np.float32)
    rope = np.zeros((P, P), np.float32)
    for m in range(P):
        if (m // 16) % 2 == 0:
            rope[m + 16, m] = -1.0
        else:
            rope[m - 16, m] = 1.0
    half = A_HD // 2
    inv_freq = np.float32(10000.0) ** (-np.arange(0, half, 2, dtype=np.float32) / np.float32(half))
    tok = np.arange(LAT)
    row, col = (tok // GRID_W).astype(np.float32), (tok % GRID_W).astype(np.float32)
    ar, ac = row[:, None] * inv_freq, col[:, None] * inv_freq
    ang = np.concatenate([ar, ar, ac, ac] * 2, axis=-1).T.astype(np.float32)
    selp = np.zeros((P, 2, P), np.float32)
    for h in range(HEADS):
        selp[h, h // 2, 64 * (h % 2):64 * (h % 2) + 64] = 1.0
    f = np.concatenate([ident, tri_f, tri_b, rope, np.cos(ang), np.sin(ang),
                        selp.reshape(P, -1)], axis=1).astype(np.float32)
    b = np.stack([ident, (1 - tri_f) * -1e30, (1 - tri_b) * -1e30], axis=1).astype(np.float32)
    m = np.zeros((P, 2, LEVELS, P), np.float32)
    for lv in range(LEVELS):
        blk = k >> lv
        up = (blk[:, None] // 2 == blk[None, :] // 2) & (blk[:, None] % 2 == 0) & (blk[None, :] % 2 == 1)
        m[:, 0, lv], m[:, 1, lv] = up, up.T
    return f, b, m


def plan():
    segs, chunks, where, gaps, beside = [], [], {}, {}, {}
    taken = {"act": 0, "dve": 0}

    def chunk(l, kind, i):
        chunks.append([l, kind, i, None])
        return len(chunks) - 1

    def seg(l, kind, i, c, engine, bank=None, evacuated=True):
        n = len(segs)
        if evacuated:
            taken[engine] += 1
        if bank is None:
            bank = len([s for s in segs if s[4] < 2 and s[1] != "ff2"]) % 2
        segs.append((l, kind, i, c, bank,
                     engine if evacuated else None, taken[engine]))
        if c is not None:
            chunks[c][3] = n
        where.setdefault((l, kind), []).append(n)
        return n

    def group(l, kind, engine, order=range(4), bank=None):
        for i in order:
            if i % 2 == 0:
                group.chunk = chunk(l, kind, i // 2)
            n = seg(l, kind, i, group.chunk, engine, bank)
        return n

    def columns(block, bank=None):
        l, n, c = block
        return seg(l, "adam", n, c, "dve", bank)

    block = None
    for l in range(DEPTH):
        if l == 0:
            for n in range(ADA_NOW):
                seg(l, "ada", n, chunk(l, "ada", n), "act")
                if n > 0:
                    seg(l, "adat", n - 1, None, "dve")
            seg(l, "adat", ADA_NOW - 1, None, "dve")
        group(l, "gq", "act", [0])
        seg(l, "gate", 0, None, "dve")
        group(l, "gq", "act", [1, 2, 3])
        group(l, "gk", "act")
        group(l, "gv", "act")
        group(l, "gz", "dve")
        count = 0
        for p in range(4):
            pieces = []
            for q in range(4):
                if block is not None:
                    pieces.append([(columns(block, 2 + 4 * (count % 2)), 0, 4)])
                    count += 1
                n = ADA_NOW + 4 * p + q
                block = (l, n, chunk(l, "ada", n))
                if q < 3:
                    kind, i = (("mqk", "mv", "mo")[(3 * p + q) // 4], (3 * p + q) % 4)
                    n = group(l, kind, "act" if kind == "mo" else "dve", [i], 2 + 4 * (count % 2))
                    count += 1
                    pieces += [[(n, k, k + 1)] for k in range(4)]
            for x in range(GAPS):
                gaps[(l, p, x)] = sum(pieces[x * len(pieces) // GAPS:(x + 1) * len(pieces) // GAPS], [])
        beside[(l, -1)] = [columns(block), group(l, "aq", "dve", [0])]
        block = None
        for u in range(8):
            beside[(l, u)] = [columns(block)] if block is not None else []
            block = (l + 1, u, chunk(l + 1, "ada", u)) if l + 1 < DEPTH else None
            beside[(l, u)] += [group(l, ("aq", "ak", "av")[m // 4], "dve", [m % 4])
                               for m in range(1 + 11 * u // 8, 1 + 11 * (u + 1) // 8)]
        first = chunk(l, "bg", (2, 0))
        seg(l, "bg", (2, 0), first, "act")
        beside[(l, 8)] = [columns(block)] if block is not None else []
        block = None
        for b in (2, 1, 0):
            for half in range(2):
                for nb in range(2):
                    at_first = (b, half, nb) == (2, 0, 0)
                    bg = first if at_first else chunk(l, "bg", (b, 2 * half + nb))
                    if nb == 0:
                        wb = chunk(l, "wb", (b, half))
                    for i in range(2):
                        cc = 4 * half + 2 * nb + i
                        if not (at_first and i == 0):
                            seg(l, "bg", (b, cc), bg, "act")
                        seg(l, "by", (b, cc), wb, "dve")
        for nb in range(4):
            c = chunk(l, "wo", nb)
            for i in range(2):
                seg(l, "wo", 2 * nb + i, c, "act")
        for n in range(16):
            c = chunk(l, "ff1", n)
            for i in range(2):
                seg(l, "ff1", 2 * n + i, c, "act")
        for nb in range(4):
            for kc in range(4):
                c = chunk(l, "ff2", (nb, kc))
                for i in range(2):
                    seg(l, "ff2", (nb, kc, i), c, "act", bank=2 + (2 * nb + i) % 5, evacuated=kc == 3)
    return segs, chunks, where, gaps, beside


def hybrid_trunk(nc, x, c, ctx, c_ctx, w_ada, b_ada, norm_gains, w_in, b_in, a_lambda, a_norm,
                 m_fbias, m_norm, g_conv, g_alog, g_dtbias, g_norm, w_branch, w_out, w_ff1, w_ff2,
                 const_f, const_b, const_m, out):
    SEGS, CHUNKS, WHERE, IN_GAP, BESIDE = plan()

    def tokens(l):
        return (0, TOK) if l < DEPTH - 1 else (CTX, LAT)

    with ExitStack() as stack:
        def sb(name, shape, dt=F32):
            return stack.enter_context(nc.sbuf_tensor(name, shape, dt))

        def sem(name):
            return stack.enter_context(nc.semaphore(name))

        bank = [stack.enter_context(nc.psum_tensor(f"bank{i}", [P, 512], F32)) for i in range(8)]

        cf = sb("cf", [P, 4 * P + 2 * LAT + 2 * P])
        ident, tri = cf[:, 0:P], [cf[:, P:2 * P], cf[:, 2 * P:3 * P]]
        rope_r = cf[:, 3 * P:4 * P]
        cos_t, sin_t = cf[:, 512:768], cf[:, 768:1024]
        sel = [cf[0:4, h:h + 1].broadcast_to((HEADS, P)) for h in range(HEADS)]
        selp = [cf[0:4, 1024 + i * P:1024 + (i + 1) * P] for i in range(2)]
        cb = sb("cb", [P, 3, P], BF16)
        ident_b = cb[:, 0, :]
        mask_b = [cb[:, 1 + d, :].unsqueeze(1).broadcast_to((P, HEADS, P)) for d in range(2)]
        cm = sb("cm", [P, 2, LEVELS, P], U8)
        ones = sb("ones", [P, P])
        cols1 = sb("cols1", [P, DEPTH, P])
        cols2 = sb("cols2", [P, DEPTH, P])
        gate_bias = sb("gate_bias", [P, DEPTH, 32])
        fdt_bias = sb("fdt_bias", [P, DEPTH, 16])
        alog = sb("alog", [P, DEPTH, 8])
        v_bias = sb("v_bias", [P, 2, 512])
        w_gates = sb("w_gates", [P, KD, 32])

        xt = sb("xt", [P, KD, TOK])
        ht = sb("ht", [P, KD, TOK])
        ring = sb("ring", [P, RING, CW])
        arena = sb("arena", [P, 19480])
        work = sb("work", [P, 18, 512])

        def part(at, n):
            return arena[:, at:at + n]

        gq = part(0, 2048).rearrange("p (h t) -> p h t", h=4)
        gk = part(2048, 2048).rearrange("p (h t) -> p h t", h=4)
        gz = part(4096, 2048).rearrange("p (h t) -> p h t", h=4)
        gk_tok = part(6144, 2048).rearrange("p (t c) -> p t c", t=NT)
        gv_tok = part(8192, 2048).rearrange("p (t c) -> p t c", t=NT)
        oacc = part(10240, 2048).rearrange("p (t c) -> p t c", t=NT)
        raw = part(14336, 1560).rearrange("p (r s c) -> p r s c", r=3, s=2)
        mq = part(12288, 1024).rearrange("p (i t) -> p i t", i=2)
        mk = part(13312, 1024).rearrange("p (i t) -> p i t", i=2)
        mo = part(14336, 2048).rearrange("p (h t) -> p h t", h=4)
        mv = part(16384, 2064).rearrange("p (t h c) -> p t h c", t=NT, h=4)
        mk_tok = part(18448, 1024).rearrange("p (t c) -> p t c", t=NT)
        aq, ak, av = gq, gk, gk_tok
        hidden = part(0, 16384).rearrange("p (f t) -> p f t", f=FT)
        ot_of = {1: part(0, 4096).rearrange("p (k t) -> p k t", k=KD), 3: work[:, 0:8, :]}
        level_masks = part(1024, 2 * LEVELS * P)
        rows1 = part(0, DEPTH * P).rearrange("p (l c) -> p l c", l=DEPTH)
        rows2 = part(256, DEPTH * P).rearrange("p (l c) -> p l c", l=DEPTH)
        lamv = part(512, DEPTH * 4 * A_HD).rearrange("p (l a c) -> p l a c", l=DEPTH, a=4)
        merged = work[:, 10:18, :]
        gate_sig = [part(12288, 512), part(12800, 512)]
        gated = [part(13312, 512), part(13824, 512)]

        silu_c = sb("silu_c", [P, 2, KD])
        ada = sb("ada", [P, 2, 48, 2])
        mod_scale = sb("mod_scale", [P, 2, KD, 2])
        out_gate = sb("out_gate", [P, 2, KD, 2])
        gates = sb("gates", [P, NT, 32])
        zgate = sb("zgate", [P, NT, 16])
        egate = sb("egate", [P, NT, 16])
        lgate = sb("lgate", [P, NT, 16])
        coef = sb("coef", [P, 16])
        beta = sb("beta", [P, NT, 8])
        nbeta = sb("nbeta", [P, NT, 8])
        lam2 = sb("lam2", [P, DEPTH, 2])
        nlam = sb("nlam", [P, DEPTH])
        gcol = [sb(f"gcol{d}", [P, 16]) for d in range(2)]
        gecol = [sb(f"gecol{d}", [P, 16]) for d in range(2)]
        gstate = sb("gstate", [P, 2, HEADS, G_HD])
        row_buf = sb("row_buf", [P, 8, P])
        mrow = row_buf[0:4, :, :]
        grow = [mrow[:, 4 * d, :] for d in range(2)]
        rstd = row_buf[:, 0:4, :].rearrange("p a c -> p (a c)")
        ada_sums = sb("ada_sums", [P, 2, 2, 256])
        ada_product = sb("ada_product", [P, 256])
        ada_rows = ada_sums[0:2, :, 0, :]
        mmax = sb("mmax", [4, 2])
        mcol_of = sb("mcol", [P, 2, 16])
        mden = sb("mden", [P, 8])
        mstate = gstate[:, :, :, :].rearrange("p d h c -> p (d h c)")[:, 0:4 * (M_V + 1)]\
            .rearrange("p (d i c) -> p d i c", d=2, i=2)
        amax = sb("amax", [P, 2, 8])
        post_stat = sb("post_stat", [P, NT, HEADS])

        names = (
            "consts_in params_in rows_in x_in chunk_in0 chunk_in1 chunk_in2 chunk_in3 gatew_in out_stored "
            "ones_set masks_ready pads_set states_zero "
            "dense_ready taken_act taken_dve act_step dve_step pool_step "
            "vbias_in cols_psum cols_ready csig silu_ready ada_latents ada_context ada_ready "
            "xtr_psum xtr_ready lam_sum lam_exp "
            "sq_ready sq_used norm_root out_sum scaled_ready h_ready res_scaled res_odd "
            "gates_z gates_exp gates_ready "
            "conv_done conv_sig conv_out vt_psum vt_out l2_sq l2_sum l2_root l2_out kt_psum kt_out "
            "gz_sig "
            "slots_set "
            "ml_small ml_rows ml_exp ml_cols ml_ecol ml_arg ml_decay ml_qk ml_p ml_qb ml_qg ml_kw ml_num "
            "ml_h ml_c ml_state mkt_psum mkt_out "
            "post_sq post_sum post_root post_norm post_tr post_out "
            "rope_psum rope_out at_s at_max at_e at_w at_wt at_wtout at_o at_oout "
            "y_ready hid_ready res_ready final_psum final_out"
        ).split()
        S = {n: sem(n) for n in names}
        gd_names = ("small rows cols ecol neg ke arg decay qk b qkd eye u0 t0 t1 m mout u uout t tout ks r qs qg "
                    "v vn o oacc s state").split()
        G = [{n: sem(f"gd_{n}_{way}") for n in gd_names} for way in ("forward", "backward")]

        block = stack.enter_context(nc.Block())

        out_units = [[u for u in range(8) if l < DEPTH - 1 or UNITS[u][1] >= 2] for l in range(DEPTH)]

        CHUNK_OF = [[0, 1, 2, 3], [1, 0, 3, 2]]

        def gd_gives(l, p):
            return l < DEPTH - 1 or p >= 2

        def gd_outs(l, p):
            return sum(4 if k < DEPTH - 1 else 2 for k in range(l)) + (p + 1 if l < DEPTH - 1 else max(p - 1, 0))

        def slot(d, i):
            return work[:, 9 * d + i, :]

        def parity(a, lv, q):
            return a.rearrange("p (h b q s) -> p h b q s", h=HEADS, q=2, s=2 ** lv)[:, :, :, q, :]

        def compact(a, lv):
            return a.rearrange("p (h b s) -> p h b s", h=HEADS, s=2 ** lv)

        def product(b, lv, q):
            return parity(bank[b][:, :], lv, q) if lv == 1 else compact(bank[b][:, 0:256], lv)

        def sofar(counts, l):
            return sum(counts[:l])

        def evacuated(eng, n):
            eng.wait_ge(S["taken_" + SEGS[n][5]], SEGS[n][6])

        ADA_SEGS = [n for n in range(len(SEGS)) if SEGS[n][1] == "adam"]

        def modulation_block(eng, l, n):
            m = [SEGS[s][0::2][:2] == (l, n) for s in ADA_SEGS].index(True)
            c = SEGS[ADA_SEGS[m]][3]
            eng.wait_ge(S[f"chunk_in{c % RING}"], 16 * (c // RING + 1))
            eng.wait_ge(S["dense_ready"], (ADA_SEGS[m - 2] if m >= 2 else seg_of(0, "adat", ADA_NOW - 1)) + 1)
            return m, ring[:, c % RING, :].rearrange("p (k n) -> p k n", k=KD)

        def last_columns(l, now):
            if l == 0:
                return seg_of(l, "adat") if now else seg_of(l, "adam")
            return seg_of(l, "adam", ADA_NOW - 1 if now else -1)

        def completed(fill):
            return [n for n, _, to in fill if to == 4]

        def seg_of(l, kind, i=-1):
            return WHERE[(l, kind)][i]

        def token_tiles(l):
            t0, n = tokens(l)
            return list(range(t0 // P, (t0 + n) // P))

        def seg_tokens(l, kind):
            return (0, TOK) if kind in ("gk", "gv", "mqk", "mv", "ak", "av") else tokens(l)

        def post_count(l, b):
            return 3 * NT * l + {2: 0, 1: 1, 0: 2}[b] * len(token_tiles(l))

        def attn_units(l):
            return sum(4 * len(token_tiles(k)) for k in range(l))

        def norm_count(l, which):
            return 4 * l + which

        def residual_done(eng, n):
            eng.wait_ge(S["res_ready"], n * KD // 2)
            eng.wait_ge(S["res_odd"], n * KD // 2)

        def scaled_count(l, which):
            return 2 * KD * l + KD * (which // 2)

        def outputs(l, u):
            return sofar([len(v) for v in out_units], l) + len([v for v in out_units[l] if v <= u])

        def mlstm_c(i):
            return bank[3][:, 129 * i:129 * i + 129]

        def load_rows(eng, l):
            rows_of = lambda v: v.rearrange("(j p) -> j p", p=P)
            table1 = [(B_AQ, b_in[l, 0:3072]), (B_GQ, b_in[l, G_Q:G_Q + 2048]), (B_BG, b_in[l, BR_G:BR_G + 3072]),
                      (B_ADA, b_ada[l, :]), (R_C, c[0, :]), (R_C + 8, c_ctx[:])]
            for r, src in table1:
                v = rows_of(src)
                eng.dma_start(rows1[r:r + v.shape[0], l, :], v).then_inc(S["rows_in"], 16)
            eng.dma_start(rows2[0:32, l, :], norm_gains[l].rearrange("g (j p) -> (g j) p", p=P)).then_inc(S["rows_in"], 16)
            eng.dma_start(rows2[R_CONV:R_CONV + 60, l, :],
                         g_conv[l].rearrange("k (j p) -> (k j) p", p=P)).then_inc(S["rows_in"], 16)
            eng.dma_start(rows2[R_AN:R_AN + 1, l, :], a_norm[l:l + 1, :]).then_inc(S["rows_in"], 16)
            eng.dma_start(rows2[R_MN:R_MN + 4, l, :], m_norm[l]).then_inc(S["rows_in"], 16)
            eng.dma_start(rows2[R_GN:R_GN + 1, l, :], g_norm[l:l + 1, :]).then_inc(S["rows_in"], 16)

        @block.sync
        def _(sp):
            sp.dma_start(cf[:, :], const_f).then_inc(S["x_in"], 16)
            load_rows(sp, 0)
            sp.dma_start(work[:, 8, 0:3 * P].rearrange("p (a c) -> p a c", a=3), const_b).then_inc(S["consts_in"], 16)
            sp.dma_start(level_masks, const_m.rearrange("p a b c -> p (a b c)")).then_inc(S["consts_in"], 16)

            def chunk_source(l, kind, i):
                tall = lambda w: w.rearrange("(k p) n -> p k n", p=P)
                cols = {"gq": G_Q, "gk": G_K, "gv": G_V, "gz": G_Z, "mqk": M_QKC, "mv": M_VC, "mo": M_O,
                        "aq": A_Q, "ak": A_K, "av": A_V}
                if kind == "ada":
                    return tall(w_ada[l][:, 256 * i:256 * i + 256]), 8
                if kind in cols:
                    at = cols[kind] + 256 * i
                    return tall(w_in[l][:, at:at + 256]), 8
                if kind == "bg":
                    at = BR_G + 1024 * i[0] + 256 * i[1]
                    return tall(w_in[l][:, at:at + 256]), 8
                if kind == "wb":
                    return tall(w_branch[l, i[0]][:, 512 * i[1]:512 * i[1] + 512]), 4
                if kind == "wo":
                    return tall(w_out[l][:, 256 * i:256 * i + 256]), 8
                if kind == "ff1":
                    return tall(w_ff1[l][:, 256 * i:256 * i + 256]), 8
                return tall(w_ff2[l][1024 * i[1]:1024 * i[1] + 1024, 256 * i[0]:256 * i[0] + 256]), 8

            for n, (l, kind, i, _) in enumerate(CHUNKS):
                if n >= RING:
                    sp.wait_ge(S["dense_ready"], CHUNKS[n - RING][3] + 1)
                src, k = chunk_source(l, kind, i)
                sp.dma_start(ring[:, n % RING, :].rearrange("p (k n) -> p k n", k=k), src)\
                    .then_inc(S[f"chunk_in{n % RING}"], 16)
                if kind == "gq" and i == 0:
                    if l > 0:
                        sp.wait_ge(S["dense_ready"], seg_of(l - 1, "gate") + 1)
                    tall = lambda w: w.rearrange("(k p) n -> p k n", p=P)
                    sp.dma_start(w_gates[:, :, 0:16], tall(w_in[l][:, M_GATES:M_GATES + 16])).then_inc(S["gatew_in"], 16)
                    sp.dma_start(w_gates[:, :, 16:32], tall(w_in[l][:, G_GATES:G_GATES + 16])).then_inc(S["gatew_in"], 16)
            for n in range(4):
                hf, t = n // 2, n % 2
                sp.wait_ge(S["final_out"], n + 1)
                sp.dma_start(out[0, t * P:(t + 1) * P, 512 * hf:512 * (hf + 1)], work[:, n, :]).then_inc(S["out_stored"], 16)
            sp.wait_ge(S["out_stored"], 16 * 4)

        @block.gpsimd
        def _(pool):
            steps = [0]

            def link(ins):
                steps[0] += 1
                ins.then_inc(S["pool_step"], 1)
                pool.wait_ge(S["pool_step"], steps[0])

            nc.gpsimd.memset(ones[:, :], 1.0).then_inc(S["ones_set"], 1)
            for d in range(2):
                nc.gpsimd.memset(slot(d, 5), 0.0).then_inc(S["slots_set"], 1)
            for l in range(DEPTH):
                flat = lambda v: v.rearrange("a b -> (a b)").partition_broadcast(P)
                pool.dma_start(gate_bias[:, l, 0:16], b_in[l, M_GATES:M_GATES + 16].partition_broadcast(P)).then_inc(S["params_in"], 16)
                pool.dma_start(gate_bias[:, l, 16:32], b_in[l, G_GATES:G_GATES + 16].partition_broadcast(P)).then_inc(S["params_in"], 16)
                pool.dma_start(fdt_bias[:, l, 0:8], flat(m_fbias[l])).then_inc(S["params_in"], 16)
                pool.dma_start(fdt_bias[:, l, 8:16], flat(g_dtbias[l])).then_inc(S["params_in"], 16)
                pool.dma_start(alog[:, l, :], flat(g_alog[l])).then_inc(S["params_in"], 16)
                pool.dma_start(lamv[:, l, :, :].rearrange("p a b -> p (a b)"), flat(a_lambda[l])).then_inc(S["params_in"], 16)

            pool.wait_ge(S["x_in"], 16 * 3)
            pool.wait_ge(S["consts_in"], 16 * 2)
            pool.wait_ge(S["silu_ready"], 1)

            def modulation_sum(l, n):
                m, w = modulation_block(pool, l, n)
                acc = ada_sums[:, m % 2, 1, :]
                link(nc.gpsimd.tensor_scalar(acc, w[:, 0, :], silu_c[:, 1, 0:1], None, ALU.mult))
                for k in range(1, KD):
                    link(nc.gpsimd.tensor_scalar(ada_product[:, :], w[:, k, :], silu_c[:, 1, k:k + 1], None, ALU.mult))
                    ins = nc.gpsimd.tensor_tensor(acc, acc, ada_product[:, :], ALU.add)
                    if k < KD - 1:
                        link(ins)
                ins.then_inc(S["ada_context"], 1)

            for l in range(DEPTH):
                if l > 0:
                    evacuated(pool, seg_of(l - 1, "av"))
                for a, at in ((0, M_VC), (1, A_V)):
                    pool.dma_start(v_bias[:, a, :], b_in[l, at:at + 512].partition_broadcast(P)).then_inc(S["vbias_in"], 16)
                if l > 0:
                    residual_done(pool, 2 * l)
                for r in range(3):
                    for s in range(2):
                        nc.gpsimd.memset(raw[:, r, s, 0:2], 0.0)
                        nc.gpsimd.memset(raw[:, r, s, 258:260], 0.0)
                nc.gpsimd.memset(mv[:, :, :, M_V:M_V + 1], 1.0).then_inc(S["pads_set"], 1)
                nc.gpsimd.memset(gstate[:, :, :, :], 0.0).then_inc(S["states_zero"], 1)
                nc.gpsimd.memset(mmax[:, :], 0.0).then_inc(S["states_zero"], 1)

                for j in range(8):
                    t0, n = seg_tokens(l, "gq" if j < 4 else "gk")
                    src = (gq if j < 4 else gk)[:, j % 4, t0:t0 + n]
                    pool.wait_ge(S["conv_out"], 12 * l + j + 1)
                    if j >= 2 or l > 0:
                        pool.wait_ge(S["l2_sum"], 8 * l + j - 1)
                    nc.gpsimd.tensor_tensor(work[:, 10 + j % 2, 0:n], src, src, ALU.mult).then_inc(S["l2_sq"], 1)

                four = lambda a: a.rearrange("p (h c) -> p h c", h=4)
                pool.wait_ge(S["conv_out"], 12 * (l + 1))
                pool.wait_ge(S["l2_out"], 8 * (l + 1))
                for p in range(4):
                    g = 4 * l + p
                    for d in range(2):
                        if g > 0:
                            pool.wait_ge(G[d]["v"], g)
                        nc.gpsimd.tensor_copy(four(slot(d, 3)), ident.unsqueeze(1).broadcast_to((P, 4, P)))\
                            .then_inc(G[d]["eye"], 1)
                    for d in range(2):
                        pool.wait_ge(G[d]["neg"], g + 1)
                        keys = four(gk_tok[:, CHUNK_OF[d][p], :])
                        nc.gpsimd.tensor_tensor(four(slot(d, 7)), keys,
                                                gecol[d][:, 4:8].unsqueeze(2).broadcast_to((P, 4, P)), ALU.mult)\
                            .then_inc(G[d]["ke"], 1)
                    for n in range(ADA_NOW + 4 * p, ADA_NOW + 4 * p + 4):
                        modulation_sum(l, n)

                def post_squares(b):
                    for j, t in enumerate(token_tiles(l)):
                        n = post_count(l, b) + j
                        if b == 2:
                            for d in range(2):
                                pool.wait_ge(G[d]["oacc"], gd_outs(l, 3))
                        elif b == 1:
                            pool.wait_ge(S["ml_h"], 2 * sofar([len(v) for v in out_units], l + 1))
                        else:
                            pool.wait_ge(S["at_oout"], attn_units(l + 1))
                        if n >= 2:
                            pool.wait_ge(S["post_sum"], n - 1)
                        nc.gpsimd.tensor_tensor(work[:, 8 + j % 2, :], oacc[:, t, :], oacc[:, t, :],
                                                ALU.mult).then_inc(S["post_sq"], 1)
                post_squares(2)
                if l + 1 < DEPTH:
                    for n in range(ADA_NOW):
                        modulation_sum(l + 1, n)
                post_squares(1)

                t0, n = tokens(l)
                for j in range(16):
                    cc = j % 8
                    if j == 8:
                        post_squares(0)
                    evacuated(pool, seg_of(l, "by", 8 + j))
                    nc.gpsimd.tensor_tensor(merged[:, cc, 0:n], merged[:, cc, 0:n], gated[j % 2][:, 0:n],
                                            ALU.add).then_inc(S["y_ready"], 1)
                    if cc == 7:
                        pool.wait_ge(S["y_ready"], 16 * l + j + 1)
                def residual_odd(which):
                    t0, n = tokens(l)
                    for k in range(1, KD, 2):
                        pool.wait_ge(S["res_scaled"], KD * (2 * l + which // 2) + k + 1)
                        nc.gpsimd.tensor_tensor(xt[:, k, t0:t0 + n], xt[:, k, t0:t0 + n], ot_of[which][:, k, 0:n],
                                                ALU.add).then_inc(S["res_odd"], 1)

                residual_odd(1)
                for f in range(FT):
                    evacuated(pool, seg_of(l, "ff1", f))
                    nc.gpsimd.tensor_tensor(hidden[:, f, 0:n], work[:, 8 + f % 2, 0:n], work[:, 8 + f % 2, 0:n],
                                            ALU.mult).then_inc(S["hid_ready"], 1)
                residual_odd(3)

        @block.scalar
        def _(act):
            steps = [0]

            def link(ins):
                steps[0] += 1
                ins.then_inc(S["act_step"], 1)
                act.wait_ge(S["act_step"], steps[0])

            def dense(l, kind, idx=None):
                for n in WHERE[(l, kind)] if idx is None else [WHERE[(l, kind)][k] for k in idx]:
                    take(n)

            def sublayer_out(l, which, k, ps, n):
                m = KD * norm_count(l, which) + k
                act.wait_ge(S["sq_used"], m - 1)
                nc.scalar.activation(work[:, 8 + k % 2, 0:n], ps[:, 0:n], ACT.Square).then_inc(S["sq_ready"], 1)
                for a in range(0, n, CTX):
                    cond = 1 if a + tokens(l)[0] < CTX else 0
                    ins = nc.scalar.activation(ot_of[which][:, k, a:a + CTX], ps[:, a:a + CTX], ACT.Identity,
                                               scale=out_gate[:, which // 2, k, cond:cond + 1])
                ins.then_inc(S["taken_act"], 1)
                if k == KD - 2:
                    link(nc.scalar.activation(eps_col[:, 1:2], ones[:, 0:1], ACT.Sqrt))

            def take(n):
                l, kind, i, _, bk, engine, o = SEGS[n]
                if engine != "act" and kind != "gz":
                    return
                act.wait_ge(S["dense_ready"], n + 1)
                ps = bank[bk]
                t0, tn = seg_tokens(l, kind)
                if kind == "ada":
                    if i >= 2:
                        act.wait_ge(S["dense_ready"], seg_of(l, "adat", i - 2) + 1)
                    nc.scalar.copy(ada_rows[:, i % 2, :], ps[0:2, 0:256]).then_inc(S["taken_act"], 1)
                elif kind in ("gq", "gk", "gv"):
                    j = {"gq": 0, "gk": 4, "gv": 8}[kind] + i
                    if j >= 3:
                        act.wait_ge(S["conv_done"], 12 * l + j - 2)
                    else:
                        act.wait_ge(S["pads_set"], l + 1)
                    s0, sn = t0 // CTX, tn // CTX
                    nc.scalar.activation(raw[:, j % 3, s0:s0 + sn, 2:258],
                                         ps[:, 0:tn].rearrange("p (s c) -> p s c", s=sn), ACT.Identity,
                                         bias=cols1[:, l, B_GQ + j:B_GQ + j + 1]).then_inc(S["taken_act"], 1)
                elif kind == "gz":
                    if 4 * l + i >= 2:
                        evacuated(act, prev_gz(l, i, 2))
                    nc.scalar.activation(work[:, 8 + i % 2, 0:tn], ps[:, 0:tn], ACT.Sigmoid,
                                         bias=cols1[:, l, B_GZ + i:B_GZ + i + 1]).then_inc(S["gz_sig"], 1)
                elif kind == "mo":
                    if i == 0:
                        act.wait_ge(S["conv_done"], 12 * (l + 1))
                    nc.scalar.activation(mo[:, i, t0:t0 + tn], ps[:, 0:tn], ACT.Sigmoid,
                                         bias=cols1[:, l, B_MO + i:B_MO + i + 1]).then_inc(S["taken_act"], 1)
                elif kind == "bg":
                    b, cc = i
                    k = WHERE[(l, "bg")].index(n)
                    if k >= 2:
                        evacuated(act, seg_of(l, "by", k - 2))
                    nc.scalar.activation(gate_sig[k % 2][:, 0:tn], ps[:, 0:tn], ACT.Sigmoid,
                                         bias=cols1[:, l, B_BG + 8 * b + cc:B_BG + 8 * b + cc + 1])\
                        .then_inc(S["taken_act"], 1)
                elif kind == "wo":
                    sublayer_out(l, 1, i, ps, tn)
                elif kind == "ff1":
                    if FT * l + i >= 2:
                        act.wait_ge(S["hid_ready"], FT * l + i - 1)
                    nc.scalar.activation(work[:, 8 + i % 2, 0:tn], ps[:, 0:tn], ACT.Relu).then_inc(S["taken_act"], 1)
                elif kind == "ff2" and engine == "act":
                    nb, _, q = i
                    if 2 * nb + q == 0:
                        act.wait_ge(S["hid_ready"], FT * (l + 1))
                    sublayer_out(l, 3, 2 * nb + q, ps, tn)

            def prev_gz(l, i, back):
                k = 4 * l + i - back
                return seg_of(k // 4, "gz", k % 4)

            act.dma_start(ht[:, 0:4, :].rearrange("p (t a) c -> p t (a c)", t=2),
                         ctx[0].rearrange("(t p) c -> p t c", p=P)).then_inc(S["x_in"], 16)
            act.dma_start(ht[:, 4:8, :].rearrange("p (t a) c -> p t (a c)", t=2),
                         x[0].rearrange("(t p) c -> p t c", p=P)).then_inc(S["x_in"], 16)
            for l in range(1, DEPTH):
                load_rows(act, l)
            act.wait_ge(S["ones_set"], 1)

            for l in range(DEPTH):
                act.wait_ge(S["cols_psum"], 2 * l + 1)
                nc.scalar.copy(cols1[:, l, :], bank[2 + 2 * l][:, 0:P]).then_inc(S["cols_ready"], 1)
                act.wait_ge(S["cols_psum"], 2 * l + 2)
                nc.scalar.copy(cols2[:, l, 0:98], bank[3 + 2 * l][:, 0:98]).then_inc(S["cols_ready"], 1)
            act.wait_ge(S["cols_ready"], 4)
            nc.scalar.activation(silu_c[:, :, :].rearrange("p a k -> p (a k)"), cols1[:, 0, R_C:R_C + 16],
                                 ACT.Sigmoid).then_inc(S["csig"], 1)
            for k in range(KD):
                act.wait_ge(S["xtr_psum"], k + 1)
                nc.scalar.copy(xt[:, k, :], bank[4 + k % 4][:, :]).then_inc(S["xtr_ready"], 1)
            act.wait_ge(S["lam_sum"], 1)
            nc.scalar.activation(lam2[:, :, :], lam2[:, :, :], ACT.Exp).then_inc(S["lam_exp"], 1)

            def norm(l, which):
                t0, n = (0, TOK) if which == 0 else tokens(l)
                q = norm_count(l, which)
                for k in range(KD) if which in (0, 2) else ():
                    if which == 0 and l == 0:
                        act.wait_ge(S["xtr_ready"], KD)
                    else:
                        before = 2 * l + which // 2 - 1
                        if k % 2 == 0:
                            act.wait_ge(S["res_ready"], before * KD // 2 + k // 2 + 1)
                        else:
                            act.wait_ge(S["res_odd"], before * KD // 2 + k // 2 + 1)
                    if KD * q + k >= 2:
                        act.wait_ge(S["sq_used"], KD * q + k - 1)
                    nc.scalar.activation(work[:, 8 + k % 2, 0:n], xt[:, k, t0:t0 + n], ACT.Square).then_inc(S["sq_ready"], 1)
                if which in (0, 2):
                    act.wait_ge(S["sq_used"], KD * q + KD)
                else:
                    act.wait_ge(S["out_sum"], 2 * l + which // 2 + 1)
                nc.scalar.activation(rstd[:, 0:n], bank[7][:, 0:n], ACT.Sqrt, bias=eps_col[:, 0:1],
                                     scale=1.0 / DM).then_inc(S["norm_root"], 1)

            def modulate(l, which):
                t0, n = (0, TOK) if which == 0 else tokens(l)
                s = which // 2
                if which == 0:
                    act.wait_ge(S["ada_ready"], 2 * l + 1)
                else:
                    act.wait_ge(S["ada_ready"], 2 * l + 2)
                for k in range(KD):
                    act.wait_ge(S["scaled_ready"], scaled_count(l, which) + k + 1)
                    for a in range(t0, t0 + n, CTX):
                        cond = 1 if a < CTX else 0
                        last = nc.scalar.activation(ht[:, k, a:a + CTX], work[:, k, a - t0:a - t0 + CTX], ACT.Identity,
                                                    scale=mod_scale[:, s, k, cond:cond + 1],
                                                    bias=ada[:, l % 2, 24 * s + k, cond:cond + 1])
                    last.then_inc(S["h_ready"], 1)

            act.wait_ge(S["masks_ready"], 1)
            eps_col = sb("eps_col", [P, 2])
            link(nc.scalar.activation(eps_col[:, 0:1], ones[:, 0:1], ACT.Copy, scale=EPS))

            for l in range(DEPTH):
                if l == 0:
                    dense(l, "ada")
                norm(l, 0)
                modulate(l, 0)
                dense(l, "gq", [0])
                act.wait_ge(S["gates_z"], l + 1)
                link(nc.scalar.activation(egate[:, :, :], egate[:, :, :], ACT.Exp, scale=-1.0))
                nc.scalar.activation(coef[:, 8:16], alog[:, l, :], ACT.Exp)
                nc.scalar.activation(beta[:, :, :], gates[:, :, 24:32], ACT.Exp, scale=-1.0)
                nc.scalar.activation(egate[:, :, :], egate[:, :, :], ACT.Ln, bias=1.0).then_inc(S["gates_exp"], 1)

                def conv_sigmoid(j):
                    t0, n = seg_tokens(l, "gq" if j < 4 else "gk")
                    act.wait_ge(S["conv_done"], 12 * l + j + 1)
                    if j >= 2:
                        act.wait_ge(S["conv_out"], 12 * l + j - 1)
                    nc.scalar.activation(work[:, 2 + j % 2, 0:n], work[:, j % 2, 0:n], ACT.Sigmoid).then_inc(S["conv_sig"], 1)

                def l2_root(j):
                    t0, n = seg_tokens(l, "gq" if j < 4 else "gk")
                    act.wait_ge(S["l2_sum"], 8 * l + j + 1)
                    if j >= 2:
                        act.wait_ge(S["l2_out"], 8 * l + j - 1)
                    nc.scalar.activation(work[:, 12 + j % 2, 0:n], bank[6 + j % 2][:, 0:n], ACT.Sqrt,
                                         bias=eps_col[:, 0:1]).then_inc(S["l2_root"], 1)

                for j in range(12):
                    if j > 0:
                        dense(l, ("gq", "gk", "gv")[j // 4], [j % 4])
                    if j >= 1:
                        conv_sigmoid(j - 1)
                    if j >= 4:
                        l2_root(j - 4)
                conv_sigmoid(11)
                for h in range(4):
                    dense(l, "gz", [h])
                    act.wait_ge(S["vt_psum"], 4 * l + h + 1)
                    nc.scalar.copy(gv_tok[:, :, h * P:(h + 1) * P],
                                   bank[4 + h % 2][:, :].rearrange("p (t c) -> p t c", t=NT)).then_inc(S["vt_out"], 1)
                    act.wait_ge(S["kt_psum"], 4 * l + h + 1)
                    nc.scalar.copy(gk_tok[:, :, h * P:(h + 1) * P],
                                   bank[2 + h % 2][:, :].rearrange("p (t c) -> p t c", t=NT)).then_inc(S["kt_out"], 1)

                for p in range(4):
                    g = 4 * l + p
                    for d in range(2):
                        act.wait_ge(G[d]["small"], g + 1)
                        if g > 0:
                            act.wait_ge(G[d]["state"], g)
                        nc.scalar.copy(grow[d], bank[4 * d + 3][0:4, 0:P]).then_inc(G[d]["rows"], 1)
                    for d in range(2):
                        act.wait_ge(G[d]["cols"], g + 1)
                        nc.scalar.activation(gecol[d][:, 0:12], gcol[d][:, 0:12], ACT.Exp).then_inc(G[d]["ecol"], 1)
                    for d in range(2):
                        act.wait_ge(G[d]["arg"], g + 1)
                        for h in range(HEADS):
                            hs = slice(h * P, (h + 1) * P)
                            ins = nc.scalar.activation(slot(d, 0)[:, hs], bank[4 * d][:, hs], ACT.Exp,
                                                       bias=gcol[d][:, 12 + h:13 + h])
                        ins.then_inc(G[d]["decay"], 1)
                    for d in range(2):
                        act.wait_ge(G[d]["t0"], g + 1)
                        nc.scalar.copy(slot(d, 4), bank[4 * d + 3][:, :]).then_inc(G[d]["t1"], 1)
                    for lv in range(1, LEVELS):
                        for d in range(2):
                            act.wait_ge(G[d]["m"], (LEVELS - 1) * g + lv)
                            nc.scalar.copy(parity(slot(d, 5), lv, d), product(4 * d, lv, d))\
                                .then_inc(G[d]["mout"], 1)
                        for pause in (2 * lv - 2, 2 * lv - 1):
                            for n in completed(IN_GAP[(l, p, pause)]):
                                take(n)

                def post_roots(b):
                    for j, t in enumerate(token_tiles(l)):
                        n = post_count(l, b) + j
                        act.wait_ge(S["post_sum"], n + 1)
                        nc.scalar.activation(post_stat[:, t, :], post_stat[:, t, :], ACT.Sqrt, bias=eps_col[:, 0:1],
                                             scale=1.0 / P).then_inc(S["post_root"], 1)

                act.wait_ge(S["mkt_psum"], l + 1)
                nc.scalar.copy(mk_tok[:, 0:2, :].rearrange("p t c -> p (t c)"), bank[2][:, :])
                nc.scalar.copy(mk_tok[:, 2:4, :].rearrange("p t c -> p (t c)"), bank[3][:, :]).then_inc(S["mkt_out"], 1)
                post_roots(2)

                for u, (d, t) in enumerate(UNITS):
                    g = 8 * l + u
                    mcol = mcol_of[:, u % 2, :]
                    o = sofar([len(v) for v in out_units], l) + len([v for v in out_units[l] if v <= u])
                    act.wait_ge(S["ml_rows"], g + 1)
                    nc.scalar.activation(mrow[:, 7, :], mrow[:, 4, :], ACT.Exp).then_inc(S["ml_exp"], 1)
                    act.wait_ge(S["ml_cols"], g + 1)
                    n = 14 if u in out_units[l] else 10
                    nc.scalar.copy(mcol[:, 8:n], bank[5][:, 264:256 + n])
                    nc.scalar.activation(mcol[:, 0:8], bank[5][:, 256:264], ACT.Exp).then_inc(S["ml_ecol"], 1)
                    if u in out_units[l]:
                        act.wait_ge(S["ml_arg"], o)
                        act.wait_ge(S["ml_ecol"], g + 1)
                        for q in range(HEADS):
                            hs = slice(q * P, (q + 1) * P)
                            ins = nc.scalar.activation(work[:, 0, hs], bank[2][:, hs], ACT.Exp, bias=mcol[:, 10 + q:11 + q])
                        ins.then_inc(S["ml_decay"], 1)
                    for n in BESIDE[(l, u)]:
                        take(n)
                post_roots(1)
                act.wait_ge(S["ml_qg"], outputs(l, 7))
                dense(l, "bg", [0])

                steps_a = attn_units(l + 1) - attn_units(l)

                def at_exp(k):
                    g = attn_units(l) + k
                    nk = CTX if token_tiles(l)[k // 4] < 2 else TOK
                    q = g % 2
                    act.wait_ge(S["at_max"], g + 1)
                    if g >= 2:
                        act.wait_ge(S["at_w"], g - 1)
                    for m in range(2):
                        nc.scalar.activation(work[:, 4 * q + m, 0:nk], bank[2 + 4 * q + m][:, 0:nk], ACT.Exp,
                                             bias=amax[:, q, m:m + 1],
                                             accum_out=amax[:, q, 2 + m:3 + m]).then_inc(S["at_e"], 1)

                at_exp(0)
                for k in range(steps_a):
                    g = attn_units(l) + k
                    nk = CTX if token_tiles(l)[k // 4] < 2 else TOK
                    if k + 1 < steps_a:
                        at_exp(k + 1)
                    fill = list(range(32 // steps_a // 2 * k, 32 // steps_a // 2 * (k + 1)))
                    dense(l, "bg", [j for j in fill[:1] if j > 0])
                    act.wait_ge(S["at_wt"], g + 1)
                    nc.scalar.copy(work[:, 4 * (g % 2) + 3, 0:nk], bank[4][:, 0:nk]).then_inc(S["at_wtout"], 1)
                    dense(l, "bg", fill[1:])
                post_roots(0)
                act.wait_ge(S["ada_ready"], 2 * l + 2)

                dense(l, "bg", range(16, 24))
                dense(l, "wo")
                norm(l, 1)
                norm(l, 2)
                modulate(l, 2)
                dense(l, "ff1")
                dense(l, "ff2")
                norm(l, 3)

        @block.vector
        def _(dve):
            steps = [0]

            def link(ins):
                steps[0] += 1
                ins.then_inc(S["dve_step"], 1)
                dve.wait_ge(S["dve_step"], steps[0])

            four = lambda a: a.rearrange("p (h c) -> p h c", h=4)
            wide = lambda a, n=P: a.unsqueeze(2).broadcast_to((P, 4, n))

            def modulation_sum(l, n, start=0, end=KD):
                m, w = modulation_block(dve, l, n)
                acc = ada_sums[:, m % 2, 0, :]
                for k in range(start, end):
                    if k == 0:
                        ins = nc.vector.tensor_scalar(acc, w[:, k, :], silu_c[:, 0, k:k + 1], None, ALU.mult)
                    else:
                        ins = nc.vector.scalar_tensor_tensor(out=acc, in0=w[:, k, :], scalar=silu_c[:, 0, k:k + 1],
                                                             in1=acc, op0=ALU.mult, op1=ALU.add)
                    if k < KD - 1:
                        link(ins)
                    else:
                        ins.then_inc(S["ada_latents"], 1)

            def dense(l, kind, idx=None):
                for n in WHERE[(l, kind)] if idx is None else [WHERE[(l, kind)][k] for k in idx]:
                    take(n)

            def take(n):
                l, kind, i, _, bk, engine, o = SEGS[n]
                if engine != "dve":
                    return
                dve.wait_ge(S["dense_ready"], n + 1)
                ps = bank[bk]
                t0, tn = seg_tokens(l, kind)
                if kind in ("adat", "adam"):
                    at = B_ADA + 2 * i
                    ins = nc.vector.tensor_tensor(ada[:, l % 2, 2 * i:2 * i + 2, :],
                                                  ps[:, 0:4].rearrange("p (j a) -> p j a", a=2),
                                                  cols1[:, l, at:at + 2].unsqueeze(2).broadcast_to((P, 2, 2)), ALU.add)
                elif kind == "gate":
                    ins = nc.vector.tensor_tensor(gates[:, :, :], ps[:, 0:128].rearrange("p (t c) -> p t c", t=NT),
                                                  gate_bias[:, l, :].unsqueeze(1).broadcast_to((P, NT, 32)), ALU.add)
                elif kind == "gz":
                    dve.wait_ge(S["gz_sig"], 4 * l + i + 1)
                    ins = nc.vector.scalar_tensor_tensor(out=gz[:, i, t0:t0 + tn], in0=ps[:, 0:tn],
                                                         scalar=cols1[:, l, B_GZ + i:B_GZ + i + 1],
                                                         in1=work[:, 8 + i % 2, 0:tn], op0=ALU.add, op1=ALU.mult)
                elif kind == "mqk":
                    dst, b, f = (mq, B_MQ, 1.0) if i < 2 else (mk, B_MK, M_QK ** -0.5)
                    ins = nc.vector.tensor_scalar(dst[:, i % 2, :], ps[:, :], cols1[:, l, b + i % 2:b + i % 2 + 1], f,
                                                  ALU.add, ALU.mult)
                elif kind in ("mv", "av"):
                    c, tp = i // 2, i % 2
                    if kind == "mv" and i == 0:
                        dve.wait_ge(S["vbias_in"], 32 * (l + 1))
                        dve.wait_ge(S["conv_done"], 12 * (l + 1))
                    if kind == "mv":
                        dst = mv[:, 2 * tp:2 * tp + 2, 2 * c:2 * c + 2, 0:M_V]
                    else:
                        dst = av[:, 2 * tp:2 * tp + 2, 256 * c:256 * c + 256].rearrange("p t (h c) -> p t h c", h=2)
                    b = v_bias[:, 0 if kind == "mv" else 1, 256 * c:256 * c + 256].rearrange("p (h c) -> p h c", h=2)
                    ins = nc.vector.tensor_tensor(dst, ps[:, :].rearrange("p (t h c) -> p t h c", t=2, h=2),
                                                  b.unsqueeze(1).broadcast_to((P, 2, 2, P)), ALU.add)
                elif kind in ("aq", "ak"):
                    dst, b, f = (aq, B_AQ, A_HD ** -0.5) if kind == "aq" else (ak, B_AK, 1.0)
                    ins = nc.vector.tensor_scalar(dst[:, i, t0:t0 + tn], ps[:, 0:tn], cols1[:, l, b + i:b + i + 1], f,
                                                  ALU.add, ALU.mult)
                elif kind == "by":
                    k = WHERE[(l, "by")].index(n)
                    evacuated(dve, WHERE[(l, "bg")][k])
                    if k >= 10:
                        dve.wait_ge(S["y_ready"], 16 * l + k - 9)
                    dst = merged[:, i[1], 0:tn] if k < 8 else gated[k % 2][:, 0:tn]
                    ins = nc.vector.tensor_tensor(dst, ps[:, 0:tn], gate_sig[k % 2][:, 0:tn], ALU.mult)
                ins.then_inc(S["taken_dve"], 1)

            dve.wait_ge(S["csig"], 1)
            nc.vector.tensor_tensor(silu_c[:, :, :].rearrange("p a k -> p (a k)"),
                                    silu_c[:, :, :].rearrange("p a k -> p (a k)"), cols1[:, 0, R_C:R_C + 16],
                                    ALU.mult).then_inc(S["silu_ready"], 1)
            dve.wait_ge(S["x_in"], 16 * 3)
            dve.wait_ge(S["consts_in"], 16 * 2)
            dve.wait_ge(S["params_in"], 16 * 12)
            nc.vector.tensor_copy(cm[:, :, :, :].rearrange("p a b c -> p (a b c)"), level_masks)
            nc.vector.tensor_copy(cb[:, :, :].rearrange("p a c -> p (a c)"), work[:, 8, 0:3 * P]).then_inc(S["masks_ready"], 1)
            dve.wait_ge(S["slots_set"], 2)
            lam_prod = work[:, 9, 0:DEPTH * 2 * A_HD].rearrange("p (l m c) -> p l m c", l=DEPTH, m=2)
            for l in range(DEPTH):
                for m in range(2):
                    link(nc.vector.tensor_tensor(lam_prod[:, l, m, :], lamv[:, l, 2 * m, :], lamv[:, l, 2 * m + 1, :], ALU.mult))
            nc.vector.tensor_reduce(lam2[:, :, :], lam_prod, op=ALU.add, axis=AX_X).then_inc(S["lam_sum"], 1)
            dve.wait_ge(S["lam_exp"], 1)
            for l in range(DEPTH):
                lam_init = 0.8 - 0.6 * math.exp(-0.3 * l)
                link(nc.vector.tensor_tensor(nlam[:, l:l + 1], lam2[:, l, 1:2], lam2[:, l, 0:1], ALU.subtract))
                link(nc.vector.tensor_scalar(nlam[:, l:l + 1], nlam[:, l:l + 1], -lam_init, None, ALU.add))
            nc.vector.memset(coef[:, 0:8], -1.0)

            def root_to_rstd(l, which):
                t0, n = (0, TOK) if which == 0 else tokens(l)
                dve.wait_ge(S["norm_root"], norm_count(l, which) + 1)
                link(nc.vector.reciprocal(rstd[:, 0:n], rstd[:, 0:n]))

            def normed(l, which):
                t0, n = (0, TOK) if which == 0 else tokens(l)
                root_to_rstd(l, which)
                for k in range(KD):
                    nc.vector.tensor_tensor(work[:, k, 0:n], xt[:, k, t0:t0 + n], rstd[:, 0:n], ALU.mult)\
                        .then_inc(S["scaled_ready"], 1)

            def residual(l, which):
                t0, n = tokens(l)
                total = work[:, 0 if which == 1 else 10, 0:n]
                for k in range(KD):
                    m = KD * norm_count(l, which) + k
                    dve.wait_ge(S["sq_ready"], m + 1)
                    sq = work[:, 8 + k % 2, 0:n]
                    if k == 0:
                        ins = nc.vector.tensor_copy(total, sq)
                    else:
                        dve.wait_ge(S["sq_used"], m)
                        ins = nc.vector.tensor_tensor(total, total, sq, ALU.add)
                    ins.then_inc(S["sq_used"], 1)
                root_to_rstd(l, which)
                evacuated(dve, seg_of(l, "wo" if which == 1 else "ff2"))
                ot = ot_of[which]
                done = KD * (2 * l + which // 2)
                for k in range(KD):
                    nc.vector.tensor_tensor(ot[:, k, 0:n], ot[:, k, 0:n], rstd[:, 0:n], ALU.mult).then_inc(S["res_scaled"], 1)
                    if k % 2 == 1:
                        dve.wait_ge(S["res_scaled"], done + k)
                        nc.vector.tensor_tensor(xt[:, k - 1, t0:t0 + n], xt[:, k - 1, t0:t0 + n], ot[:, k - 1, 0:n], ALU.add)\
                            .then_inc(S["res_ready"], 1)
                residual_done(dve, 2 * l + which // 2 + 1)

            for l in range(DEPTH):
                def gain(k):
                    return cols2[:, l, R_GAIN + 8 * k:R_GAIN + 8 * k + 8].unsqueeze(2).broadcast_to((P, KD, 2))

                def scale_columns(s):
                    link(nc.vector.tensor_scalar(mod_scale[:, s, :, :], ada[:, l % 2, 24 * s + 8:24 * s + 16, :], 1.0, None,
                                                 ALU.add))
                    return nc.vector.tensor_tensor(mod_scale[:, s, :, :], mod_scale[:, s, :, :], gain(2 * s), ALU.mult)

                if l == 0:
                    dense(l, "adat")
                evacuated(dve, last_columns(l, True))
                scale_columns(0).then_inc(S["ada_ready"], 1)
                normed(l, 0)

                dense(l, "gate")
                evacuated(dve, seg_of(l, "gate"))
                two = lambda a: a.unsqueeze(1).broadcast_to((P, NT, a.shape[1]))
                for d in range(2):
                    link(nc.vector.scalar_tensor_tensor(out=zgate[:, :, 4 * d:4 * d + 4], in0=gates[:, :, 8 * d + 4:8 * d + 8],
                                                        scalar=-1.0, in1=two(fdt_bias[:, l, 4 * d:4 * d + 4]),
                                                        op0=ALU.mult, op1=ALU.subtract))
                link(nc.vector.tensor_tensor(zgate[:, :, 8:16], gates[:, :, 16:24], two(fdt_bias[:, l, 8:16]), ALU.add))
                nc.vector.scalar_tensor_tensor(out=egate[:, :, :], in0=zgate[:, :, :], scalar=-1.0, in1=zgate[:, :, :],
                                               op0=ALU.mult, op1=ALU.max).then_inc(S["gates_z"], 1)
                dve.wait_ge(S["gates_exp"], l + 1)
                link(nc.vector.tensor_scalar(coef[:, 8:16], coef[:, 8:16], -1.0, None, ALU.mult))
                link(nc.vector.scalar_tensor_tensor(out=lgate[:, :, :], in0=zgate[:, :, :], scalar=0.0, in1=egate[:, :, :],
                                                    op0=ALU.max, op1=ALU.add))
                link(nc.vector.tensor_tensor(lgate[:, :, :], lgate[:, :, :], two(coef[:, :]), ALU.mult))
                link(nc.vector.tensor_scalar(beta[:, :, :], beta[:, :, :], 1.0, None, ALU.add))
                link(nc.vector.reciprocal(beta[:, :, :], beta[:, :, :]))
                nc.vector.tensor_scalar(nbeta[:, :, :], beta[:, :, :], -1.0, None, ALU.mult).then_inc(S["gates_ready"], 1)
                dve.wait_ge(S["gates_ready"], l + 1)

                def conv(j):
                    t0, n = seg_tokens(l, "gq" if j < 4 else "gk")
                    s0, sn = t0 // CTX, n // CTX
                    seg = seg_of(l, ("gq", "gk", "gv")[j // 4], j % 4)
                    evacuated(dve, seg)
                    if j == 0:
                        dve.wait_ge(S["h_ready"], 2 * KD * l + KD)
                    if j >= 2:
                        dve.wait_ge(S["conv_out"], 12 * l + j - 1)
                    acc = work[:, j % 2, 0:n].rearrange("p (s c) -> p s c", s=sn)
                    tap = lambda k: cols2[:, l, R_CONV + 12 * k + j:R_CONV + 12 * k + j + 1]
                    src = lambda k: raw[:, j % 3, s0:s0 + sn, k:k + CTX]
                    link(nc.vector.tensor_scalar(acc, src(0), tap(0), None, ALU.mult))
                    for k in range(1, CONV_K):
                        ins = nc.vector.scalar_tensor_tensor(out=acc, in0=src(k), scalar=tap(k), in1=acc,
                                                             op0=ALU.mult, op1=ALU.add)
                        if k < CONV_K - 1:
                            link(ins)
                    ins.then_inc(S["conv_done"], 1)

                def conv_silu(j):
                    t0, n = seg_tokens(l, "gq" if j < 4 else "gk")
                    dve.wait_ge(S["conv_sig"], 12 * l + j + 1)
                    dst = (gq[:, j % 4, t0:t0 + n], gk[:, j % 4, t0:t0 + n], work[:, 4 + j % 4, 0:n])[j // 4]
                    nc.vector.tensor_tensor(dst, work[:, j % 2, 0:n], work[:, 2 + j % 2, 0:n], ALU.mult)\
                        .then_inc(S["conv_out"], 1)

                def l2_scale(j):
                    t0, n = seg_tokens(l, "gq" if j < 4 else "gk")
                    dst = (gq if j < 4 else gk)[:, j % 4, t0:t0 + n]
                    r = work[:, 12 + j % 2, 0:n]
                    dve.wait_ge(S["l2_root"], 8 * l + j + 1)
                    link(nc.vector.reciprocal(r, r))
                    nc.vector.scalar_tensor_tensor(out=dst, in0=dst, scalar=G_HD ** -0.5 if j < 4 else 1.0, in1=r,
                                                   op0=ALU.mult, op1=ALU.mult).then_inc(S["l2_out"], 1)

                for j in range(12):
                    conv(j)
                    if j >= 1:
                        conv_silu(j - 1)
                    if j >= 4:
                        l2_scale(j - 4)
                conv_silu(11)
                dense(l, "gz")

                for p in range(4):
                    g = 4 * l + p
                    o = gd_outs(l, p)
                    for d in range(2):
                        small = bank[4 * d + 3]
                        dve.wait_ge(G[d]["rows"], g + 1)
                        link(nc.vector.tensor_copy(gcol[d][:, 0:4], small[:, 128:132]))
                        nc.vector.tensor_scalar(gcol[d][:, 12:16], small[:, 128:132], -1.0, None, ALU.mult)
                        nc.vector.tensor_copy(gcol[d][:, 8:12], small[:, 132:136])
                        nc.vector.tensor_tensor(gcol[d][:, 4:8], small[:, 132:136], gcol[d][:, 0:4], ALU.subtract)\
                            .then_inc(G[d]["cols"], 1)
                    for d in range(2):
                        dve.wait_ge(G[d]["ecol"], g + 1)
                        nc.vector.tensor_scalar(gecol[d][:, 12:16], gecol[d][:, 0:4], -1.0, None, ALU.mult)\
                            .then_inc(G[d]["neg"], 1)
                    for d in range(2):
                        t = CHUNK_OF[d][p]
                        dve.wait_ge(G[d]["decay"], g + 1)
                        for h in range(HEADS):
                            hs = slice(h * P, (h + 1) * P)
                            ins = nc.vector.scalar_tensor_tensor(out=slot(d, 1)[:, hs], in0=bank[4 * d + 1][:, hs],
                                                                 scalar=nbeta[:, t, 4 * d + h:4 * d + h + 1],
                                                                 in1=slot(d, 0)[:, hs], op0=ALU.mult, op1=ALU.mult)
                        ins.then_inc(G[d]["b"], 1)
                    for d in range(2):
                        t = CHUNK_OF[d][p]
                        dve.wait_ge(G[d]["ks"], g + 1)
                        if d == 0:
                            for a in range(2):
                                dve.wait_ge(G[a]["neg"], g + 1)
                        for h in range(HEADS):
                            hs = slice(h * P, (h + 1) * P)
                            ins = nc.vector.scalar_tensor_tensor(out=slot(d, 6)[:, hs], in0=bank[4 * d + 3][:, hs],
                                                                 scalar=gecol[d][:, 12 + h:13 + h],
                                                                 in1=gv_tok[:, t, hs], op0=ALU.mult, op1=ALU.add)
                        ins.then_inc(G[d]["r"], 1)
                    for d in range(2):
                        dve.wait_ge(G[d]["eye"], g + 1)
                        dve.wait_ge(G[d]["b"], g + 1)
                        nc.vector.copy_predicated(four(slot(d, 3)), cm[:, d, 0, :].unsqueeze(1).broadcast_to((P, HEADS, P)),
                                                  four(slot(d, 1))).then_inc(G[d]["u0"], 1)
                    if gd_gives(l, p):
                        for d in range(2):
                            dve.wait_ge(G[d]["qk"], o)
                            nc.vector.tensor_tensor(slot(d, 2), bank[4 * d + 2][:, :], slot(d, 0), ALU.mult)\
                                .then_inc(G[d]["qkd"], 1)
                    if gd_gives(l, p):
                        for d in range(2):
                            t = CHUNK_OF[d][p]
                            dve.wait_ge(G[d]["qs"], o)
                            ins = nc.vector.tensor_tensor(four(slot(d, 8)), four(bank[4 * d + 2][:, :]),
                                                          wide(gecol[d][:, 0:4]), ALU.mult)
                            ins.then_inc(G[d]["qg"], 1)
                        if p % 2 == 1:
                            for d in range(2):
                                t = CHUNK_OF[d][p]
                                dve.wait_ge(G[d]["qg"], o)
                                dve.wait_ge(G[1 - d]["oacc"], o - 1)
                                link(nc.vector.tensor_tensor(slot(d, 8), slot(d, 8), oacc[:, t, :], ALU.add))
                    for d in range(2):
                        dve.wait_ge(G[d]["t1"], g + 1)
                    for lv in range(1, LEVELS):
                        k = (LEVELS - 1) * g + lv
                        for n in completed(IN_GAP[(l, p, 2 * lv - 2)]):
                            take(n)
                        for d in range(2):
                            mask = lambda side, q: cm[:, side, lv, :].rearrange(
                                "p (b q s) -> p b q s", q=2, s=2 ** lv)[:, :, q, :].unsqueeze(1)\
                                .broadcast_to((P, HEADS, P >> (lv + 1), 2 ** lv))
                            if lv < LEVELS - 1:
                                dve.wait_ge(G[d]["t"], (LEVELS - 2) * g + lv)
                                nc.vector.copy_predicated(parity(slot(d, 4), lv, d), mask(1 - d, d),
                                                          product(4 * d + 3, lv, d)).then_inc(G[d]["tout"], 1)
                            dve.wait_ge(G[d]["u"], k)
                            nc.vector.copy_predicated(parity(slot(d, 3), lv, 1 - d), mask(d, 1 - d),
                                                      product(4 * d + 1, lv, 1 - d)).then_inc(G[d]["uout"], 1)
                        for z in range(4 * (lv - 1), 4 * lv, 2):
                            modulation_sum(l, ADA_NOW + 4 * p + z // 6, 4 * (z % 6) // 3, 4 * (z % 6 + 2) // 3)
                        for n in completed(IN_GAP[(l, p, 2 * lv - 1)]):
                            take(n)
                    for d in range(2):
                        t = CHUNK_OF[d][p]
                        dve.wait_ge(G[d]["v"], g + 1)
                        nc.vector.tensor_tensor(four(slot(d, 5)), four(bank[4 * d][:, :]), wide(beta[:, t, 4 * d:4 * d + 4]),
                                                ALU.mult).then_inc(G[d]["vn"], 1)
                    for d in range(2):
                        t = CHUNK_OF[d][p]
                        if gd_gives(l, p):
                            dve.wait_ge(G[d]["o"], o)
                            dve.wait_ge(G[d]["qg"], o)
                            ins = nc.vector.tensor_tensor(oacc[:, t, :], bank[4 * d + 2][:, :], slot(d, 8), ALU.add)
                            ins.then_inc(G[d]["oacc"], 1)
                        dve.wait_ge(G[d]["s"], g + 1)
                        for h in range(HEADS):
                            ins = nc.vector.scalar_tensor_tensor(out=gstate[:, d, h, :], in0=gstate[:, d, h, :],
                                                                 scalar=gecol[d][:, 8 + h:9 + h],
                                                                 in1=bank[4 * d][:, h * P:(h + 1) * P],
                                                                 op0=ALU.mult, op1=ALU.add)
                        ins.then_inc(G[d]["state"], 1)
                        dve.wait_ge(G[d]["state"], g + 1)
                for d in range(2):
                    dve.wait_ge(G[d]["oacc"], gd_outs(l, 3))
                def rows(u):
                    g = 8 * l + u
                    d = UNITS[u][0]
                    end = P - 1 if d == 0 else 0
                    R = lambda r: mrow[:, r, :]
                    fwd = lambda a: a if d == 0 else a[:, ::-1]
                    dve.wait_ge(S["ml_small"], g + 1)
                    if u > 0:
                        dve.wait_ge(S["ml_cols"], g)
                        if outputs(l, u - 1) > 0:
                            dve.wait_ge(S["ml_qb"], outputs(l, u - 1))
                    elif l > 0:
                        dve.wait_ge(S["states_zero"], 2 * l + 2)
                    link(nc.vector.tensor_copy(R(0), bank[5][0:4, 128:256]))
                    link(nc.vector.tensor_tensor(R(1), bank[5][0:4, 0:128], R(0), ALU.subtract))
                    link(nc.vector.tensor_tensor_scan(fwd(R(2)), fwd(R(1)), fwd(R(1)), mmax[:, d:d + 1], ALU.max, ALU.max))
                    nc.vector.tensor_scalar(R(3), R(2), -1.0, None, ALU.mult)
                    nc.vector.tensor_scalar(R(4), R(2), -1.0, mmax[:, d:d + 1], ALU.mult, ALU.add)
                    link(nc.vector.scalar_tensor_tensor(out=R(5), in0=R(2), scalar=-1.0, in1=R(0), op0=ALU.mult, op1=ALU.subtract))
                    link(nc.vector.tensor_tensor(mmax[:, d:d + 1], R(0)[:, end:end + 1], R(2)[:, end:end + 1], ALU.add))
                    nc.vector.tensor_scalar(R(6), R(1), R(2)[:, end:end + 1], None, ALU.subtract).then_inc(S["ml_rows"], 1)

                def post(b, beside=()):
                    tiles = token_tiles(l)
                    for j, t in enumerate(tiles):
                        dve.wait_ge(S["post_sq"], post_count(l, b) + j + 1)
                        nc.vector.tensor_reduce(post_stat[:, t, :], four(work[:, 8 + j % 2, :]), op=ALU.add, axis=AX_X)\
                            .then_inc(S["post_sum"], 1)
                    if b == 2:
                        rows(0)
                    for n in beside:
                        take(n)
                    for j, t in enumerate(tiles):
                        n = post_count(l, b) + j
                        dve.wait_ge(S["post_root"], n + 1)
                        link(nc.vector.reciprocal(post_stat[:, t, :], post_stat[:, t, :]))
                        nc.vector.tensor_tensor(four(oacc[:, t, :]), four(oacc[:, t, :]), wide(post_stat[:, t, :]), ALU.mult)\
                            .then_inc(S["post_norm"], 1)
                    for j, t in enumerate(tiles):
                        n = post_count(l, b) + j
                        dve.wait_ge(S["post_tr"], n + 1)
                        ps = bank[6 + j % 2]
                        ts = slice(t * P, (t + 1) * P)
                        if b == 2:
                            ins = nc.vector.scalar_tensor_tensor(out=gz[:, :, ts], in0=four(ps[:, :]),
                                                                 scalar=cols2[:, l, R_GN:R_GN + 1], in1=gz[:, :, ts],
                                                                 op0=ALU.mult, op1=ALU.mult)
                        elif b == 1:
                            for h in range(HEADS):
                                ins = nc.vector.scalar_tensor_tensor(out=mo[:, h, ts], in0=ps[:, h * P:(h + 1) * P],
                                                                     scalar=cols2[:, l, R_MN + h:R_MN + h + 1],
                                                                     in1=mo[:, h, ts], op0=ALU.mult, op1=ALU.mult)
                        else:
                            lam_init = 0.8 - 0.6 * math.exp(-0.3 * l)
                            ins = nc.vector.tensor_scalar(aq[:, :, ts], four(ps[:, :]), cols2[:, l, R_AN:R_AN + 1],
                                                          1.0 - lam_init, ALU.mult, ALU.mult)
                        ins.then_inc(S["post_out"], 1)
                post(2, BESIDE[(l, -1)])

                link(nc.vector.memset(mstate, 0.0))
                for u, (d, t) in enumerate(UNITS):
                    g = 8 * l + u
                    gives = u in out_units[l]
                    o = outputs(l, u)
                    mcol = mcol_of[:, u % 2, :]
                    dve.wait_ge(S["ml_ecol"], g + 1)
                    if u == 0:
                        dve.wait_ge(S["mkt_out"], l + 1)
                    keys = mk_tok[:, t, :].rearrange("p (h c) -> p h c", h=4)
                    kw = work[:, 3, 0:256].rearrange("p (h c) -> p h c", h=4)
                    nc.vector.tensor_tensor(kw, keys, wide(mcol[:, 4:8], M_QK), ALU.mult).then_inc(S["ml_kw"], 1)
                    if gives:
                        dve.wait_ge(S["ml_qb"], o)
                        nc.vector.tensor_tensor(work[:, 2, 0:256].rearrange("p (i c) -> p i c", i=2),
                                                mq[:, :, t * P:(t + 1) * P],
                                                bank[7][:, 0:256].rearrange("p (i c) -> p i c", i=2), ALU.mult)\
                            .then_inc(S["ml_qg"], 1)
                        dve.wait_ge(S["ml_decay"], o)
                        dve.wait_ge(S["ml_qk"], o)
                        nc.vector.tensor_tensor(work[:, 1, 0:256], bank[3][:, 0:256], work[:, 0, 0:256], ALU.mult)
                        nc.vector.tensor_tensor(work[:, 1, 256:512], bank[6][:, 0:256], work[:, 0, 256:512], ALU.mult)\
                            .then_inc(S["ml_p"], 1)
                    if l + 1 < DEPTH:
                        modulation_sum(l + 1, u)
                    for j, n in enumerate(BESIDE[(l, u)]):
                        take(n)
                        if j == 0 and u < 7:
                            rows(u + 1)
                    if gives:
                        dve.wait_ge(S["ml_num"], o)
                        num = [bank[4 + 2 * i][:, 0:258].rearrange("p (h c) -> p h c", h=2) for i in range(2)]
                        nc.vector.tensor_copy(mden[:, 0:2], num[0][:, :, M_V])
                        link(nc.vector.tensor_copy(mden[:, 2:4], num[1][:, :, M_V]))
                        link(nc.vector.scalar_tensor_tensor(out=mden[:, 4:8], in0=mden[:, 0:4], scalar=-1.0, in1=mden[:, 0:4],
                                                            op0=ALU.mult, op1=ALU.max))
                        link(nc.vector.tensor_tensor(mden[:, 4:8], mden[:, 4:8], mcol[:, 0:4], ALU.max))
                        link(nc.vector.reciprocal(mden[:, 4:8], mden[:, 4:8]))
                        for i in range(2):
                            r = mden[:, 4 + 2 * i:6 + 2 * i].unsqueeze(2).broadcast_to((P, 2, P))
                            acc = oacc[:, t, :].rearrange("p (k r c) -> p r k c", k=2, r=2)[:, i]
                            if u in FIRST_VISIT:
                                ins = nc.vector.tensor_tensor(acc, num[i][:, :, 0:M_V], r, ALU.mult)
                            else:
                                tmp = work[:, 4, 256 * i:256 * i + 256].rearrange("p (h c) -> p h c", h=2)
                                link(nc.vector.tensor_tensor(tmp, num[i][:, :, 0:M_V], r, ALU.mult))
                                ins = nc.vector.tensor_tensor(acc, acc, tmp, ALU.add)
                            ins.then_inc(S["ml_h"], 1)
                    dve.wait_ge(S["ml_c"], g + 1)
                    for i in range(2):
                        ins = nc.vector.scalar_tensor_tensor(out=mstate[:, d, i, :], in0=mstate[:, d, i, :],
                                                             scalar=mcol[:, 8 + i:9 + i],
                                                             in1=mlstm_c(i),
                                                             op0=ALU.mult, op1=ALU.add)
                    ins.then_inc(S["ml_state"], 1)
                    if gives:
                        dve.wait_ge(S["ml_h"], 2 * o)
                    dve.wait_ge(S["ml_state"], g + 1)
                post(1)

                evacuated(dve, last_columns(l, False))
                for s in range(2):
                    link(nc.vector.tensor_tensor(out_gate[:, s, :, :], ada[:, l % 2, 24 * s + 16:24 * s + 24, :],
                                                 gain(2 * s + 1), ALU.mult))
                scale_columns(1).then_inc(S["ada_ready"], 1)
                for n in BESIDE[(l, 8)]:
                    take(n)

                for j in range(8):
                    dst = (aq if j < 4 else ak)[:, j % 4, CTX:TOK]
                    n = 8 * l + j
                    dve.wait_ge(S["rope_psum"], n + 1)
                    link(nc.vector.tensor_tensor(dst, dst, cos_t, ALU.mult))
                    link(nc.vector.tensor_tensor(work[:, 4, 0:256], bank[4 + j % 2][:, 0:256], sin_t, ALU.mult))
                    nc.vector.tensor_tensor(dst, dst, work[:, 4, 0:256], ALU.add).then_inc(S["rope_out"], 1)

                steps_a = attn_units(l + 1) - attn_units(l)

                def at_max(k):
                    g = attn_units(l) + k
                    nk = CTX if token_tiles(l)[k // 4] < 2 else TOK
                    q = g % 2
                    dve.wait_ge(S["at_s"], g + 1)
                    for m in range(2):
                        ins = nc.vector.tensor_reduce(amax[:, q, m:m + 1], bank[2 + 4 * q + m][:, 0:nk], op=ALU.max,
                                                      axis=AX_X, negate=True)
                    ins.then_inc(S["at_max"], 1)

                def at_take(k):
                    g = attn_units(l) + k
                    t, h = token_tiles(l)[k // 4], k % 4
                    dve.wait_ge(S["at_o"], g + 1)
                    nc.vector.tensor_copy(oacc[:, t, h * P:(h + 1) * P], bank[5][:, 0:P]).then_inc(S["at_oout"], 1)

                at_max(0)
                for k in range(steps_a):
                    g = attn_units(l) + k
                    nk = CTX if token_tiles(l)[k // 4] < 2 else TOK
                    q = g % 2
                    st = amax[:, q, :]
                    e0, e1, w = work[:, 4 * q, 0:nk], work[:, 4 * q + 1, 0:nk], work[:, 4 * q + 2, 0:nk]
                    if k + 1 < steps_a:
                        at_max(k + 1)
                    dve.wait_ge(S["at_e"], 2 * g + 2)
                    link(nc.vector.reciprocal(st[:, 4:6], st[:, 2:4]))
                    link(nc.vector.tensor_tensor(st[:, 6:7], st[:, 5:6], nlam[:, l:l + 1], ALU.mult))
                    link(nc.vector.tensor_scalar(e1, e1, st[:, 6:7], None, ALU.mult))
                    if g >= 2:
                        dve.wait_ge(S["at_wt"], g - 1)
                    nc.vector.scalar_tensor_tensor(out=w, in0=e0, scalar=st[:, 4:5], in1=e1,
                                                   op0=ALU.mult, op1=ALU.add).then_inc(S["at_w"], 1)
                    for j in range(32 // steps_a // 2 * k, 32 // steps_a // 2 * (k + 1)):
                        dense(l, "by", [j])
                    at_take(k)
                dve.wait_ge(S["at_oout"], attn_units(l + 1))
                post(0)

                dense(l, "by", range(16, 24))
                residual(l, 1)
                normed(l, 2)
                residual(l, 3)

            for n in range(4):
                dve.wait_ge(S["final_psum"], n + 1)
                nc.vector.tensor_copy(work[:, n, :], bank[2 + n][:, :]).then_inc(S["final_out"], 1)

        @block.tensor
        def _(pe):
            mm = nc.tensor.matmul

            def chunk_arrived(n):
                pe.wait_ge(S[f"chunk_in{n % RING}"], 16 * (n // RING + 1))

            def bank_free(n):
                for m in range(n - 1, -1, -1):
                    if SEGS[m][4] == SEGS[n][4]:
                        if SEGS[m][5] is not None:
                            evacuated(pe, m)
                        return

            def dense(l, kind, idx=None):
                for n in WHERE[(l, kind)] if idx is None else [WHERE[(l, kind)][k] for k in idx]:
                    segment(n)

            def segment(n, start=0, end=4):
                l, kind, i, ch, bk, engine, _ = SEGS[n]
                ps = bank[bk]
                t0, tn = seg_tokens(l, kind)
                if start == 0:
                    bank_free(n)
                if ch is not None and kind != "adam":
                    chunk_arrived(ch)
                    k_of = 4 if kind == "by" else 8
                    w = ring[:, ch % RING, :].rearrange("p (k n) -> p k n", k=k_of)
                if kind == "ada":
                    for k in range(2 * start, 2 * end):
                        last = mm(ps[0:2, 0:256], silu_c[:, :, k], w[:, k, :], start=k == 0, stop=k == KD - 1)
                elif kind == "adat":
                    evacuated(pe, seg_of(l, "ada", i))
                    for q in range(2):
                        last = mm(ps[:, 2 * q:2 * q + 2], ada_rows[:, i % 2, q * P:(q + 1) * P], ident[0:2, 0:2],
                                  start=True, stop=True)
                elif kind == "adam":
                    m = sum(SEGS[k][1] == "adam" for k in range(n))
                    pe.wait_ge(S["ada_latents"], m + 1)
                    pe.wait_ge(S["ada_context"], m + 1)
                    for q in range(2):
                        for a in range(2):
                            last = mm(ps[:, 2 * q + a:2 * q + a + 1], ada_sums[:, m % 2, a, q * P:(q + 1) * P], ones[:, 0:1],
                                      start=True, stop=True)
                elif kind == "gate":
                    pe.wait_ge(S["gatew_in"], 32 * (l + 1))
                    for t in range(NT):
                        for k in range(KD):
                            last = mm(ps[:, 32 * t:32 * t + 32], ht[:, k, t * P:(t + 1) * P], w_gates[:, k, :],
                                      start=k == 0, stop=k == KD - 1)
                elif kind in ("mv", "av"):
                    for a in range(2):
                        t = 2 * (i % 2) + a
                        for k in range(KD):
                            if not 4 * start <= a * KD + k < 4 * end:
                                continue
                            last = mm(ps[:, a * 256:(a + 1) * 256], ht[:, k, t * P:(t + 1) * P], w[:, k, :],
                                      start=k == 0, stop=k == KD - 1)
                elif kind in ("gq", "gk", "gv", "gz", "mqk", "mo", "aq", "ak", "bg", "ff1"):
                    q = (i[1] if kind == "bg" else i) % 2
                    for k in range(2 * start, 2 * end):
                        if i == 0 and kind in ("gq", "ff1"):
                            pe.wait_ge(S["h_ready"], 2 * KD * l + (KD if kind == "ff1" else 0) + k + 1)
                        last = mm(ps[:, 0:tn], w[:, k, q * P:(q + 1) * P], ht[:, k, t0:t0 + tn],
                                  start=k == 0, stop=k == KD - 1)
                elif kind == "by":
                    b, cc = i
                    y = {2: gz, 1: mo, 0: aq}[b]
                    pe.wait_ge(S["post_out"], post_count(l, b) + len(token_tiles(l)))
                    for k in range(4):
                        last = mm(ps[:, 0:tn], w[:, k, (cc % 4) * P:(cc % 4 + 1) * P], y[:, k, t0:t0 + tn],
                                  start=k == 0, stop=k == 3)
                elif kind == "wo":
                    q = i % 2
                    pe.wait_ge(S["y_ready"], 16 * (l + 1))
                    for k in range(KD):
                        last = mm(ps[:, 0:tn], w[:, k, q * P:(q + 1) * P], merged[:, k, 0:tn],
                                  start=k == 0, stop=k == KD - 1)
                elif kind == "ff2":
                    nb, kc, q = i
                    pe.wait_ge(S["hid_ready"], FT * l + 8 * kc + 8)
                    for k in range(KD):
                        last = mm(ps[:, 0:tn], w[:, k, q * P:(q + 1) * P], hidden[:, 8 * kc + k, 0:tn],
                                  start=kc == 0 and k == 0, stop=kc == 3 and k == KD - 1)
                if end == 4:
                    last.then_inc(S["dense_ready"], 1)

            pe.wait_ge(S["x_in"], 16 * 3)
            pe.wait_ge(S["rows_in"], 16 * 22)
            for l in range(DEPTH):
                nc.tensor.transpose(bank[2 + 2 * l][:, 0:P], rows1[:, l, :], ident).then_inc(S["cols_psum"], 1)
                nc.tensor.transpose(bank[3 + 2 * l][:, 0:98], rows2[0:98, l, :], ident[0:98, 0:98]).then_inc(S["cols_psum"], 1)
            pe.wait_ge(S["cols_ready"], 4)
            x_tok = ht[:, :, :].rearrange("p (t a) c -> p t (a c)", t=NT)
            for k in range(KD):
                if k >= 4:
                    pe.wait_ge(S["xtr_ready"], k - 3)
                for t in range(NT):
                    last = nc.tensor.transpose(bank[4 + k % 4][:, t * P:(t + 1) * P], x_tok[:, t, k * P:(k + 1) * P], ident)
                last.then_inc(S["xtr_psum"], 1)
            pe.wait_ge(S["xtr_ready"], KD)
            pe.wait_ge(S["masks_ready"], 1)
            pe.wait_ge(S["silu_ready"], 1)
            pe.wait_ge(S["ones_set"], 1)

            def norm(l, which):
                for k in range(KD):
                    norm_sum(l, which, k)

            def output_sum(l, which):
                n = tokens(l)[1]
                pe.wait_ge(S["sq_used"], KD * norm_count(l, which) + KD)
                mm(bank[7][:, 0:n], ones[:, :], work[:, 0 if which == 1 else 10, 0:n], start=True, stop=True)\
                    .then_inc(S["out_sum"], 1)

            def norm_sum(l, which, k):
                n = TOK if which == 0 else tokens(l)[1]
                m = KD * norm_count(l, which) + k
                pe.wait_ge(S["sq_ready"], m + 1)
                mm(bank[7][:, 0:n], ones[:, :], work[:, 8 + k % 2, 0:n], start=k == 0, stop=k == KD - 1)\
                    .then_inc(S["sq_used"], 1)

            for l in range(DEPTH):
                if l == 0:
                    for n in range(WHERE[(0, "gq")][0]):
                        segment(n)
                norm(l, 0)
                def l2_sum(j):
                    n = seg_tokens(l, "gq" if j < 4 else "gk")[1]
                    pe.wait_ge(S["l2_sq"], 8 * l + j + 1)
                    if j >= 2:
                        pe.wait_ge(S["l2_root"], 8 * l + j - 1)
                    mm(bank[6 + j % 2][:, 0:n], ones[:, :], work[:, 10 + j % 2, 0:n], start=True, stop=True).then_inc(S["l2_sum"], 1)

                for j in range(12):
                    dense(l, ("gq", "gk", "gv")[j // 4], [j % 4])
                    if j == 0:
                        dense(l, "gate")
                    if 3 <= j < 11:
                        l2_sum(j - 3)
                for h in range(4):
                    dense(l, "gz", [h])
                    pe.wait_ge(S["conv_out"], 12 * l + 9 + h)
                    if h >= 2:
                        pe.wait_ge(S["vt_out"], 4 * l + h - 1)
                    for t in range(NT):
                        last = nc.tensor.transpose(bank[4 + h % 2][:, t * P:(t + 1) * P], work[:, 4 + h, t * P:(t + 1) * P], ident)
                    last.then_inc(S["vt_psum"], 1)
                    pe.wait_ge(S["l2_out"], 8 * l + 5 + h)
                    if h >= 2:
                        pe.wait_ge(S["kt_out"], 4 * l + h - 1)
                    for t in range(NT):
                        last = nc.tensor.transpose(bank[2 + h % 2][:, t * P:(t + 1) * P], gk[:, h, t * P:(t + 1) * P], ident)
                    last.then_inc(S["kt_psum"], 1)
                pe.wait_ge(S["kt_out"], 4 * l + 4)
                pe.wait_ge(S["vt_out"], 4 * l + 4)
                pe.wait_ge(S["gates_ready"], l + 1)
                pe.wait_ge(S["states_zero"], 2 * l + 2)
                pe.wait_ge(S["slots_set"], 2)
                evacuated(pe, seg_of(l, "gz", 2))
                evacuated(pe, seg_of(l, "gz", 3))

                H = lambda h: slice(h * P, (h + 1) * P)
                C = lambda h, lv: H(h) if lv == 1 else slice(h * 64, (h + 1) * 64)
                half = lambda a, lv, q: a if lv == 1 else a.rearrange("p (b q s) -> p b q s", q=2, s=2 ** lv)[:, :, q, :]
                for p in range(4):
                    g = 4 * l + p
                    o = gd_outs(l, p)
                    gives = gd_gives(l, p)
                    for d in range(2):
                        t = CHUNK_OF[d][p]
                        ts = slice(t * P, (t + 1) * P)
                        log_g = lgate[:, t, 8 + 4 * d:12 + 4 * d]
                        small = bank[4 * d + 3]
                        mm(small[0:4, 0:P], log_g, tri[d], start=True, stop=True)
                        mm(small[:, 128:132], tri[d], log_g, start=True, stop=True)
                        mm(small[:, 132:136], ones[:, :], log_g, start=True, stop=True).then_inc(G[d]["small"], 1)
                        for h in range(HEADS):
                            mm(bank[4 * d + 1][:, H(h)], gk[:, h, ts], gk[:, h, ts], start=True, stop=True)
                    for d in range(2):
                        pe.wait_ge(G[d]["rows"], g + 1)
                        if g > 0:
                            pe.wait_ge(G[d]["state"], g)
                        mm(bank[4 * d][:, :], ident_b, mask_b[d], start=True, stop=False)
                        for h in range(HEADS):
                            last = mm(bank[4 * d][:, H(h)], sel[h], grow[d], start=False, stop=h == HEADS - 1)
                        last.then_inc(G[d]["arg"], 1)
                    for d in range(2):
                        ts = slice(CHUNK_OF[d][p] * P, (CHUNK_OF[d][p] + 1) * P)
                        pe.wait_ge(G[d]["cols"], g + 1)
                        for h in range(HEADS):
                            last = mm(bank[4 * d + 3][:, H(h)], gk[:, h, ts], gstate[:, d, h, :], start=True, stop=True)
                        last.then_inc(G[d]["ks"], 1)
                    if gives:
                        for d in range(2):
                            ts = slice(CHUNK_OF[d][p] * P, (CHUNK_OF[d][p] + 1) * P)
                            if o > 1:
                                pe.wait_ge(G[d]["oacc"], o - 1)
                            for h in range(HEADS):
                                last = mm(bank[4 * d + 2][:, H(h)], gk[:, h, ts], gq[:, h, ts], start=True, stop=True)
                            last.then_inc(G[d]["qk"], 1)
                    for d in range(2):
                        pe.wait_ge(G[d]["u0"], g + 1)
                        pe.wait_ge(G[d]["r"], g + 1)
                        for h in range(HEADS):
                            last = nc.tensor.transpose(bank[4 * d + 3][:, H(h)], slot(d, 3)[:, H(h)], ident)
                        last.then_inc(G[d]["t0"], 1)
                    if gives:
                        for d in range(2):
                            ts = slice(CHUNK_OF[d][p] * P, (CHUNK_OF[d][p] + 1) * P)
                            pe.wait_ge(G[d]["qkd"], o)
                            for h in range(HEADS):
                                last = mm(bank[4 * d + 2][:, H(h)], gq[:, h, ts], gstate[:, d, h, :], start=True, stop=True)
                            last.then_inc(G[d]["qs"], 1)
                    for lv in range(1, LEVELS):
                        k = (LEVELS - 1) * g + lv
                        kt = (LEVELS - 2) * g + lv
                        for d in range(2):
                            if lv == 1:
                                pe.wait_ge(G[d]["t1"], g + 1)
                                pe.wait_ge(G[d]["decay"], g + 1)
                                pe.wait_ge(G[d]["b"], g + 1)
                            else:
                                pe.wait_ge(G[d]["tout"], kt - 1)
                            for h in range(HEADS):
                                last = mm(bank[4 * d][:, C(h, lv)], slot(d, 1)[:, H(h)], half(slot(d, 4)[:, H(h)], lv, d),
                                          start=True, stop=True)
                            last.then_inc(G[d]["m"], 1)
                        if lv == 1 and gives:
                            for d in range(2):
                                pe.wait_ge(G[d]["qg"], o)
                        for n, start, end in IN_GAP[(l, p, 2 * lv - 2)]:
                            segment(n, start, end)
                        for d in range(2):
                            pe.wait_ge(G[d]["mout"], k)
                            if lv > 1:
                                pe.wait_ge(G[d]["uout"], k - 1)
                            if lv < LEVELS - 1:
                                for h in range(HEADS):
                                    last = mm(bank[4 * d + 3][:, C(h, lv)], slot(d, 3)[:, H(h)], half(slot(d, 5)[:, H(h)], lv, d),
                                              start=True, stop=True)
                                last.then_inc(G[d]["t"], 1)
                            for h in range(HEADS):
                                last = mm(bank[4 * d + 1][:, C(h, lv)], slot(d, 5)[:, H(h)], half(slot(d, 3)[:, H(h)], lv, 1 - d),
                                          start=True, stop=True)
                            last.then_inc(G[d]["u"], 1)
                        for n, start, end in IN_GAP[(l, p, 2 * lv - 1)]:
                            segment(n, start, end)
                    for d in range(2):
                        pe.wait_ge(G[d]["uout"], (LEVELS - 1) * (g + 1))
                        for h in range(HEADS):
                            last = mm(bank[4 * d][:, H(h)], slot(d, 3)[:, H(h)], slot(d, 6)[:, H(h)], start=True, stop=True)
                        last.then_inc(G[d]["v"], 1)
                    for d in range(2):
                        pe.wait_ge(G[d]["vn"], g + 1)
                        pe.wait_ge(G[d]["ke"], g + 1)
                        evacuated(pe, [n for x in range(GAPS) for n in completed(IN_GAP[(l, p, x)])
                                       if SEGS[n][4] == 4 * d + 2][-1])
                        if gives:
                            for h in range(HEADS):
                                last = mm(bank[4 * d + 2][:, H(h)], slot(d, 2)[:, H(h)], slot(d, 5)[:, H(h)],
                                          start=True, stop=True)
                            last.then_inc(G[d]["o"], 1)
                        for h in range(HEADS):
                            last = mm(bank[4 * d][:, H(h)], slot(d, 7)[:, H(h)], slot(d, 5)[:, H(h)], start=True, stop=True)
                        last.then_inc(G[d]["s"], 1)
                for d in range(2):
                    pe.wait_ge(G[d]["state"], 4 * (l + 1))
                    pe.wait_ge(G[d]["oacc"], gd_outs(l, 3))

                def post(b):
                    for j, t in enumerate(token_tiles(l)):
                        n = post_count(l, b) + j
                        pe.wait_ge(S["post_norm"], n + 1)
                        if j >= 2:
                            pe.wait_ge(S["post_out"], n - 1)
                        for h in range(HEADS):
                            last = nc.tensor.transpose(bank[6 + j % 2][:, H(h)], oacc[:, t, H(h)], ident)
                        last.then_inc(S["post_tr"], 1)
                    pe.wait_ge(S["post_out"], post_count(l, b) + len(token_tiles(l)))

                evacuated(pe, seg_of(l, "mqk"))
                evacuated(pe, seg_of(l, "mv"))
                for t in range(NT):
                    for i in range(2):
                        at = (t % 2) * 256 + i * P
                        last = nc.tensor.transpose(bank[2 + t // 2][:, at:at + P], mk[:, i, t * P:(t + 1) * P], ident)
                last.then_inc(S["mkt_psum"], 1)

                def gate_rows(u):
                    d, t = UNITS[u]
                    if 8 * l + u > 0:
                        pe.wait_ge(S["ml_ecol"], 8 * l + u)
                    mm(bank[5][0:4, 0:P], gates[:, t, 8 * d:8 * d + 4], ident, start=True, stop=True)
                    mm(bank[5][0:4, P:2 * P], lgate[:, t, 4 * d:4 * d + 4], tri[d], start=True, stop=True)\
                        .then_inc(S["ml_small"], 1)

                gate_rows(0)
                for n in BESIDE[(l, -1)]:
                    segment(n)
                post(2)

                pe.wait_ge(S["mkt_out"], l + 1)
                pe.wait_ge(S["pads_set"], l + 1)

                for u, (d, t) in enumerate(UNITS):
                    g = 8 * l + u
                    gives = u in out_units[l]
                    o = outputs(l, u)
                    ts = slice(t * P, (t + 1) * P)
                    pe.wait_ge(S["ml_rows"], g + 1)
                    pe.wait_ge(S["ml_exp"], g + 1)
                    mm(bank[5][:, 256:260], mrow[:, 5, :], ident[0:4, 0:4].rearrange("p (i r) -> p r i", r=2),
                       start=True, stop=True)
                    mm(bank[5][:, 260:264], mrow[:, 6, :], ident[0:4, 0:4], start=True, stop=True)
                    end = P - 1 if d == 0 else 0
                    for i in range(2):
                        last = mm(bank[5][:, 264 + i:265 + i], selp[i], mrow[:, 7, end:end + 1], start=True, stop=True)
                    if gives:
                        last = mm(bank[5][:, 266:270], mrow[:, 1, :], ident[0:4, 0:4].rearrange("p (i r) -> p r i", r=2),
                                  start=True, stop=True)
                    last.then_inc(S["ml_cols"], 1)
                    if gives:
                        mm(bank[2][:, :], ident_b, mask_b[d], start=True, stop=False)
                        for q in range(HEADS):
                            h = 2 * (q % 2) + q // 2
                            last = mm(bank[2][:, H(q)], sel[h], mrow[:, 3, :], start=False, stop=q == HEADS - 1)
                        last.then_inc(S["ml_arg"], 1)
                        for i in range(2):
                            last = mm(bank[7][:, i * P:(i + 1) * P], selp[i], mrow[:, 7, :], start=True, stop=True)
                        last.then_inc(S["ml_qb"], 1)
                    if g > 0:
                        pe.wait_ge(S["ml_state"], g)
                    if gives:
                        if o > 1:
                            pe.wait_ge(S["ml_h"], 2 * o - 2)
                        for h in range(HEADS):
                            i, r = h // 2, 64 * (h % 2)
                            last = mm(bank[3 + 3 * (h % 2)][:, H(i)], mk[r:r + 64, i, ts], mq[r:r + 64, i, ts],
                                      start=True, stop=True)
                        last.then_inc(S["ml_qk"], 1)
                    for j, n in enumerate(BESIDE[(l, u)]):
                        segment(n)
                        if j == 0 and u < 7:
                            gate_rows(u + 1)
                    if gives:
                        pe.wait_ge(S["ml_p"], o)
                        pe.wait_ge(S["ml_qg"], o)
                        for h in range(HEADS):
                            i, r = h // 2, 64 * (h % 2)
                            dst = bank[4 + 2 * (h % 2)][:, 129 * i:129 * i + 129]
                            mm(dst, work[:, 1, H(2 * (h % 2) + i)], mv[:, t, h, :], start=True, stop=False)
                            last = mm(dst, work[r:r + 64, 2, i * P:(i + 1) * P], mstate[r:r + 64, d, i, :],
                                      start=False, stop=True)
                        last.then_inc(S["ml_num"], 1)
                    pe.wait_ge(S["ml_kw"], g + 1)
                    for h in range(HEADS):
                        i, r = h // 2, 64 * (h % 2)
                        last = mm(mlstm_c(i)[r:r + 64, :], work[:, 3, 64 * h:64 * h + 64], mv[:, t, h, :], start=True, stop=True)
                    last.then_inc(S["ml_c"], 1)
                pe.wait_ge(S["ml_h"], 2 * outputs(l, 7))
                pe.wait_ge(S["ml_state"], 8 * (l + 1))
                dense(l, "bg", [0])
                post(1)

                for n in BESIDE[(l, 8)]:
                    segment(n)

                evacuated(pe, seg_of(l, "ak"))
                evacuated(pe, seg_of(l, "av"))
                for j in range(8):
                    src = (aq if j < 4 else ak)[:, j % 4, CTX:TOK]
                    if j >= 2:
                        pe.wait_ge(S["rope_out"], 8 * l + j - 1)
                    mm(bank[4 + j % 2][:, 0:LAT], rope_r, src, start=True, stop=True).then_inc(S["rope_psum"], 1)
                pe.wait_ge(S["rope_out"], 8 * l + 8)
                steps_a = attn_units(l + 1) - attn_units(l)

                def scores(k):
                    g = attn_units(l) + k
                    t, h = token_tiles(l)[k // 4], k % 4
                    nk = CTX if t < 2 else TOK
                    if g >= 2:
                        pe.wait_ge(S["at_e"], 2 * g - 2)
                    for m in range(2):
                        r = 64 * m
                        last = mm(bank[2 + 4 * (g % 2) + m][:, 0:nk], aq[r:r + 64, h, t * P:(t + 1) * P],
                                  ak[r:r + 64, h, 0:nk], start=True, stop=True)
                    last.then_inc(S["at_s"], 1)

                scores(0)
                for k in range(steps_a):
                    g = attn_units(l) + k
                    t, h = token_tiles(l)[k // 4], k % 4
                    nk = CTX if t < 2 else TOK
                    q = g % 2
                    if k + 1 < steps_a:
                        scores(k + 1)
                    fill = []
                    for j in range(32 // steps_a // 2 * k, 32 // steps_a // 2 * (k + 1)):
                        fill += [("bg", j), ("by", j)]
                    for kind, j in fill[:len(fill) // 2]:
                        if (kind, j) != ("bg", 0):
                            dense(l, kind, [j])
                    pe.wait_ge(S["at_w"], g + 1)
                    if g >= 1:
                        pe.wait_ge(S["at_wtout"], g)
                    for kt in range(nk // P):
                        last = nc.tensor.transpose(bank[4][:, H(kt)], work[:, 4 * q + 2, H(kt)], ident)
                    last.then_inc(S["at_wt"], 1)
                    for kind, j in fill[len(fill) // 2:]:
                        dense(l, kind, [j])
                    pe.wait_ge(S["at_wtout"], g + 1)
                    if g >= 1:
                        pe.wait_ge(S["at_oout"], g)
                    for kt in range(nk // P):
                        last = mm(bank[5][:, 0:P], work[:, 4 * q + 3, H(kt)], av[:, kt, H(h)], start=kt == 0,
                                  stop=kt == nk // P - 1)
                    last.then_inc(S["at_o"], 1)
                dense(l, "bg", [16])
                post(0)
                for j in range(16, 24):
                    if j > 16:
                        dense(l, "bg", [j])
                    dense(l, "by", [j])
                dense(l, "wo")
                output_sum(l, 1)
                norm(l, 2)
                dense(l, "ff1")
                dense(l, "ff2")
                output_sum(l, 3)

            for hf in range(2):
                pe.wait_ge(S["res_ready"], (2 * DEPTH - 1) * KD // 2 + 2 * hf + 2)
                pe.wait_ge(S["res_odd"], (2 * DEPTH - 1) * KD // 2 + 2 * hf + 2)
                for t in range(2):
                    for q in range(4):
                        last = nc.tensor.transpose(bank[2 + 2 * hf + t][:, q * P:(q + 1) * P],
                                                   xt[:, 4 * hf + q, CTX + t * P:CTX + (t + 1) * P], ident)
                    last.then_inc(S["final_psum"], 1)


_INS = ["x", "c", "ctx", "c_ctx", "w_ada", "b_ada", "norm_gains", "w_in", "b_in", "a_lambda", "a_norm",
        "m_fbias", "m_norm", "g_conv", "g_alog", "g_dtbias", "g_norm", "w_branch", "w_out", "w_ff1", "w_ff2"]


def kernel(**inputs):
    import numpy as _np
    import concourse.bacc as _bacc
    from concourse import mybir as _mybir
    from concourse.bass_utils import run_bass_kernel_spmd as _run

    nc = _bacc.Bacc("TRN2", target_bir_lowering=False, num_devices=1)
    arrays, args = {}, []
    const_f, const_b, const_m = shape_constants()
    every = [(n, _np.ascontiguousarray(inputs[n])) for n in _INS]
    every += [("const_f", const_f), ("const_b", const_b), ("const_m", const_m)]
    for name, a in every:
        arrays[f"in_{name}"] = a
        args.append(nc.dram_tensor(f"in_{name}", a.shape, _mybir.dt.from_np(a.dtype), kind="ExternalInput").ap())
    args.append(nc.dram_tensor("out_0", (1, LAT, DM), F32, kind="ExternalOutput").ap())
    hybrid_trunk(nc, *args)
    r = _run(nc, [arrays], core_ids=[0])
    return r.results[0]["out_0"]
```
